# Optimizing a Trainium2 kernel written in Bass

```python
import jax
import jax.numpy as jnp
from jax import lax
import numpy as np

D_MODEL = 1024
BATCH = 1
SEQ = 1024
DEPTH = 1
DEC_BATCH = 8
DEC_SEQ = 8
PAST_LEN = 1024
PAGE_SIZE = 128

SWA_GROUPS = ((128, 1), (512, 4), (2048, 16))
N_GROUPS = 3
H_A = 4
HD_A = 128
W_A = H_A * HD_A
N_A = N_GROUPS * 3 * W_A
BLK = 128
H_B = 8
Q_RANK = 384
KV_RANK = 256
NOPE = 64
ROPE_B = 32
VD_B = 64
N_MEM = 256
H_M = 4
HD_M = 128
D_FF = 2816
CONV_W = 3

ROPE_THETA = 10000.0
EPS = 1e-6
NEG_INF = -1e30
N_IN = N_A + Q_RANK + KV_RANK + ROPE_B + H_M * HD_M + 3 * D_MODEL

kernel_name = 'hybrid_dilated_mla_memory_convffn_step'

def rms_norm(x, w):
    x32 = x.astype(jnp.float32)
    y = x32 * lax.rsqrt(jnp.mean(x32 * x32, axis=-1, keepdims=True) + EPS)
    return (y * w.astype(jnp.float32)).astype(x.dtype)

def rope(x, pos):
    dim = x.shape[-1]
    half = dim // 2
    inv_freq = ROPE_THETA ** (-jnp.arange(half, dtype=jnp.float32) * (2.0 / dim))
    ang = pos.astype(jnp.float32)[:, None] * inv_freq[None, :]
    shape = (ang.shape[0],) + (1,) * (x.ndim - 3) + (half,)
    cos = jnp.cos(ang).reshape(shape)
    sin = jnp.sin(ang).reshape(shape)
    x32 = x.astype(jnp.float32)
    x1, x2 = x32[..., :half], x32[..., half:]
    return jnp.concatenate([x1 * cos - x2 * sin, x1 * sin + x2 * cos], axis=-1).astype(x.dtype)

def project_mixers(h, pos, w_in, norm_cq, w_uq, norm_ckv):
    B, T, _ = h.shape
    p = h @ w_in
    o0 = N_A
    o1 = o0 + Q_RANK
    o2 = o1 + KV_RANK
    o3 = o2 + ROPE_B
    o4 = o3 + H_M * HD_M
    qkv_a = p[..., :o0].reshape(B, T, N_GROUPS, 3, H_A, HD_A)
    q_a = rope(qkv_a[:, :, :, 0], pos)
    kv_a = jnp.stack([rope(qkv_a[:, :, :, 1], pos), qkv_a[:, :, :, 2]], axis=3)
    q_b = (rms_norm(p[..., o0:o1], norm_cq) @ w_uq).reshape(B, T, H_B, NOPE + ROPE_B)
    q_nope = q_b[..., :NOPE]
    q_rope = rope(q_b[..., NOPE:], pos)
    c_kv = rms_norm(p[..., o1:o2], norm_ckv)
    k_rope = rope(p[..., o2:o3], pos)
    q_m = p[..., o3:o4].reshape(B, T, H_M, HD_M)
    gates = p[..., o4:].reshape(B, T, 3, D_MODEL)
    return q_a, kv_a, q_nope, q_rope, c_kv, k_rope, q_m, gates

def dilated_prompt(q, kv, dil, span):
    B, S, H, hd = q.shape
    n_blk = -(-S // (dil * BLK))
    Lp = n_blk * BLK
    pad = Lp * dil - S

    def to_streams(t):
        t = jnp.pad(t, [(0, 0), (0, pad)] + [(0, 0)] * (t.ndim - 2))
        t = t.reshape((B, Lp, dil) + t.shape[2:])
        t = jnp.moveaxis(t, 2, 1)
        return t.reshape((B, dil, n_blk, BLK) + t.shape[3:])

    def from_streams(t):
        rest = t.shape[4:]
        t = t.reshape((B, dil, Lp) + rest)
        t = jnp.moveaxis(t, 1, 2).reshape((B, Lp * dil) + rest)
        return t[:, :S]

    qs = to_streams(q)
    kvs = to_streams(kv)
    n_prev = -(-span // BLK)
    prevs = [jnp.pad(kvs, [(0, 0), (0, 0), (sft, 0)] + [(0, 0)] * 4)[:, :, :n_blk] for sft in range(n_prev, 0, -1)]
    kk = jnp.concatenate(prevs + [kvs], axis=3)
    KL = (n_prev + 1) * BLK
    s = jnp.einsum('brnqhd,brnkhd->brhnqk', qs, kk[:, :, :, :, 0]) * (hd ** -0.5)
    a = jnp.arange(BLK)[:, None]
    b = jnp.arange(KL)[None, :]
    dist = a + n_prev * BLK - b
    blk = jnp.arange(n_blk)[:, None, None]
    valid = (dist >= 0) & (dist <= span) & (blk * BLK + b - n_prev * BLK >= 0)
    s = jnp.where(valid, s.astype(jnp.float32), NEG_INF)
    lse = jax.nn.logsumexp(s, axis=-1)
    p = jnp.exp(s - lse[..., None]).astype(q.dtype)
    o = jnp.einsum('brhnqk,brnkhd->brnqhd', p, kk[:, :, :, :, 1])
    return from_streams(o), from_streams(jnp.moveaxis(lse, 2, -1))

def dilated_sample(q, kv_new, kv_buf, dil, span, window):
    Wb = kv_buf.shape[1]
    T = q.shape[1]
    kv_all = jnp.concatenate([kv_buf, kv_new], axis=1)
    idx = Wb + jnp.arange(T)[:, None] - dil * jnp.arange(span + 1)[None, :]
    valid = idx >= 0
    kg = jnp.take(kv_all, jnp.maximum(idx, 0), axis=1)
    s = jnp.einsum('bthd,btjhd->bhtj', q, kg[:, :, :, 0]) * (q.shape[-1] ** -0.5)
    s = jnp.where(valid, s.astype(jnp.float32), NEG_INF)
    lse = jax.nn.logsumexp(s, axis=-1)
    p = jnp.exp(s - lse[..., None]).astype(q.dtype)
    o = jnp.einsum('bhtj,btjhd->bthd', p, kg[:, :, :, 1])
    new_buf = kv_all[:, -min(window, Wb + T):]
    return o, jnp.moveaxis(lse, 1, 2), new_buf

def combine_groups(outs, lses):
    wts = jax.nn.softmax(jnp.stack(lses, axis=0), axis=0)
    return jnp.einsum('gbth,gbthd->bthd', wts.astype(outs[0].dtype), jnp.stack(outs, axis=0))

def mla_prompt(q_nope, q_rope, c_kv, k_rope, w_uk, w_uv):
    B, S, H, _ = q_nope.shape
    k_nope = jnp.einsum('bsr,rhn->bshn', c_kv, w_uk)
    v = jnp.einsum('bsr,rhv->bshv', c_kv, w_uv)
    nb = S // BLK
    qn_b = q_nope.reshape(B, nb, BLK, H, NOPE).swapaxes(0, 1)
    qr_b = q_rope.reshape(B, nb, BLK, H, ROPE_B).swapaxes(0, 1)
    key_pos = jnp.arange(S)
    scale = (NOPE + ROPE_B) ** -0.5

    def block(args):
        qn, qr, i = args
        s = (jnp.einsum('bqhn,bkhn->bhqk', qn, k_nope) + jnp.einsum('bqhe,bke->bhqk', qr, k_rope)) * scale
        q_pos = i * BLK + jnp.arange(BLK)
        s = jnp.where(key_pos[None, :] <= q_pos[:, None], s.astype(jnp.float32), NEG_INF)
        p = jax.nn.softmax(s, axis=-1).astype(v.dtype)
        return jnp.einsum('bhqk,bkhv->bqhv', p, v)

    o = lax.map(block, (qn_b, qr_b, jnp.arange(nb)))
    return o.swapaxes(0, 1).reshape(B, S, H, VD_B)

def mla_sample(q_nope, q_rope, c_kv, k_rope, pool_ckv, pool_krope, page_table, w_uk, w_uv):
    B, T = q_nope.shape[:2]
    ckv_past = pool_ckv[page_table].reshape(B, -1, KV_RANK)
    kr_past = pool_krope[page_table].reshape(B, -1, ROPE_B)
    P = ckv_past.shape[1]
    scale = (NOPE + ROPE_B) ** -0.5
    q_lat = jnp.einsum('bthn,rhn->bthr', q_nope, w_uk)
    s_past = jnp.einsum('bthr,bsr->bhts', q_lat, ckv_past) + jnp.einsum('bthe,bse->bhts', q_rope, kr_past)
    s_new = jnp.einsum('bthr,bur->bhtu', q_lat, c_kv) + jnp.einsum('bthe,bue->bhtu', q_rope, k_rope)
    causal = jnp.arange(T)[None, :] <= jnp.arange(T)[:, None]
    s_new = jnp.where(causal, s_new.astype(jnp.float32), NEG_INF)
    s = jnp.concatenate([s_past.astype(jnp.float32), s_new], axis=-1) * scale
    p = jax.nn.softmax(s, axis=-1).astype(c_kv.dtype)
    o_lat = jnp.einsum('bhts,bsr->bthr', p[..., :P], ckv_past) + jnp.einsum('bhtu,bur->bthr', p[..., P:], c_kv)
    return jnp.einsum('bthr,rhv->bthv', o_lat, w_uv)

def memory_kv(mem, norm_mem, w_mem_kv):
    B = mem.shape[0]
    return (rms_norm(mem, norm_mem) @ w_mem_kv).reshape(B, N_MEM, 2, H_M, HD_M)

def memory_attention(q_m, mem_kv):
    s = jnp.einsum('bthd,bmhd->bhtm', q_m, mem_kv[:, :, 0]) * (HD_M ** -0.5)
    p = jax.nn.softmax(s.astype(jnp.float32), axis=-1).astype(q_m.dtype)
    return jnp.einsum('bhtm,bmhd->bthd', p, mem_kv[:, :, 1])

def merge_branches(gates, o_a, o_b, o_m, w_o_a, w_o_b, w_o_m, w_out):
    B, T = gates.shape[:2]
    g = jax.nn.sigmoid(gates.astype(jnp.float32)).astype(o_a.dtype)
    m = (g[:, :, 0] * (o_a.reshape(B, T, -1) @ w_o_a)
         + g[:, :, 1] * (o_b.reshape(B, T, -1) @ w_o_b)
         + g[:, :, 2] * (o_m.reshape(B, T, -1) @ w_o_m))
    return m @ w_out

def conv_ffn(h, prev, w_up, conv_w, conv_b, w_down):
    u = h @ w_up
    T = u.shape[1]
    if prev is None:
        prev = jnp.zeros((u.shape[0], CONV_W - 1, u.shape[2]), u.dtype)
    buf = jnp.concatenate([prev, u], axis=1)
    c = conv_b
    for k in range(CONV_W):
        c = c + buf[:, k:k + T] * conv_w[k]
    g, val = c[..., :D_FF], c[..., D_FF:]
    out = (jax.nn.gelu(g, approximate=True) * val) @ w_down
    return out, buf[:, T:]

def trunk_layer(x, pos, mix_fn, conv_prev, lw):
    (n_pre, n_post, f_pre, f_post, w_in_l, n_cq, w_uq_l, n_ckv,
     w_o_a_l, w_o_b_l, w_o_m_l, w_out_l, w_up_l, cw_l, cb_l, w_down_l) = lw
    h = rms_norm(x, n_pre)
    q_a, kv_a, qn, qr, ckv, kr, q_m, gates = project_mixers(h, pos, w_in_l, n_cq, w_uq_l, n_ckv)
    o_a, o_b, o_m, mix_state = mix_fn(q_a, kv_a, qn, qr, ckv, kr, q_m)
    x = x + rms_norm(merge_branches(gates, o_a, o_b, o_m, w_o_a_l, w_o_b_l, w_o_m_l, w_out_l), n_post)
    f, conv_state = conv_ffn(rms_norm(x, f_pre), conv_prev, w_up_l, cw_l, cb_l, w_down_l)
    x = x + rms_norm(f, f_post)
    return x, mix_state, conv_state

def setup_inputs(seed: int = 0) -> dict:
    key = jax.random.key(seed)
    ks = jax.random.split(key, 40)
    f32 = jnp.float32

    def nrm(k, shape, scale=1.0):
        return jax.random.normal(k, shape, f32) * scale

    def gain(k, n):
        return 1.0 + 0.05 * jax.random.normal(k, (DEPTH, n), f32)

    n_pages = PAST_LEN // PAGE_SIZE
    n_used = DEC_BATCH * n_pages
    n_pool = n_used + max(1, n_used // 4)
    page_table = jax.random.permutation(ks[0], n_pool)[:n_used].reshape(DEC_BATCH, n_pages).astype(jnp.int32)
    return {
        'x_prompt': nrm(ks[1], (BATCH, SEQ, D_MODEL)),
        'x_sample': nrm(ks[2], (DEC_BATCH, DEC_SEQ, D_MODEL)),
        'cache_swa_g0': nrm(ks[3], (DEPTH, DEC_BATCH, min(SWA_GROUPS[0][0], PAST_LEN), 2, H_A, HD_A)),
        'cache_swa_g1': nrm(ks[4], (DEPTH, DEC_BATCH, min(SWA_GROUPS[1][0], PAST_LEN), 2, H_A, HD_A)),
        'cache_swa_g2': nrm(ks[5], (DEPTH, DEC_BATCH, min(SWA_GROUPS[2][0], PAST_LEN), 2, H_A, HD_A)),
        'cache_mla_ckv': nrm(ks[6], (DEPTH, n_pool, PAGE_SIZE, KV_RANK)),
        'cache_mla_krope': nrm(ks[7], (DEPTH, n_pool, PAGE_SIZE, ROPE_B)),
        'cache_mem_kv': nrm(ks[8], (DEPTH, DEC_BATCH, N_MEM, 2, H_M, HD_M)),
        'state_ffn_conv': nrm(ks[9], (DEPTH, DEC_BATCH, CONV_W - 1, 2 * D_FF)),
        'page_table': page_table,
        'mem_prompt': nrm(ks[10], (BATCH, N_MEM, D_MODEL)),
        'norm_attn_pre': gain(ks[11], D_MODEL),
        'norm_attn_post': gain(ks[12], D_MODEL),
        'norm_ffn_pre': gain(ks[13], D_MODEL),
        'norm_ffn_post': gain(ks[14], D_MODEL),
        'norm_mem': gain(ks[15], D_MODEL),
        'w_in': nrm(ks[16], (DEPTH, D_MODEL, N_IN), D_MODEL ** -0.5),
        'norm_cq': gain(ks[17], Q_RANK),
        'w_uq': nrm(ks[18], (DEPTH, Q_RANK, H_B * (NOPE + ROPE_B)), Q_RANK ** -0.5),
        'norm_ckv': gain(ks[19], KV_RANK),
        'w_uk': nrm(ks[20], (DEPTH, KV_RANK, H_B, NOPE), KV_RANK ** -0.5),
        'w_uv': nrm(ks[21], (DEPTH, KV_RANK, H_B, VD_B), KV_RANK ** -0.5),
        'w_mem_kv': nrm(ks[22], (DEPTH, D_MODEL, 2 * H_M * HD_M), D_MODEL ** -0.5),
        'w_o_a': nrm(ks[23], (DEPTH, W_A, D_MODEL), W_A ** -0.5),
        'w_o_b': nrm(ks[24], (DEPTH, H_B * VD_B, D_MODEL), (H_B * VD_B) ** -0.5),
        'w_o_m': nrm(ks[25], (DEPTH, H_M * HD_M, D_MODEL), (H_M * HD_M) ** -0.5),
        'w_out': nrm(ks[26], (DEPTH, D_MODEL, D_MODEL), D_MODEL ** -0.5),
        'w_up': nrm(ks[27], (DEPTH, D_MODEL, 2 * D_FF), D_MODEL ** -0.5),
        'conv_w': nrm(ks[28], (DEPTH, CONV_W, 2 * D_FF), CONV_W ** -0.5),
        'conv_b': nrm(ks[29], (DEPTH, 2 * D_FF), 0.01),
        'w_down': nrm(ks[30], (DEPTH, D_FF, D_MODEL), D_FF ** -0.5),
    }

def reference(x_prompt, x_sample, cache_swa_g0, cache_swa_g1, cache_swa_g2, cache_mla_ckv, cache_mla_krope,
              cache_mem_kv, state_ffn_conv, page_table, mem_prompt, norm_attn_pre, norm_attn_post, norm_ffn_pre,
              norm_ffn_post, norm_mem, w_in, norm_cq, w_uq, norm_ckv, w_uk, w_uv, w_mem_kv, w_o_a, w_o_b, w_o_m,
              w_out, w_up, conv_w, conv_b, w_down):
    S = x_prompt.shape[1]
    T = x_sample.shape[1]
    P = cache_swa_g0.shape[0] and PAST_LEN
    pos_p = jnp.arange(S)
    pos_s = P + jnp.arange(T)
    caches_swa = (cache_swa_g0, cache_swa_g1, cache_swa_g2)
    xp, xs = x_prompt, x_sample
    ps = [[] for _ in range(7)]
    ss = [[] for _ in range(6)]
    for l in range(DEPTH):
        lw = (norm_attn_pre[l], norm_attn_post[l], norm_ffn_pre[l], norm_ffn_post[l], w_in[l], norm_cq[l], w_uq[l],
              norm_ckv[l], w_o_a[l], w_o_b[l], w_o_m[l], w_out[l], w_up[l], conv_w[l], conv_b[l], w_down[l])
        mem_kv_p = memory_kv(mem_prompt, norm_mem[l], w_mem_kv[l])

        def prompt_mix(q_a, kv_a, qn, qr, ckv, kr, q_m):
            outs, lses, bufs = [], [], []
            for g, (win, dil) in enumerate(SWA_GROUPS):
                o, lse = dilated_prompt(q_a[:, :, g], kv_a[:, :, g], dil, win // dil)
                outs.append(o)
                lses.append(lse)
                bufs.append(kv_a[:, -min(win, S):, g])
            o_a = combine_groups(outs, lses)
            o_b = mla_prompt(qn, qr, ckv, kr, w_uk[l], w_uv[l])
            o_m = memory_attention(q_m, mem_kv_p)
            return o_a, o_b, o_m, (bufs[0], bufs[1], bufs[2], ckv, kr, mem_kv_p)

        def sample_mix(q_a, kv_a, qn, qr, ckv, kr, q_m):
            outs, lses, bufs = [], [], []
            for g, (win, dil) in enumerate(SWA_GROUPS):
                o, lse, nb = dilated_sample(q_a[:, :, g], kv_a[:, :, g], caches_swa[g][l], dil, win // dil, win)
                outs.append(o)
                lses.append(lse)
                bufs.append(nb)
            o_a = combine_groups(outs, lses)
            o_b = mla_sample(qn, qr, ckv, kr, cache_mla_ckv[l], cache_mla_krope[l], page_table, w_uk[l], w_uv[l])
            o_m = memory_attention(q_m, cache_mem_kv[l])
            return o_a, o_b, o_m, (bufs[0], bufs[1], bufs[2], ckv, kr)

        xp, mst_p, conv_p = trunk_layer(xp, pos_p, prompt_mix, None, lw)
        xs, mst_s, conv_s = trunk_layer(xs, pos_s, sample_mix, state_ffn_conv[l], lw)
        for i, t in enumerate(mst_p + (conv_p,)):
            ps[i].append(t)
        for i, t in enumerate(mst_s + (conv_s,)):
            ss[i].append(t)
    p_st = [jnp.stack(t, axis=0) for t in ps]
    s_st = [jnp.stack(t, axis=0) for t in ss]
    return (xp, xs, p_st[0], p_st[1], p_st[2], p_st[3], p_st[4], p_st[5], p_st[6],
            s_st[0], s_st[1], s_st[2], s_st[3], s_st[4], s_st[5])


_drawn_inputs = setup_inputs


def setup_inputs(seed=0):
    import zlib

    import numpy as np

    out = dict(_drawn_inputs(seed))
    spreads = {}
    factors = {'norm_cq': 2.734, 'conv_b': 6.864}
    for name, (base, spread) in spreads.items():
        noise = np.random.default_rng([zlib.crc32(name.encode()), seed]).standard_normal(out[name].shape)
        drawn = base * np.exp(spread * noise) if base else spread * noise
        out[name] = jnp.asarray(drawn.astype(out[name].dtype))
    for name, factor in factors.items():
        out[name] = (out[name] * factor).astype(out[name].dtype)
    return out
```

```python
from contextlib import ExitStack

import numpy as np

import concourse.bass as bass
from concourse import mybir

ALU = mybir.AluOpType
ACT = mybir.ActivationFunctionType
AX = mybir.AxisListType
F32 = mybir.dt.float32
F32R = mybir.dt.float32r
I32 = mybir.dt.int32

P = 128
D = 1024
KD = D // P
S = 1024
NB, TS = 8, 8
NSMP = NB * TS
N = S + NSMP
PT_TILES = S // P
TILES = PT_TILES + 1
PAST = 1024
GROUPS = ((128, 1), (512, 4), (2048, 16))
G = len(GROUPS)
H = 4
HD = 128
HB, NOPE, RB, VD = 8, 64, 32, 64
QR, KR = 384, 256
NMEM = 256
DFF = 2816
EPS = 1e-6
SCALE_A = HD ** -0.5
SCALE_B = (NOPE + RB) ** -0.5
LOWEST = -3.0e38
COL = [(0, 384), (384, 384), (768, 320)]


def rows_of(t):
    return P if t < PT_TILES else NSMP


class Mem:

    spent = []

    def __init__(self, nc, ctx, name):
        self.nc, self.ctx, self.name = nc, ctx, name

    def sb(self, name, shape, dt=F32):
        return self.ctx.enter_context(self.nc.sbuf_tensor(f"{self.name}_{name}", shape, dt))

    def ps(self, name, shape):
        return self.ctx.enter_context(self.nc.psum_tensor(f"{self.name}_{name}", shape, F32))

    def sem(self, name):
        sem = self.ctx.enter_context(self.nc.semaphore(f"{self.name}_{name}"))
        Mem.spent.append(sem.num)
        return sem


def clear_spent(pool, numbers):
    first = None
    for n in sorted(numbers):
        if first is None or n != last + 1:
            if first is not None:
                pool.sem_clear(range(first, last + 1))
            first = n
        last = n
    pool.sem_clear(range(first, last + 1))


def mm3(pe, out, w_hi, w_lo, x_hi, x_lo, start, stop):
    pe.matmul(out, w_hi, x_hi, start=start, stop=False)
    pe.matmul(out, w_hi, x_lo, start=False, stop=False)
    return pe.matmul(out, w_lo, x_hi, start=False, stop=stop)


class WeightRing:

    RAW = 3

    def __init__(self, m, src, width, slots):
        self.src, self.width, self.R = src, width, slots
        self.raw = m.sb("w_raw", [P, self.RAW, width])
        self.hi = m.sb("w_hi", [P, slots, width], F32R)
        self.lo = m.sb("w_lo", [P, slots, width], F32R)
        self.landed = [m.sem(f"w_landed{i}") for i in range(self.RAW)]
        self.rounded = m.sem("w_rounded")
        self.ready = m.sem("w_ready")
        self.used = m.sem("w_used")

    def load(self, sp, base, j):
        sp.wait_ge(self.ready, base + j + 1)
        sp.dma_start(self.raw[:, j % self.RAW, :], self.src[base + j]).then_inc(self.landed[j % self.RAW], 16)

    def round_hi(self, act, base, j, free=False):
        act.wait_ge(self.landed[j % self.RAW], 16 * self.turn(base, j) + 16)
        if not free:
            act.wait_ge(self.used, base + j + 1)
        act.activation(self.hi[:, j % self.R, :], self.raw[:, j % self.RAW, :], ACT.Copy).then_inc(self.rounded, 1)

    def rest_lo(self, dve, base, j):
        dve.wait_ge(self.rounded, base + j + 1)
        dve.tensor_tensor(self.lo[:, j % self.R, :], self.raw[:, j % self.RAW, :],
                          self.hi[:, j % self.R, :].bitcast(F32), ALU.subtract).then_inc(self.ready, 1)

    def turn(self, base, j):
        if isinstance(base, int):
            return (base + j) // self.RAW
        return self.turns(base) + j // self.RAW

    def credit(self, dve, pe):
        if dve is not None:
            dve.sem_inc(self.ready, self.RAW)
        if pe is not None:
            pe.sem_inc(self.used, self.R)

    def wait(self, pe, base, j):
        pe.wait_ge(self.ready, base + j + 1 + self.RAW)


def normalise(nc, io, name, items):
    with ExitStack() as ctx:
        m = Mem(nc, ctx, name)
        XS = 3
        xs = m.sb("x", [P, XS, D])
        sq = m.sb("sq", [P, D])
        ss = m.sb("ss", [P, 16])
        rstd = m.sb("rstd", [P, 16])
        half = m.sb("half", [P, 1])
        ident = m.sb("ident", [P, P])
        gains = m.sb("gains", [P, 3, KD])
        h = m.sb("h", [P, 2, D])
        h32 = m.sb("h32", [P, 2, KD, P])
        ps = m.ps("t", [P, 2, KD, P])
        landed = [m.sem(f"landed{i}") for i in range(XS)]
        const = m.sem("const")
        sq_done, mean_done, rstd_done = m.sem("sq_done"), m.sem("mean_done"), m.sem("rstd_done")
        h_done, turned, gained, hi_done, lo_done, half_set = (m.sem(x) for x in
            ("h_done", "turned", "gained", "hi_done", "lo_done", "half_set"))
        with nc.Block() as block:
            @block.sync
            def _(sp):
                sp.dma_start(ident[:], io["ident"]).then_inc(const, 16)
                sp.dma_start(gains[:], io["gains_pre"]).then_inc(const, 16)
                for i, (src, r, *_) in enumerate(items):
                    if i >= XS:
                        sp.wait_ge(h_done, i - XS + 1)
                    sp.dma_start(xs[0:r, i % XS, :], src).then_inc(landed[i % XS], 16)

            @block.scalar
            def _(act):
                def square(i):
                    r = items[i][1]
                    act.wait_ge(landed[i % XS], 16 * (i // XS + 1))
                    if i:
                        act.wait_ge(sq_done, i)
                    act.activation(sq[0:r, :], xs[0:r, i % XS, :], ACT.Square,
                                   accum_out=ss[0:r, i:i + 1]).then_inc(sq_done, 1)

                square(0)
                for i, (_, r, _, hi, _, c) in enumerate(items):
                    if i + 1 < len(items):
                        square(i + 1)
                    act.wait_ge(gained, i + 1)
                    act.activation(hi[:, :, c:c + r], h32[:, i % 2, :, 0:r], ACT.Copy).then_inc(hi_done, 1)

            @block.gpsimd
            def _(pool):
                pool.memset(half[:], -0.5).then_inc(half_set, 1)
                pool.wait_ge(half_set, 1)
                for i, (_, r, *_) in enumerate(items):
                    pool.wait_ge(sq_done, i + 1)
                    pool.tensor_scalar(ss[0:r, i:i + 1], ss[0:r, i:i + 1], 1.0 / D, EPS, ALU.mult,
                                       ALU.add).then_inc(mean_done, 1)
                    pool.wait_ge(mean_done, i + 1)
                    pool.tensor_tensor(rstd[0:r, i:i + 1], ss[0:r, i:i + 1], half[0:r, :], ALU.pow)\
                        .then_inc(rstd_done, 1)

            @block.tensor
            def _(pe):
                pe.wait_ge(const, 32)
                for i, (_, r, *_) in enumerate(items):
                    pe.wait_ge(h_done, i + 1)
                    if i >= 2:
                        pe.wait_ge(gained, i - 1)
                    for k in range(KD):
                        ins = pe.transpose(ps[:, i % 2, k, 0:r], h[0:r, i % 2, k * P:(k + 1) * P], ident[0:r, 0:r])
                    ins.then_inc(turned, 1)

            @block.vector
            def _(dve):
                dve.wait_ge(const, 32)
                for i, (_, r, g, hi, lo, c) in enumerate(items):
                    dve.wait_ge(rstd_done, i + 1)
                    if i >= 2:
                        dve.wait_ge(turned, i - 1)
                    dve.tensor_scalar(h[0:r, i % 2, :], xs[0:r, i % XS, :], rstd[0:r, i:i + 1], None,
                                      ALU.mult).then_inc(h_done, 1)
                    dve.wait_ge(turned, i + 1)
                    if i >= 2:
                        dve.wait_ge(lo_done, i - 1)
                    gain = gains[:, g, :].rearrange("p (k a) -> p k a", a=1).broadcast_to([P, KD, r])
                    dve.tensor_tensor(h32[:, i % 2, :, 0:r], ps[:, i % 2, :, 0:r], gain, ALU.mult).then_inc(gained, 1)
                    dve.wait_ge(hi_done, i + 1)
                    dve.tensor_tensor(lo[:, :, c:c + r], h32[:, i % 2, :, 0:r], hi[:, :, c:c + r].bitcast(F32),
                                      ALU.subtract).then_inc(lo_done, 1)


def blocks_of(t):
    out = []
    for g, (win, _) in enumerate(GROUPS):
        reach = min(win // P, PT_TILES - 1)
        for kt in range(max(0, t - reach), t + 1):
            out.append((g, kt))
    return out


REACH = [min(w // P, PT_TILES - 1) for w, _ in GROUPS]
MASK_BACK = [min(r, 4) for r in REACH]
MASK_AT = [sum(r + 1 for r in MASK_BACK[:g]) for g in range(G)]
MASK_BLOCKS = sum(r + 1 for r in MASK_BACK)
MOST = len(blocks_of(PT_TILES - 1))


def mask_at(g, back, n):
    if REACH[g] > MASK_BACK[g] and back >= n:
        return MASK_AT[g]
    return MASK_AT[g] + MASK_BACK[g] - back


def runs_of(t, by=4):
    bl, out = blocks_of(t), []
    for j, (g, kt) in enumerate(bl):
        if out and out[-1][2] == g and out[-1][0] // by == j // by:
            out[-1][1] += 1
        else:
            out.append([j, 1, g, kt])
    return out


def window_attention(nc, io, hT_hi, hT_lo):
    with ExitStack() as ctx:
        m = Mem(nc, ctx, "win")
        ring = WeightRing(m, io["w_swa"], 2 * 3 * P, 6)
        CH = 12
        PR = G * TILES
        QB = [0]
        for t in range(PT_TILES):
            QB.append(QB[-1] + -(-len(blocks_of(t)) // 4))
        NQ = QB[-1]
        NST = 2 * G + 2
        ident = m.sb("ident", [P, P])
        mask = m.sb("mask", [P, MASK_BLOCKS * P])
        cosb = m.sb("cos", [P, TILES, HD // 2])
        sinb = m.sb("sin", [P, TILES, 2, HD // 2])
        qkT = m.sb("qkT", [P, G, 2, N])
        kv = m.sb("kv", [P, G, TILES, 2, HD])
        qrot = m.sb("qrot", [P, 2, HD])
        ra = m.sb("ra", [P, 2, 2, 2, HD // 2])
        rb = m.sb("rb", [P, 2, 2, 2, HD // 2])
        prob = m.sb("prob", [P, 2, MOST * P])
        spare = m.sb("spare", [P, 1])
        mx = m.sb("mx", [P, 2, 8])
        nm = m.sb("nm", [P, 2])
        den = m.sb("den", [P, 2])
        rden = m.sb("rden", [P, 2])
        probT = m.sb("probT", [P, 2, 4 * P])
        oT = m.sb("oT", [P, S])
        ps = m.ps("ps", [P, 8, 512])
        names = ("const", "pj_done", "ab_done", "rotated", "v_done", "tq_done", "tq_read", "s_done", "mx_read",
                 "nm_done", "exp_done", "rden_done", "p_done", "tp_done", "tp_read", "o_done", "o_read", "stored",
                 "o_stored", "kept")
        s = {n: m.sem(n) for n in names}

        ring.turns = lambda base: (base // ring.RAW)

        with nc.Block() as block:
            @block.sync
            def _(sp):
                for dst, src in ((ident, "ident"), (mask, "mask_p"), (cosb, "cos_a"), (sinb, "sin_a")):
                    sp.dma_start(dst[:], io[src]).then_inc(s["const"], 16)
                with sp.Fori(0, H) as h:
                    for j in range(CH):
                        ring.load(sp, CH * h, j)
                        if j % 6 == 5:
                            b = 2 * h + j // 6
                            for g, (win, _) in enumerate(GROUPS):
                                first, n = max(0, PAST + TS - win) - max(0, PAST - win), min(win, PAST + TS) - TS
                                sp.dma_start(io["s_swa"][g][b, 0:n], io[f"cache{g}"][b, first:first + n])\
                                    .then_inc(s["kept"], 16)
                    sp.wait_ge(s["tq_read"], PR * h + PR + 2)
                    sp.wait_ge(s["v_done"], PR * h + PR + 2)
                    for g, (win, _) in enumerate(GROUPS):
                        keep = min(win, S) // P
                        for c in range(2):
                            sp.dma_start(io["p_swa"][g].rearrange("(t p) c h d -> c h p t d", p=P)[c, h],
                                           kv[:, g, PT_TILES - keep:PT_TILES, c, :]).then_inc(s["stored"], 16)
                    sp.dma_start(io["smp_kv"][h], kv[0:NSMP, :, TILES - 1]).then_inc(s["stored"], 16)
                    sp.dma_start(io["smp_qk"][h], qkT[:, :, :, S:N].rearrange("p g c n -> p (g c) n"))\
                        .then_inc(s["stored"], 16)
                sp.wait_ge(s["stored"], 16 * NST * (H + 1))
                sp.wait_ge(s["o_stored"], 16 * (H + 1))
                sp.wait_ge(s["kept"], 16 * G * NB)

            @block.tensor
            def _(pe):
                pe.sem_inc(ring.used, ring.R)
                pe.wait_ge(s["const"], 64)

                def turn_qk(h, p, last_chunk=False):
                    g, t = divmod(p, TILES)
                    r = rows_of(t)
                    pe.wait_ge(s["rotated"], PR * h + p + 3)
                    pe.wait_ge(s["tq_read"], PR * h + (2 if p == 0 else p + 1))
                    ins = pe.transpose(ps[:, 2 + p % 2, 0:P], qrot[:, p % 2, :], ident[:])
                    if last_chunk:
                        ins.then_inc(ring.used, 1)
                    pe.transpose(ps[:, 2 + p % 2, P:2 * P], kv[:, g, t, 0, :], ident[:]).then_inc(s["tq_done"], 1)

                def scores(h, t):
                    pe.wait_ge(s["mx_read"], PT_TILES * h + t + 1)
                    for j, n, g, kt in runs_of(t):
                        ins = pe.matmul(ps[:, j // 4, (j % 4) * P:(j % 4 + n) * P], qkT[:, g, 0, t * P:(t + 1) * P],
                                        qkT[:, g, 1, kt * P:(kt + n) * P], start=True, stop=True)
                    ins.then_inc(s["s_done"], 1)

                def turn_p(h, t, q):
                    nblk = len(blocks_of(t))
                    pe.wait_ge(s["tp_read"], NQ * h + (2 if QB[t] + q == 0 else QB[t] + q + 1))
                    for j in range(4 * q, min(4 * q + 4, nblk)):
                        ins = pe.transpose(ps[:, 4 + (QB[t] + q) % 2, (j % 4) * P:(j % 4 + 1) * P],
                                           prob[:, t % 2, j * P:(j + 1) * P], ident[:])
                    ins.then_inc(s["tp_done"], 1)

                with pe.Fori(0, H) as h:
                    for p in range(PR):
                        g, t = divmod(p, TILES)
                        r = rows_of(t)
                        pe.wait_ge(s["ab_done"], PR * h + (2 if p == 0 else p + 1))
                        pe.wait_ge(s["v_done"], PR * h + (2 if p == 0 else p + 1))
                        for c in range(4):
                            j = 4 * g + c
                            if t == 0:
                                ring.wait(pe, CH * h, j)
                            for i in range(2):
                                k = 2 * c + i
                                x = slice(t * P, t * P + r)
                                w = slice(i * 3 * P, (i + 1) * 3 * P)
                                ins = mm3(pe, ps[0:r, p % 2, 0:3 * P], hT_hi[:, k, x], hT_lo[:, k, x],
                                          ring.hi[:, j % ring.R, w], ring.lo[:, j % ring.R, w], k == 0, k == KD - 1)
                            if t == TILES - 1 and c < 3:
                                ins.then_inc(ring.used, 1)
                        ins.then_inc(s["pj_done"], 1)
                        if p:
                            turn_qk(h, p - 1, t == TILES - 1)
                    turn_qk(h, PR - 1)
                    pe.wait_ge(s["tq_read"], PR * h + PR + 2)
                    pe.wait_ge(s["v_done"], PR * h + PR + 2)
                    scores(h, 0)
                    for t in range(PT_TILES):
                        if t + 1 < PT_TILES:
                            scores(h, t + 1)
                        bl = blocks_of(t)
                        nq = -(-len(bl) // 4)
                        pe.wait_ge(s["p_done"], PT_TILES * h + t + 1)
                        turn_p(h, t, 0)
                        pe.wait_ge(s["o_read"], PT_TILES * h + t + 1)
                        for q in range(nq):
                            if q + 1 < nq:
                                turn_p(h, t, q + 1)
                            pe.wait_ge(s["tp_read"], NQ * h + QB[t] + q + 3)
                            for j in range(4 * q, min(4 * q + 4, len(bl))):
                                g, kt = bl[j]
                                ins = pe.matmul(ps[:, 6 + t % 2, 0:P], kv[:, g, kt, 1, :],
                                                probT[:, (QB[t] + q) % 2, (j % 4) * P:(j % 4 + 1) * P],
                                                start=j == 0, stop=j == len(bl) - 1)
                        ins.then_inc(s["o_done"], 1)

            @block.scalar
            def _(act):
                act.sem_inc(s["v_done"], 2)
                act.sem_inc(s["tq_read"], 2)
                act.sem_inc(s["tp_read"], 2)
                act.sem_inc(s["o_read"], 2)
                act.sem_inc(s["stored"], 16 * NST)
                act.sem_inc(s["o_stored"], 16)

                def turned_qk(h, p):
                    g, t = divmod(p, TILES)
                    r = rows_of(t)
                    act.wait_ge(s["tq_done"], PR * h + p + 1)
                    act.activation(qkT[:, g, :, t * P:t * P + r],
                                   ps[:, 2 + p % 2, 0:2 * P].rearrange("p (a b) -> p a b", a=2)[:, :, 0:r],
                                   ACT.Copy).then_inc(s["tq_read"], 1)

                def exps(h, t):
                    w = len(blocks_of(t)) * P
                    act.wait_ge(s["nm_done"], PT_TILES * h + t + 1)
                    act.activation(prob[:, t % 2, 0:w], prob[:, t % 2, 0:w], ACT.Exp, bias=nm[:, t % 2:t % 2 + 1],
                                   accum_out=den[:, t % 2:t % 2 + 1]).then_inc(s["exp_done"], 1)

                with act.Fori(0, H) as h:
                    for j in range(6):
                        ring.round_hi(act, CH * h, j)
                    act.wait_ge(s["stored"], 16 * NST * h + 16 * NST)
                    for p in range(PR):
                        g, t = divmod(p, TILES)
                        r = rows_of(t)
                        act.wait_ge(s["pj_done"], PR * h + p + 1)
                        act.activation(kv[0:r, g, t, 1, :], ps[0:r, p % 2, 2 * P:3 * P], ACT.Copy)\
                            .then_inc(s["v_done"], 1)
                        if t == TILES - 1:
                            for j in ((6, 7, 8, 9), (10, 11), ())[g]:
                                ring.round_hi(act, CH * h, j)
                        if p:
                            turned_qk(h, p - 1)
                    turned_qk(h, PR - 1)
                    act.wait_ge(s["o_stored"], 16 * h + 16)
                    exps(h, 0)
                    for t in range(PT_TILES):
                        nblk = len(blocks_of(t))
                        for q in range(-(-nblk // 4)):
                            w = (min(4 * q + 4, nblk) - 4 * q) * P
                            act.wait_ge(s["tp_done"], NQ * h + QB[t] + q + 1)
                            act.activation(probT[:, (QB[t] + q) % 2, 0:w], ps[:, 4 + (QB[t] + q) % 2, 0:w],
                                           ACT.Copy).then_inc(s["tp_read"], 1)
                        if t + 1 < PT_TILES:
                            exps(h, t + 1)
                        act.wait_ge(s["o_done"], PT_TILES * h + t + 1)
                        act.activation(oT[:, t * P:(t + 1) * P], ps[:, 6 + t % 2, 0:P], ACT.Copy)\
                            .then_inc(s["o_read"], 1)
                    act.wait_ge(s["o_read"], PT_TILES * h + PT_TILES + 2)
                    act.dma_start(io["oT_scr"][0, bass.ts(h, P), 0:S], oT[:]).then_inc(s["o_stored"], 16)

            @block.vector
            def _(dve):
                dve.sem_inc(ring.ready, ring.RAW)
                dve.sem_inc(s["ab_done"], 2)
                dve.sem_inc(s["mx_read"], 1)
                dve.memset(kv[NSMP:P, :, TILES - 1], 0.0)
                dve.wait_ge(s["const"], 64)

                def rotate(h, p):
                    g, t = divmod(p, TILES)
                    r = rows_of(t)
                    dve.wait_ge(s["v_done"], PR * h + p + 3)
                    dve.wait_ge(s["rotated"], PR * h + (2 if p == 0 else p + 1))
                    x = ps[0:r, p % 2, 0:2 * HD].rearrange("p (a b c) -> p a b c", a=2, b=2)
                    co = cosb[0:r, t, :].rearrange("p (a b c) -> p a b c", a=1, b=1).broadcast_to([r, 2, 2, HD // 2])
                    dve.tensor_tensor(ra[0:r, p % 2], x, co, ALU.mult)
                    for i in range(2):
                        si = sinb[0:r, t, i, :].rearrange("p (a c) -> p a c", a=1).broadcast_to([r, 2, HD // 2])
                        ins = dve.tensor_tensor(rb[0:r, p % 2, :, i, :], x[:, :, 1 - i, :], si, ALU.mult)
                        if i:
                            ins.then_inc(s["ab_done"], 1)

                def mask_max(h, t):
                    dve.wait_ge(s["s_done"], PT_TILES * h + t + 1)
                    dve.tensor_scalar(spare[:], ident[:, 0:1], 1.0, None, ALU.mult)
                    runs = runs_of(t)
                    for i, (j, n, g, kt) in enumerate(runs):
                        at = mask_at(g, t - kt, n)
                        ins = dve.tensor_tensor_reduce(
                            prob[:, t % 2, j * P:(j + n) * P], ps[:, j // 4, (j % 4) * P:(j % 4 + n) * P],
                            mask[:, at * P:(at + n) * P], SCALE_A, LOWEST, ALU.add, ALU.max, mx[:, t % 2, i:i + 1])
                    ins.then_inc(s["mx_read"], 1)
                    dve.wait_ge(s["mx_read"], PT_TILES * h + t + 2)
                    dve.tensor_reduce(nm[:, t % 2:t % 2 + 1], mx[:, t % 2, 0:len(runs)], AX.X, ALU.max,
                                      negate=True).then_inc(s["nm_done"], 1)

                with dve.Fori(0, H) as h:
                    for j in range(6):
                        ring.rest_lo(dve, CH * h, j)
                    for p in range(PR):
                        g, t = divmod(p, TILES)
                        rotate(h, p)
                        if t == TILES - 1:
                            for j in ((6, 7, 8, 9), (10, 11), ())[g]:
                                ring.rest_lo(dve, CH * h, j)
                    mask_max(h, 0)
                    for t in range(PT_TILES):
                        w = len(blocks_of(t)) * P
                        dve.wait_ge(s["exp_done"], PT_TILES * h + t + 1)
                        dve.reciprocal(rden[:, t % 2:t % 2 + 1], den[:, t % 2:t % 2 + 1]).then_inc(s["rden_done"], 1)
                        dve.wait_ge(s["rden_done"], PT_TILES * h + t + 1)
                        dve.tensor_scalar(prob[:, t % 2, 0:w], prob[:, t % 2, 0:w], rden[:, t % 2:t % 2 + 1], None,
                                          ALU.mult).then_inc(s["p_done"], 1)
                        if t + 1 < PT_TILES:
                            mask_max(h, t + 1)

            @block.gpsimd
            def _(pool):
                pool.sem_inc(s["rotated"], 2)
                with pool.Fori(0, H) as h:
                    pool.wait_ge(s["stored"], 16 * NST * h + 16 * NST)
                    for p in range(PR):
                        g, t = divmod(p, TILES)
                        r = rows_of(t)
                        pool.wait_ge(s["ab_done"], PR * h + p + 3)
                        if p >= 2:
                            pool.wait_ge(s["tq_done"], PR * h + p - 1)
                        pool.tensor_tensor(qrot[0:r, p % 2, :].rearrange("p (a c) -> p a c", a=2), ra[0:r, p % 2, 0],
                                           rb[0:r, p % 2, 0], ALU.add)
                        pool.tensor_tensor(kv[0:r, g, t, 0, :].rearrange("p (a c) -> p a c", a=2), ra[0:r, p % 2, 1],
                                           rb[0:r, p % 2, 1], ALU.add).then_inc(s["rotated"], 1)

def memory_attention(nc, io, hT_hi, hT_lo, mT_hi, mT_lo):
    with ExitStack() as ctx:
        m = Mem(nc, ctx, "mem")
        ring = WeightRing(m, io["w_mem"], KD * P, 6)
        MT = NMEM // P
        KV_CH = 2 * 4
        CHUNKS = KV_CH + H
        ident = m.sb("ident", [P, P])
        kv = m.sb("kv", [P, MT, 2, H * HD])
        kT = m.sb("kT", [P, H, NMEM])
        qT = m.sb("qT", [P, H, N])
        prob = m.sb("prob", [P, 2, NMEM])
        probT = m.sb("probT", [P, 2, NMEM])
        oT = m.sb("oT", [P, H, S])
        nm, den, rden = m.sb("nm", [P, 2]), m.sb("den", [P, 2]), m.sb("rden", [P, 2])
        ps = m.ps("ps", [P, 8, 512])
        s = {n: m.sem(n) for n in ("const", "pj_done", "pj_read", "tk_done", "tk_read", "s_done", "nm_done",
                                   "exp_done", "rden_done", "p_done", "tp_done", "tp_read", "o_done", "o_read",
                                   "stored")}
        UNITS = 2 * MT + 3 * H
        ITS = [(h, t) for h in range(H) for t in range(PT_TILES)]
        ring.turns = None

        with nc.Block() as block:
            @block.sync
            def _(sp):
                sp.dma_start(ident[:], io["ident"]).then_inc(s["const"], 16)
                for j in range(CHUNKS):
                    ring.load(sp, 0, j)
                sp.wait_ge(s["pj_read"], 2 * MT)
                sp.dma_start(io["p_mem"].rearrange("(t p) c n -> p t c n", p=P), kv[:]).then_inc(s["stored"], 16)
                sp.wait_ge(s["pj_read"], UNITS)
                sp.dma_start(io["smp_qm"].rearrange("h p n -> p h n"), qT[:, :, S:N]).then_inc(s["stored"], 16)
                sp.wait_ge(s["o_read"], len(ITS))
                sp.dma_start(io["oT_scr"][2].rearrange("(h p) n -> p h n", p=P)[:, :, 0:S], oT[:])\
                    .then_inc(s["stored"], 16)
                sp.wait_ge(s["stored"], 48)

            @block.tensor
            def _(pe):
                pe.sem_inc(ring.used, ring.R)
                pe.wait_ge(s["const"], 16)
                u = 0
                for c in range(2):
                    for t in range(MT):
                        if u >= 4:
                            pe.wait_ge(s["pj_read"], u - 3)
                        for k in range(KD):
                            j = 4 * c + k // 2
                            if t == 0:
                                ring.wait(pe, 0, j)
                            w = slice(k % 2 * 512, k % 2 * 512 + 512)
                            ins = mm3(pe, ps[:, u % 4, :], mT_hi[:, k, t * P:(t + 1) * P], mT_lo[:, k, t * P:(t + 1) * P],
                                      ring.hi[:, j % ring.R, w], ring.lo[:, j % ring.R, w], k == 0, k == KD - 1)
                            if t == MT - 1 and k % 2 and k < KD - 1:
                                ins.then_inc(ring.used, 1)
                        ins.then_inc(s["pj_done"], 1)
                        u += 1
                    pe.wait_ge(s["pj_done"], u)
                    pe.sem_inc(ring.used, 1)
                for t in range(MT):
                    pe.wait_ge(s["pj_read"], t + 1)
                    for h in range(H):
                        ins = pe.transpose(ps[:, 4 + t, h * P:(h + 1) * P], kv[:, t, 0, h * P:(h + 1) * P], ident[:])
                    ins.then_inc(s["tk_done"], 1)
                for h in range(H):
                    j = KV_CH + h
                    ring.wait(pe, 0, j)
                    for c, (at, n) in enumerate(COL):
                        pe.wait_ge(s["pj_read"], u - 3)
                        for k in range(KD):
                            w = slice(k * P, (k + 1) * P)
                            ins = mm3(pe, ps[:, u % 4, 0:n], ring.hi[:, j % ring.R, w], ring.lo[:, j % ring.R, w],
                                      hT_hi[:, k, at:at + n], hT_lo[:, k, at:at + n], k == 0, k == KD - 1)
                        ins.then_inc(s["pj_done"], 1)
                        u += 1
                pe.wait_ge(s["pj_read"], UNITS)
                pe.wait_ge(s["tk_read"], MT)

                def scores(i):
                    h, t = ITS[i]
                    if i >= 2:
                        pe.wait_ge(s["exp_done"], i - 1)
                    pe.matmul(ps[:, i % 2, 0:NMEM], qT[:, h, t * P:(t + 1) * P], kT[:, h, :], start=True,
                              stop=True).then_inc(s["s_done"], 1)

                def turn(i):
                    pe.wait_ge(s["p_done"], i + 1)
                    if i >= 2:
                        pe.wait_ge(s["tp_read"], i - 1)
                    for b in range(MT):
                        ins = pe.transpose(ps[:, 4 + i % 2, b * P:(b + 1) * P], prob[:, i % 2, b * P:(b + 1) * P], ident[:])
                    ins.then_inc(s["tp_done"], 1)

                def values(i):
                    h, t = ITS[i]
                    pe.wait_ge(s["tp_read"], i + 1)
                    if i >= 2:
                        pe.wait_ge(s["o_read"], i - 1)
                    for b in range(MT):
                        ins = pe.matmul(ps[:, 6 + i % 2, 0:P], kv[:, b, 1, h * P:(h + 1) * P],
                                        probT[:, i % 2, b * P:(b + 1) * P], start=b == 0, stop=b == MT - 1)
                    ins.then_inc(s["o_done"], 1)

                n = len(ITS)
                for i in range(n + 2):
                    if i < n:
                        scores(i)
                    if 1 <= i <= n:
                        turn(i - 1)
                    if i >= 2:
                        values(i - 2)

            @block.scalar
            def _(act):
                u = 0

                def read(dst, src, scale=1.0):
                    nonlocal u
                    act.wait_ge(s["pj_done"], u + 1)
                    act.activation(dst, src, ACT.Copy, scale=scale).then_inc(s["pj_read"], 1)
                    u += 1

                for j in range(4):
                    ring.round_hi(act, 0, j)
                for j in range(4, 6):
                    ring.round_hi(act, 0, j)
                for c in range(2):
                    for t in range(MT):
                        read(kv[:, t, c, :], ps[:, u % 4, :])
                    if c == 0:
                        for j in (6, 7, 8, 9):
                            ring.round_hi(act, 0, j)
                for j in (10, 11):
                    ring.round_hi(act, 0, j)
                for t in range(MT):
                    act.wait_ge(s["tk_done"], t + 1)
                    act.activation(kT[:, :, t * P:(t + 1) * P], ps[:, 4 + t, :].rearrange("p (h n) -> p h n", h=H),
                                   ACT.Copy).then_inc(s["tk_read"], 1)
                for h in range(H):
                    for at, n in COL:
                        read(qT[:, h, at:at + n], ps[:, u % 4, 0:n], SCALE_A)

                def exps(i):
                    act.wait_ge(s["nm_done"], i + 1)
                    act.activation(prob[:, i % 2, :], ps[:, i % 2, 0:NMEM], ACT.Exp, bias=nm[:, i % 2:i % 2 + 1],
                                   accum_out=den[:, i % 2:i % 2 + 1]).then_inc(s["exp_done"], 1)

                n = len(ITS)
                for i in range(n + 2):
                    if i < n:
                        exps(i)
                    if 1 <= i <= n:
                        act.wait_ge(s["tp_done"], i)
                        act.activation(probT[:, (i - 1) % 2, :], ps[:, 4 + (i - 1) % 2, 0:NMEM], ACT.Copy)\
                            .then_inc(s["tp_read"], 1)
                    if i >= 2:
                        h, t = ITS[i - 2]
                        act.wait_ge(s["o_done"], i - 1)
                        act.activation(oT[:, h, t * P:(t + 1) * P], ps[:, 6 + i % 2, 0:P], ACT.Copy)\
                            .then_inc(s["o_read"], 1)

            @block.vector
            def _(dve):
                dve.sem_inc(ring.ready, ring.RAW)
                for j in range(CHUNKS):
                    ring.rest_lo(dve, 0, j)
                n = len(ITS)
                for i in range(n + 1):
                    if i < n:
                        dve.wait_ge(s["s_done"], i + 1)
                        dve.tensor_reduce(nm[:, i % 2:i % 2 + 1], ps[:, i % 2, 0:NMEM], AX.X, ALU.max,
                                          negate=True).then_inc(s["nm_done"], 1)
                    if i >= 1:
                        b = (i - 1) % 2
                        dve.wait_ge(s["exp_done"], i)
                        dve.reciprocal(rden[:, b:b + 1], den[:, b:b + 1]).then_inc(s["rden_done"], 1)
                        dve.wait_ge(s["rden_done"], i)
                        dve.tensor_scalar(prob[:, b, :], prob[:, b, :], rden[:, b:b + 1], None, ALU.mult)\
                            .then_inc(s["p_done"], 1)


def latent_projections(nc, io, hT_hi, hT_lo):
    with ExitStack() as ctx:
        m = Mem(nc, ctx, "lat")
        ring = WeightRing(m, io["w_lat"], 2 * QR, 6)
        KQ, KK = QR // P, KR // P
        UNIT = ((QR, KQ), (KR + RB, KK))
        ident = m.sb("ident", [P, P])
        gain = m.sb("gain", [P, QR + KR])
        cosb = m.sb("cos", [P, TILES, RB // 2])
        sinb = m.sb("sin", [P, TILES, 2, RB // 2])
        raw = m.sb("raw", [P, 2, QR])
        sq = m.sb("sq", [P, QR])
        ss = m.sb("ss", [P, 2 * TILES])
        rstd = m.sb("rstd", [P, 2 * TILES])
        half = m.sb("half", [P, 1])
        xq = m.sb("xq", [P, 2, QR])
        xk = m.sb("xk", [P, TILES, KR + RB])
        ra, rb = m.sb("ra", [P, 2, HB, RB]), m.sb("rb", [P, 2, HB, RB])
        qT_hi, qT_lo = m.sb("qT_hi", [P, KQ, N], F32R), m.sb("qT_lo", [P, KQ, N], F32R)
        cT_hi, cT_lo = m.sb("cT_hi", [P, KK, N], F32R), m.sb("cT_lo", [P, KK, N], F32R)
        krT = m.sb("krT", [RB, N])
        q = m.sb("q", [P, 2, HB, NOPE + RB])
        qTs = m.sb("qTs", [NOPE + RB, 2, HB, P])
        st = m.sb("st", [P, 2, 512])
        ps = m.ps("ps", [P, 8, 512])
        s = {n: m.sem(n) for n in ("const", "half", "pj_done", "pj_read", "sq_done", "mean_done", "rstd_done",
                                   "x_done", "ra_done", "rot_done", "t_done", "hi_done", "lo_done", "qp_done", "qp_read",
                                   "qa_done", "q_done", "qt_done", "qt_read", "e_done", "e_read", "kstored", "kr_read")}
        q_stored = [m.sem(f"q_stored{i}") for i in range(2)]
        e_stored = [m.sem(f"e_stored{i}") for i in range(2)]
        STEPS = [(u, t) for u in range(2) for t in range(TILES)]
        CHUNKS = 8 + KQ + KK + KK
        EK = [(pair, c) for pair in range(HB // 2) for c in range(S // 512)]
        EV = list(range(PT_TILES))
        NE = len(EK) + len(EV)

        with nc.Block() as block:
            @block.sync
            def _(sp):
                for dst, src in ((ident, "ident"), (gain, "gain_lat"), (cosb, "cos_b"), (sinb, "sin_b")):
                    sp.dma_start(dst[:], io[src]).then_inc(s["const"], 16)
                for j in range(CHUNKS):
                    ring.load(sp, 0, j)
                sp.wait_ge(s["x_done"], 2 * TILES)
                sp.wait_ge(s["rot_done"], TILES)
                for t0, t1, r, ckv, kr in ((0, PT_TILES, P, "p_ckv", "p_kr"), (PT_TILES, TILES, NSMP, "s_ckv", "s_kr")):
                    sp.dma_start(io[ckv].rearrange("(t p) c -> p t c", p=r), xk[0:r, t0:t1, 0:KR]).then_inc(s["kstored"], 16)
                    sp.dma_start(io[kr].rearrange("(t p) c -> p t c", p=r), xk[0:r, t0:t1, KR:KR + RB])\
                        .then_inc(s["kstored"], 16)
                sp.wait_ge(s["kr_read"], TILES)
                sp.dma_start(io["krT_scr"], krT[:]).then_inc(s["kstored"], 16)
                for t in range(TILES):
                    r = rows_of(t)
                    sp.wait_ge(s["qt_read"], t + 1)
                    sp.dma_start(io["qT_scr"].rearrange("h c n -> c h n")[:, :, t * P:t * P + r], qTs[:, t % 2, :, 0:r])\
                        .then_inc(q_stored[t % 2], 16)
                for i in range(NE):
                    sp.wait_ge(s["e_read"], i + 1)
                    if i < len(EK):
                        pair, c = EK[i]
                        dst = io["kT_scr"][pair * P:(pair + 1) * P, c * 512:(c + 1) * 512]
                    else:
                        t = EV[i - len(EK)]
                        dst = io["v_scr"][t * P:(t + 1) * P, :]
                    sp.dma_start(dst, st[:, i % 2, :]).then_inc(e_stored[i % 2], 16)
                sp.wait_ge(s["kstored"], 16 * 5)
                for i in range(2):
                    sp.wait_ge(q_stored[i], 16 * ((TILES + 1 - i) // 2))
                    sp.wait_ge(e_stored[i], 16 * (NE // 2))

            @block.tensor
            def _(pe):
                pe.sem_inc(ring.used, ring.R)
                pe.wait_ge(s["const"], 64)

                def turn(i):
                    u, t = STEPS[i]
                    r, nb = rows_of(t), UNIT[u][1]
                    pe.wait_ge(s["x_done"], i + 1)
                    if i >= 2:
                        pe.wait_ge(s["lo_done"], i - 1)
                    src = xk[0:r, t, :] if u else xq[0:r, t % 2, :]
                    if u:
                        pe.wait_ge(s["rot_done"], t + 1)
                        if t >= 2:
                            pe.wait_ge(s["kr_read"], t - 1)
                        pe.transpose(ps[0:RB, 4 + i % 2, 3 * P:3 * P + r], src[:, KR:KR + RB], ident[0:r, 0:r])
                    for b in range(nb):
                        ins = pe.transpose(ps[:, 4 + i % 2, b * P:b * P + r], src[:, b * P:(b + 1) * P], ident[0:r, 0:r])
                    ins.then_inc(s["t_done"], 1)

                for i, (u, t) in enumerate(STEPS):
                    r, (cols, _) = rows_of(t), UNIT[u]
                    if i >= 2:
                        pe.wait_ge(s["pj_read"], i - 1)
                    for k in range(KD):
                        j = 4 * u + k // 2
                        if t == 0:
                            ring.wait(pe, 0, j)
                        w = slice(k % 2 * cols, (k % 2 + 1) * cols)
                        x = slice(t * P, t * P + r)
                        ins = mm3(pe, ps[0:r, i % 2, 0:cols], hT_hi[:, k, x], hT_lo[:, k, x], ring.hi[:, j % ring.R, w],
                                  ring.lo[:, j % ring.R, w], k == 0, k == KD - 1)
                        if t == TILES - 1 and k % 2 and k < KD - 1:
                            ins.then_inc(ring.used, 1)
                    ins.then_inc(s["pj_done"], 1)
                    if t == TILES - 1:
                        pe.wait_ge(s["pj_done"], i + 1)
                        pe.sem_inc(ring.used, 1)
                    if i:
                        turn(i - 1)
                turn(len(STEPS) - 1)

                def turn_q(t):
                    r = rows_of(t)
                    pe.wait_ge(s["q_done"], t + 1)
                    if t >= 2:
                        pe.wait_ge(s["qt_read"], t - 1)
                    bank = 4 + 2 * (t % 2)
                    for h in range(HB):
                        ins = pe.transpose(ps[0:NOPE + RB, bank + h // 4, (h % 4) * P:(h % 4) * P + r], q[0:r, t % 2, h, :],
                                           ident[0:r, 0:r])
                    ins.then_inc(s["qt_done"], 1)

                pe.wait_ge(s["lo_done"], 2 * TILES)
                pe.wait_ge(s["kr_read"], TILES)
                for t in range(TILES):
                    r = rows_of(t)
                    if t >= 2:
                        pe.wait_ge(s["qp_read"], t - 1)
                    for c in range(2):
                        for k in range(KQ):
                            j = 8 + k
                            if t == 0 and c == 0:
                                ring.wait(pe, 0, j)
                            w = slice(c * QR, (c + 1) * QR)
                            x = slice(t * P, t * P + r)
                            ins = mm3(pe, ps[0:r, 2 * (t % 2) + c, 0:QR], qT_hi[:, k, x], qT_lo[:, k, x],
                                      ring.hi[:, j % ring.R, w], ring.lo[:, j % ring.R, w], k == 0, k == KQ - 1)
                    ins.then_inc(s["qp_done"], 1)
                    if t:
                        turn_q(t - 1)
                turn_q(TILES - 1)
                pe.wait_ge(s["qp_done"], TILES)
                pe.sem_inc(ring.used, KQ)
                pe.wait_ge(s["qp_read"], TILES)
                for i in range(NE):
                    if i >= 2:
                        pe.wait_ge(s["e_read"], i - 1)
                    for k in range(KK):
                        if i < len(EK):
                            pair, c = EK[i]
                            j = 8 + KQ + k
                            w = slice(pair * P, (pair + 1) * P)
                            x = slice(c * 512, (c + 1) * 512)
                            a = ring.hi[:, j % ring.R, w], ring.lo[:, j % ring.R, w], cT_hi[:, k, x], cT_lo[:, k, x]
                        else:
                            t = EV[i - len(EK)]
                            j = 8 + KQ + KK + k
                            x = slice(t * P, (t + 1) * P)
                            a = cT_hi[:, k, x], cT_lo[:, k, x], ring.hi[:, j % ring.R, 0:512], ring.lo[:, j % ring.R, 0:512]
                        if i in (0, len(EK)):
                            ring.wait(pe, 0, j)
                        ins = mm3(pe, ps[:, i % 2, :], *a, k == 0, k == KK - 1)
                    ins.then_inc(s["e_done"], 1)

            def read_q(act, t):
                r = rows_of(t)
                act.wait_ge(s["qt_done"], t + 1)
                if t >= 2:
                    act.wait_ge(q_stored[t % 2], 16 * (t // 2))
                bank = 4 + 2 * (t % 2)
                act.activation(qTs[:, t % 2, :, 0:r].rearrange("p (a h) n -> p a h n", a=2),
                               ps[0:NOPE + RB, bank:bank + 2, :].rearrange("p a (h n) -> p a h n", h=4)[:, :, :, 0:r],
                               ACT.Copy).then_inc(s["qt_read"], 1)

            @block.scalar
            def _(act):
                for j in range(6):
                    ring.round_hi(act, 0, j)

                def split(i):
                    u, t = STEPS[i]
                    r, nb = rows_of(t), UNIT[u][1]
                    act.wait_ge(s["t_done"], i + 1)
                    if u:
                        act.activation(krT[:, t * P:t * P + r], ps[0:RB, 4 + i % 2, 3 * P:3 * P + r], ACT.Copy)\
                            .then_inc(s["kr_read"], 1)
                    hi = cT_hi if u else qT_hi
                    act.activation(hi[:, 0:nb, t * P:t * P + r],
                                   ps[:, 4 + i % 2, 0:nb * P].rearrange("p (b n) -> p b n", b=nb)[:, :, 0:r],
                                   ACT.Copy).then_inc(s["hi_done"], 1)

                for i, (u, t) in enumerate(STEPS):
                    r, (cols, nb) = rows_of(t), UNIT[u]
                    act.wait_ge(s["pj_done"], i + 1)
                    if i:
                        act.wait_ge(s["sq_done"], i)
                    act.activation(sq[0:r, 0:nb * P], ps[0:r, i % 2, 0:nb * P], ACT.Square, accum_out=ss[0:r, i:i + 1])\
                        .then_inc(s["sq_done"], 1)
                    if i >= 2:
                        act.wait_ge(s["x_done"], i - 1)
                        if u and t >= 2:
                            act.wait_ge(s["ra_done"], 2 * (t - 1))
                    act.activation(raw[0:r, i % 2, 0:cols], ps[0:r, i % 2, 0:cols], ACT.Copy).then_inc(s["pj_read"], 1)
                    if t == TILES - 1:
                        for j in ((6, 7, 8, 9), (10, 11, 12, 13))[u]:
                            ring.round_hi(act, 0, j)
                    if i:
                        split(i - 1)
                split(len(STEPS) - 1)
                for t in range(TILES):
                    r = rows_of(t)
                    act.wait_ge(s["qp_done"], t + 1)
                    if t >= 2:
                        act.wait_ge(s["qt_done"], t - 1)
                    act.activation(q[0:r, t % 2].rearrange("p h c -> p (h c)").rearrange("p (a c) -> p a c", a=2),
                                   ps[0:r, 2 * (t % 2):2 * (t % 2) + 2, 0:QR], ACT.Copy, scale=SCALE_B)\
                        .then_inc(s["qp_read"], 1)
                    if t:
                        turned_q = t - 1
                        read_q(act, turned_q)
                read_q(act, TILES - 1)
                ring.round_hi(act, 0, CHUNKS - 1)
                for i in range(NE):
                    act.wait_ge(s["e_done"], i + 1)
                    if i >= 2:
                        act.wait_ge(e_stored[i % 2], 16 * (i // 2))
                    act.activation(st[:, i % 2, :], ps[:, i % 2, :], ACT.Copy).then_inc(s["e_read"], 1)

            @block.gpsimd
            def _(pool):
                pool.memset(half[:], -0.5).then_inc(s["half"], 1)
                pool.wait_ge(s["half"], 1)
                for i, (u, t) in enumerate(STEPS):
                    r = rows_of(t)
                    pool.wait_ge(s["sq_done"], i + 1)
                    pool.tensor_scalar(ss[0:r, i:i + 1], ss[0:r, i:i + 1], 1.0 / (UNIT[u][1] * P), EPS, ALU.mult,
                                       ALU.add).then_inc(s["mean_done"], 1)
                    pool.wait_ge(s["mean_done"], i + 1)
                    pool.tensor_tensor(rstd[0:r, i:i + 1], ss[0:r, i:i + 1], half[0:r, :], ALU.pow)\
                        .then_inc(s["rstd_done"], 1)

            @block.vector
            def _(dve):
                dve.sem_inc(ring.ready, ring.RAW)
                for j in range(6):
                    ring.rest_lo(dve, 0, j)
                dve.wait_ge(s["const"], 64)

                def rotate(dst, src, t, heads, b, count, done):
                    r = rows_of(t)
                    half_ = RB // 2
                    co = cosb[0:r, t, :].rearrange("p (a b c) -> p a b c", a=1, b=1).broadcast_to([r, heads, 2, half_])
                    a = ra[0:r, b, 0:heads, :].rearrange("p h (i c) -> p h i c", i=2)
                    c = rb[0:r, b, 0:heads, :].rearrange("p h (i c) -> p h i c", i=2)
                    dve.tensor_tensor(a, src, co, ALU.mult)
                    for i in range(2):
                        si = sinb[0:r, t, i, :].rearrange("p (a c) -> p a c", a=1).broadcast_to([r, heads, half_])
                        dve.tensor_tensor(c[:, :, i, :], src[:, :, 1 - i, :], si, ALU.mult).then_inc(s["ra_done"], 1)
                    dve.wait_ge(s["ra_done"], count + 2)
                    dve.tensor_tensor(dst, a, c, ALU.add).then_inc(done, 1)

                def rest(i):
                    u, t = STEPS[i]
                    r, nb = rows_of(t), UNIT[u][1]
                    hi, lo = (cT_hi, cT_lo) if u else (qT_hi, qT_lo)
                    dve.wait_ge(s["hi_done"], i + 1)
                    x = slice(t * P, t * P + r)
                    dve.tensor_tensor(lo[:, 0:nb, x], ps[:, 4 + i % 2, 0:nb * P].rearrange("p (b n) -> p b n", b=nb)[:, :, 0:r],
                                      hi[:, 0:nb, x].bitcast(F32), ALU.subtract).then_inc(s["lo_done"], 1)

                for i, (u, t) in enumerate(STEPS):
                    r, nb = rows_of(t), UNIT[u][1]
                    dve.wait_ge(s["rstd_done"], i + 1)
                    dve.wait_ge(s["pj_read"], i + 1)
                    if i >= 2:
                        dve.wait_ge(s["t_done"], i - 1)
                    dst = xk[0:r, t, 0:KR] if u else xq[0:r, t % 2, :]
                    dve.scalar_tensor_tensor(dst, raw[0:r, i % 2, 0:nb * P], rstd[0:r, i:i + 1],
                                             gain[0:r, u * QR:u * QR + nb * P], ALU.mult, ALU.mult).then_inc(s["x_done"], 1)
                    if u:
                        rotate(xk[0:r, t, KR:].rearrange("p (a i c) -> p a i c", a=1, i=2),
                               raw[0:r, i % 2, KR:KR + RB].rearrange("p (a i c) -> p a i c", a=1, i=2), t, 1, t % 2,
                               2 * t, s["rot_done"])
                    if t == TILES - 1:
                        for j in ((6, 7, 8, 9), (10, 11, 12, 13))[u]:
                            ring.rest_lo(dve, 0, j)
                    if i:
                        rest(i - 1)
                rest(len(STEPS) - 1)
                for t in range(TILES):
                    r = rows_of(t)
                    dve.wait_ge(s["qp_read"], t + 1)
                    v = q[0:r, t % 2, :, NOPE:].rearrange("p h (i c) -> p h i c", i=2)
                    rotate(v, v, t, HB, t % 2, 2 * TILES + 2 * t, s["q_done"])
                ring.rest_lo(dve, 0, CHUNKS - 1)


def latent_attention(nc, io):
    with ExitStack() as ctx:
        m = Mem(nc, ctx, "la")
        C = NOPE + RB
        PAIRS = HB // 2
        ident = m.sb("ident", [P, P])
        mask = m.sb("mask", [P, S])
        qT = m.sb("qT", [C, 2, 2, S])
        kT = m.sb("kT", [C, 2, 2, S])
        v = m.sb("v", [P, 2, PT_TILES, 2 * VD])
        prob = m.sb("prob", [P, 2, S])
        probT = m.sb("probT", [P, 2, 512])
        oT = m.sb("oT", [P, 2, S])
        spare = m.sb("spare", [P, 1])
        mx, nm, den, rden = (m.sb(n, [P, 2]) for n in ("mx", "nm", "den", "rden"))
        ps = m.ps("ps", [P, 8, 512])
        s = {n: m.sem(n) for n in ("const", "s_done", "mx_read", "nm_done", "exp_done", "rden_done", "p_done", "tp_done",
                                   "tp_read", "o_done", "o_read", "pair_used")}
        landed = [m.sem(f"landed{i}") for i in range(2)]
        o_stored = [m.sem(f"o_stored{i}") for i in range(2)]
        ITS = [(b, a, t) for b in range(2) for a in range(2) for t in range(PT_TILES)]
        NI = len(ITS)
        QB = [0]
        for _, _, t in ITS:
            QB.append(QB[-1] + t // 4 + 1)
        NQ = QB[-1]
        assert NQ % 2 == 0

        with nc.Block() as block:
            @block.sync
            def _(sp):
                sp.dma_start(ident[:], io["ident"]).then_inc(s["const"], 16)
                sp.dma_start(mask[:], io["mask_c"]).then_inc(s["const"], 16)
                with sp.Fori(0, PAIRS // 2) as g:
                    for b in range(2):
                        pair = 2 * g + b
                        sp.wait_ge(s["pair_used"], 2 * g + b + 1)
                        sp.dma_start(qT[:, b], io["qT_scr"].rearrange("(a h) c n -> a c h n", h=2)[pair][:, :, 0:S])\
                            .then_inc(landed[b], 16)
                        sp.dma_start(kT[0:NOPE, b], io["kT_scr"].rearrange("(a h c) n -> a c h n", h=2, c=NOPE)[pair])\
                            .then_inc(landed[b], 16)
                        for a in range(2):
                            sp.dma_start(kT[NOPE:C, b, a], io["krT_scr"][:, 0:S]).then_inc(landed[b], 16)
                        sp.dma_start(v[:, b], io["v_scr"].rearrange("(t p) (a c) -> a p t c", p=P, c=2 * VD)[pair])\
                            .then_inc(landed[b], 16)

            @block.tensor
            def _(pe):
                pe.sem_inc(s["pair_used"], 2)
                pe.wait_ge(s["const"], 32)

                def scores(g, i):
                    b, a, t = ITS[i]
                    if a == 0 and t == 0:
                        pe.wait_ge(landed[b], 80 * g + 80)
                    pe.wait_ge(s["mx_read"], NI * g + i + 1)
                    w = (t + 1) * P
                    for c in range(0, w, 512):
                        n = min(512, w - c)
                        ins = pe.matmul(ps[:, 2 * (i % 2) + c // 512, 0:n], qT[:, b, a, t * P:(t + 1) * P],
                                        kT[:, b, a, c:c + n], start=True, stop=True)
                    ins.then_inc(s["s_done"], 1)

                def turn(g, i, q):
                    b, a, t = ITS[i]
                    n = QB[i] + q
                    pe.wait_ge(s["tp_read"], NQ * g + n + 1)
                    for j in range(4 * q, min(4 * q + 4, t + 1)):
                        ins = pe.transpose(ps[:, 4 + n % 2, (j % 4) * P:(j % 4 + 1) * P], prob[:, i % 2, j * P:(j + 1) * P],
                                           ident[:])
                    ins.then_inc(s["tp_done"], 1)

                with pe.Fori(0, PAIRS // 2) as g:
                    scores(g, 0)
                    for i, (b, a, t) in enumerate(ITS):
                        if i + 1 < NI:
                            scores(g, i + 1)
                        pe.wait_ge(s["p_done"], NI * g + i + 1)
                        nq = t // 4 + 1
                        turn(g, i, 0)
                        pe.wait_ge(s["o_read"], NI * g + i + 1)
                        for q in range(nq):
                            if q + 1 < nq:
                                turn(g, i, q + 1)
                            n = QB[i] + q
                            pe.wait_ge(s["tp_read"], NQ * g + n + 3)
                            for j in range(4 * q, min(4 * q + 4, t + 1)):
                                ins = pe.matmul(ps[a * VD:(a + 1) * VD, 6 + i % 2, 0:P], v[:, b, j, a * VD:(a + 1) * VD],
                                                probT[:, n % 2, (j % 4) * P:(j % 4 + 1) * P], start=j == 0, stop=j == t)
                        ins.then_inc(s["o_done"], 1)
                        if a == 1 and t == PT_TILES - 1:
                            pe.wait_ge(s["o_done"], NI * g + i + 1)
                            pe.sem_inc(s["pair_used"], 1)

            @block.scalar
            def _(act):
                act.sem_inc(s["tp_read"], 2)
                act.sem_inc(s["o_read"], 2)
                for b in range(2):
                    act.sem_inc(o_stored[b], 16)

                def exps(g, i):
                    w = (ITS[i][2] + 1) * P
                    act.wait_ge(s["nm_done"], NI * g + i + 1)
                    act.activation(prob[:, i % 2, 0:w], prob[:, i % 2, 0:w], ACT.Exp, bias=nm[:, i % 2:i % 2 + 1],
                                   accum_out=den[:, i % 2:i % 2 + 1]).then_inc(s["exp_done"], 1)

                with act.Fori(0, PAIRS // 2) as g:
                    exps(g, 0)
                    for i, (b, a, t) in enumerate(ITS):
                        for q in range(t // 4 + 1):
                            n = QB[i] + q
                            w = (min(4 * q + 4, t + 1) - 4 * q) * P
                            act.wait_ge(s["tp_done"], NQ * g + n + 1)
                            act.activation(probT[:, n % 2, 0:w], ps[:, 4 + n % 2, 0:w], ACT.Copy).then_inc(s["tp_read"], 1)
                        if i + 1 < NI:
                            exps(g, i + 1)
                        if a == 0 and t == 0:
                            act.wait_ge(o_stored[b], 16 * g + 16)
                        act.wait_ge(s["o_done"], NI * g + i + 1)
                        act.activation(oT[a * VD:(a + 1) * VD, b, t * P:(t + 1) * P],
                                       ps[a * VD:(a + 1) * VD, 6 + i % 2, 0:P], ACT.Copy).then_inc(s["o_read"], 1)
                        if a == 1 and t == PT_TILES - 1:
                            act.wait_ge(s["o_read"], NI * g + i + 3)
                            act.dma_start(io["oT_scr"][1].rearrange("(a p) n -> a p n", p=P)[2 * g + b][:, 0:S], oT[:, b])\
                                .then_inc(o_stored[b], 16)
                for b in range(2):
                    act.wait_ge(o_stored[b], 16 * (PAIRS // 2) + 16)

            @block.vector
            def _(dve):
                dve.sem_inc(s["mx_read"], 2)
                dve.wait_ge(s["const"], 32)

                def mask_max(g, i):
                    b, a, t = ITS[i]
                    w = (t + 1) * P
                    dve.wait_ge(s["s_done"], NI * g + i + 1)
                    dve.tensor_scalar(spare[:], ident[:, 0:1], 1.0, None, ALU.mult)
                    sc = ps[:, 2 * (i % 2):2 * (i % 2) + 2, :].rearrange("p a n -> p (a n)")
                    dve.tensor_tensor_reduce(prob[:, i % 2, 0:w], sc[:, 0:w], mask[:, S - w:S], 1.0, LOWEST, ALU.add,
                                             ALU.max, mx[:, i % 2:i % 2 + 1]).then_inc(s["mx_read"], 1)
                    dve.wait_ge(s["mx_read"], NI * g + i + 3)
                    dve.tensor_scalar(nm[:, i % 2:i % 2 + 1], mx[:, i % 2:i % 2 + 1], -1.0, None, ALU.mult)\
                        .then_inc(s["nm_done"], 1)

                with dve.Fori(0, PAIRS // 2) as g:
                    mask_max(g, 0)
                    for i, (b, a, t) in enumerate(ITS):
                        w = (t + 1) * P
                        dve.wait_ge(s["exp_done"], NI * g + i + 1)
                        dve.reciprocal(rden[:, i % 2:i % 2 + 1], den[:, i % 2:i % 2 + 1]).then_inc(s["rden_done"], 1)
                        dve.wait_ge(s["rden_done"], NI * g + i + 1)
                        dve.tensor_scalar(prob[:, i % 2, 0:w], prob[:, i % 2, 0:w], rden[:, i % 2:i % 2 + 1], None,
                                          ALU.mult).then_inc(s["p_done"], 1)
                        if i + 1 < NI:
                            mask_max(g, i + 1)



CK = [128, 512, 512]
KEYS = sum(CK)
VBLK = (KEYS + NMEM) // P
WIN = KEYS + G * NSMP


def sample_attention(nc, io):
    with ExitStack() as ctx:
        m = Mem(nc, ctx, "sa")
        BH = 4
        R = BH * H * TS
        ident = m.sb("ident", [P, P])
        mask = m.sb("mask", [P, WIN])
        qk = m.sb("qk", [P, H, 2 * G, NSMP])
        qm = m.sb("qm", [P, H, NSMP])
        vnew = m.sb("vnew", [NSMP, H, G, HD])
        qz = m.sb("qz", [P, NB, G + 1, H, H * TS])
        kc = m.sb("kc", [P, 2, H, KEYS + NMEM])
        vc = m.sb("vc", [P, 3, VBLK, 2 * HD])
        prob = m.sb("prob", [P, WIN + NMEM])
        probT = m.sb("probT", [P, VBLK + G, P])
        out = m.sb("out", [P, 512])
        mx, nm, den, rden = m.sb("mx", [P, 4]), m.sb("nm", [P, 2]), m.sb("den", [P, 2]), m.sb("rden", [P, 2])
        ps = m.ps("ps", [P, 8, 512])
        s = {n: m.sem(n) for n in ("const", "zeroed", "spread", "k_used", "v_used", "s_done", "mx_done", "nm_done",
                                   "exp_done", "rden_done", "p_done", "tp_done", "tp_read", "o_done", "o_read", "stored",
                                   "mask_used", "masked")}
        k_in = [m.sem(f"k_in{i}") for i in range(2)]
        v_in = [m.sem(f"v_in{i}") for i in range(3)]
        PB = [(P * i, P) for i in range(KEYS // P)] + [(WIN + P * i, P) for i in range(NMEM // P)]
        PB += [(KEYS + NSMP * g, NSMP) for g in range(G)]
        NQ = -(-len(PB) // 4)

        with nc.Block() as block:
            @block.sync
            def _(sp):
                for dst, src in ((ident[:], io["ident"]), (qk[:], io["smp_qk"].rearrange("h p c n -> p h c n")),
                                 (qm[:], io["smp_qm"].rearrange("h p n -> p h n"))):
                    sp.dma_start(dst, src).then_inc(s["const"], 16)
                for g in range(G):
                    sp.dma_start(vnew[:, :, g], io["smp_kv"].rearrange("h n g c d -> c g n h d")[1, g]).then_inc(s["const"], 16)
                for g in range(G):
                    for h in range(H):
                        for c in range(2):
                            sp.dma_start(io["s_swa_new"][g].rearrange("b t c h d -> c h b t d")[c, h],
                                         io["smp_kv"].rearrange("h (b t) g c d -> g c h b t d", b=NB)[g, c, h])\
                                .then_inc(s["stored"], 16)

                def load_k(b):
                    if b >= 2:
                        sp.wait_ge(s["k_used"], b - 1)
                    sp.dma_start(kc[:, b % 2], io["k_smp"][b]).then_inc(k_in[b % 2], 16)

                def load_v(i):
                    if i >= 3:
                        sp.wait_ge(s["v_used"], i - 2)
                    sp.dma_start(vc[:, i % 3], io["v_smp"][i]).then_inc(v_in[i % 3], 16)

                sp.dma_start(mask[:], io["mask_s"][0]).then_inc(s["masked"], 16)
                for b in range(4):
                    load_k(b)
                for i in range(3):
                    load_v(i)
                sp.wait_ge(s["mask_used"], 1)
                sp.dma_start(mask[:], io["mask_s"][1]).then_inc(s["masked"], 16)
                for ks, vs in (((4, 5), range(3, NB)), ((6, 7), range(NB, 2 * NB))):
                    for b in ks:
                        load_k(b)
                    for i in vs:
                        load_v(i)
                sp.wait_ge(s["o_read"], 1)
                for br, at in ((0, 0), (2, H * NSMP)):
                    sp.dma_start(io["oT_scr"][br].rearrange("(h p) n -> p h n", p=P)[:, :, S:N],
                                 out[:, at:at + H * NSMP].rearrange("p (h n) -> p h n", h=H)).then_inc(s["stored"], 16)
                sp.wait_ge(s["stored"], 16 * (G * H * 2 + 2))

            @block.tensor
            def _(pe):
                pe.wait_ge(s["const"], 16 * (3 + G))
                pe.wait_ge(s["spread"], 1)

                def scores(half):
                    if half:
                        pe.wait_ge(s["exp_done"], 1)
                    for i in range(BH):
                        b = BH * half + i
                        pe.wait_ge(k_in[b % 2], 16 * (b // 2 + 1))
                        for bank, g, at, n in ((0, 1, CK[0], CK[1]), (1, 2, CK[0] + CK[1], CK[2]), (2, 0, 0, CK[0]),
                                               (3, G, KEYS, NMEM)):
                            for h in range(H):
                                ins = pe.matmul(ps[32 * i:32 * i + 32, bank, 0:n], qz[:, b, g, h, :],
                                                kc[:, b % 2, h, at:at + n], start=h == 0, stop=h == H - 1)
                        ins.then_inc(s["k_used"], 1)
                        for g in range(G):
                            for h in range(H):
                                ins = pe.matmul(ps[32 * i:32 * i + 32, 2, CK[0] + g * NSMP:CK[0] + (g + 1) * NSMP],
                                                qz[:, b, g, h, :], qk[:, h, 2 * g + 1, :], start=h == 0, stop=h == H - 1)
                    ins.then_inc(s["s_done"], 1)

                def turn(half, q):
                    n = NQ * half + q
                    if n >= 2:
                        pe.wait_ge(s["tp_read"], n - 1)
                    for j in range(4 * q, min(4 * q + 4, len(PB))):
                        at, w = PB[j]
                        ins = pe.transpose(ps[0:w, 4 + n % 2, (j % 4) * P:(j % 4 + 1) * P], prob[:, at:at + w], ident[:])
                    ins.then_inc(s["tp_done"], 1)

                def values(half):
                    pe.wait_ge(s["tp_read"], NQ * (half + 1))
                    for i in range(BH):
                        for hh in range(2):
                            lot = 2 * (BH * half + i) + hh
                            pe.wait_ge(v_in[lot % 3], 16 * (lot // 3 + 1))
                            for h in range(2 * hh, 2 * hh + 2):
                                rows = slice((i * H + h) * TS, (i * H + h + 1) * TS)
                                for br in range(2):
                                    first, last = ((0, KEYS // P), (KEYS // P, VBLK))[br]
                                    col = (br * H + h) * NSMP + (BH * half + i) * TS
                                    o = ps[:, 6, col:col + TS]
                                    for j in range(first, last):
                                        ins = pe.matmul(o, vc[:, lot % 3, j, (h % 2) * HD:(h % 2 + 1) * HD],
                                                        probT[:, j, rows], start=j == first, stop=br == 1 and j == last - 1)
                                    if br == 0:
                                        for g in range(G):
                                            pe.matmul(o, vnew[:, h, g, :], probT[0:NSMP, VBLK + g, rows], start=False,
                                                      stop=g == G - 1)
                            ins.then_inc(s["v_used"], 1)

                for half in range(2):
                    scores(half)
                    pe.wait_ge(s["p_done"], half + 1)
                    for q in range(NQ):
                        turn(half, q)
                    values(half)

            @block.scalar
            def _(act):
                for half in range(2):
                    act.wait_ge(s["nm_done"], half + 1)
                    act.activation(prob[:, 0:WIN], prob[:, 0:WIN], ACT.Exp, bias=nm[:, 0:1], accum_out=den[:, 0:1])
                    act.activation(prob[:, WIN:WIN + NMEM], ps[:, 3, 0:NMEM], ACT.Exp, bias=nm[:, 1:2],
                                   accum_out=den[:, 1:2]).then_inc(s["exp_done"], 1)
                    for q in range(NQ):
                        n = NQ * half + q
                        blocks = PB[4 * q:4 * q + 4]
                        act.wait_ge(s["tp_done"], n + 1)
                        if q == 0 and half:
                            act.wait_ge(s["v_used"], 2 * BH)
                        groups = [[j for j, (_, w) in enumerate(blocks) if w == width] for width in (P, NSMP)]
                        for js in groups:
                            if js:
                                w = blocks[js[0]][1]
                                ins = act.activation(
                                    probT[0:w, 4 * q + js[0]:4 * q + js[-1] + 1, :],
                                    ps[0:w, 4 + n % 2, js[0] * P:(js[-1] + 1) * P].rearrange("p (j r) -> p j r", r=P), ACT.Copy)
                        ins.then_inc(s["tp_read"], 1)
                act.wait_ge(s["v_used"], 2 * NB)
                act.activation(out[:], ps[:, 6, :], ACT.Copy).then_inc(s["o_read"], 1)

            @block.vector
            def _(dve):
                dve.memset(qz[:], 0.0).then_inc(s["zeroed"], 1)
                dve.wait_ge(s["zeroed"], 1)
                dve.wait_ge(s["const"], 16 * (3 + G))
                for h in range(H):
                    for g in range(G + 1):
                        src = qk[:, h, 2 * g, :] if g < G else qm[:, h, :]
                        ins = dve.tensor_scalar(qz[:, :, g, h, h * TS:(h + 1) * TS], src.rearrange("p (b t) -> p b t", b=NB),
                                                SCALE_A if g < G else 1.0, None, ALU.mult)
                ins.then_inc(s["spread"], 1)
                for half in range(2):
                    dve.wait_ge(s["s_done"], half + 1)
                    dve.wait_ge(s["masked"], 16 * (half + 1))
                    parts = ((0, 0, CK[0], CK[1]), (1, 0, CK[0] + CK[1], CK[2]), (2, 0, 0, CK[0]),
                             (2, CK[0], KEYS, G * NSMP))
                    if half:
                        dve.wait_ge(s["tp_done"], NQ)
                    for i, (bank, c, at, n) in enumerate(parts):
                        ins = dve.tensor_tensor_reduce(prob[:, at:at + n], ps[:, bank, c:c + n], mask[:, at:at + n], 1.0,
                                                       LOWEST, ALU.add, ALU.max, mx[:, i:i + 1])
                    ins.then_inc(s["mx_done"], 1)
                    dve.tensor_reduce(nm[:, 1:2], ps[:, 3, 0:NMEM], AX.X, ALU.max, negate=True)
                    dve.wait_ge(s["mx_done"], half + 1)
                    dve.sem_inc(s["mask_used"], 1)
                    dve.tensor_reduce(nm[:, 0:1], mx[:], AX.X, ALU.max, negate=True).then_inc(s["nm_done"], 1)
                    dve.wait_ge(s["exp_done"], half + 1)
                    dve.reciprocal(rden[:], den[:]).then_inc(s["rden_done"], 1)
                    dve.wait_ge(s["rden_done"], half + 1)
                    dve.tensor_scalar(prob[:, 0:WIN], prob[:, 0:WIN], rden[:, 0:1], None, ALU.mult)
                    dve.tensor_scalar(prob[:, WIN:], prob[:, WIN:], rden[:, 1:2], None, ALU.mult).then_inc(s["p_done"], 1)


def sample_latent(nc, io, spent):
    with ExitStack() as ctx:
        m = Mem(nc, ctx, "sl")
        KK = KR // P
        PAGES = PAST // P
        ident = m.sb("ident", [P, P])
        mask = m.sb("mask", [P, NB // 2, NSMP])
        table = m.sb("table", [1, NB * PAGES], I32)
        wukT = m.sb("wukT", [NOPE, HB, KR])
        wuv = m.sb("wuv", [P, KK, HB * VD])
        qn = m.sb("qn", [NOPE, HB, NSMP])
        qr = m.sb("qr", [RB, NB, HB, TS])
        krn = m.sb("krn", [RB, NSMP])
        cn = m.sb("cn", [NSMP, KR])
        cnT = m.sb("cnT", [P, KK, NSMP])
        ql = m.sb("ql", [P, KK, NB, HB, TS])
        page = m.sb("page", [P, 2, PAGES, 2 * KR])
        kr = m.sb("kr", [RB, 2, PAGES, P])
        prob = m.sb("prob", [P, PAST + NSMP])
        probT = m.sb("probT", [P, PAGES + 1, P])
        ol = m.sb("ol", [P, KK, NB, HB, TS])
        ob = m.sb("ob", [P, HB // 2, NSMP])
        mx, nm, den, dsum, rden = m.sb("mx", [P, 2]), m.sb("nm", [P, 1]), m.sb("den", [P, 2]), m.sb("dsum", [P, 1]), m.sb("rden", [P, 1])
        ps = m.ps("ps", [P, 8, 512])
        s = {n: m.sem(n) for n in ("const", "cn_done", "cn_read", "ql_done", "ql_read", "pg_used", "s_done", "mx_done", "nm_done",
                                   "exp_done", "dsum_done", "rden_done", "p_done", "tp_done", "tp_read",
                                   "ol_read", "ob_done", "ob_read", "stored")}
        pg_in = [m.sem(f"pg_in{i}") for i in range(2)]

        with nc.Block() as block:
            @block.gpsimd
            def _(pool):
                clear_spent(pool, spent)

            @block.sync
            def _(sp):
                sp.dma_start(table[:], io["page_table"]).then_inc(s["const"], 16)
                for dst, src in ((ident, "ident"), (mask, "mask_l"), (wukT, "w_ukT"), (wuv, "w_uv"), (cn, "s_ckv")):
                    sp.dma_start(dst[:], io[src]).then_inc(s["const"], 16)
                sp.dma_start(qn[:], io["qT_scr"].rearrange("h c n -> c h n")[0:NOPE, :, S:N]).then_inc(s["const"], 16)
                for h in range(HB):
                    sp.dma_start(qr[:, :, h, :], io["qT_scr"][h, NOPE:NOPE + RB, S:N].rearrange("c (b t) -> c b t", b=NB))\
                        .then_inc(s["const"], 16)
                sp.dma_start(krn[:], io["krT_scr"][:, S:N]).then_inc(s["const"], 16)
                sp.wait_ge(s["const"], 16 * (8 + HB))
                with sp.Fori(0, NB // 2) as g:
                    for b in range(2):
                        sp.wait_ge(s["pg_used"], 2 * g + b + 1)
                        for j in range(PAGES):
                            at = (2 * g + b) * PAGES + j
                            n = sp.value_load(table[0:1, bass.ds(at, 1)], min_val=0, max_val=io["pool"].shape[0] - 1)
                            sp.dma_start(page[:, b, j, :], io["pool"][n]).then_inc(pg_in[b], 16)
                            sp.dma_start(kr[:, b, j, :], io["pool_kr"][n]).then_inc(pg_in[b], 16)
                sp.wait_ge(s["ob_read"], 1)
                sp.dma_start(io["oT_scr"][1].rearrange("(a p) n -> p a n", p=P)[:, :, S:N], ob[:]).then_inc(s["stored"], 16)
                sp.wait_ge(s["stored"], 16)

            @block.tensor
            def _(pe):
                pe.sem_inc(s["pg_used"], 2)
                pe.wait_ge(s["const"], 16 * (8 + HB))
                for k in range(KK):
                    ins = pe.transpose(ps[:, 2, k * NSMP:(k + 1) * NSMP], cn[:, k * P:(k + 1) * P], ident[0:NSMP, 0:NSMP])
                ins.then_inc(s["cn_done"], 1)
                for k in range(KK):
                    for h in range(HB):
                        ins = pe.matmul(ps[:, k, h * NSMP:(h + 1) * NSMP], wukT[:, h, k * P:(k + 1) * P], qn[:, h, :],
                                        start=True, stop=True)
                ins.then_inc(s["ql_done"], 1)
                pe.wait_ge(s["cn_read"], 1)
                pe.wait_ge(s["ql_read"], 1)
                for g in range(NB // 2):
                    if g:
                        pe.wait_ge(s["exp_done"], g)
                    for b in range(2):
                        rows = slice(64 * b, 64 * b + 64)
                        pe.wait_ge(pg_in[b], 32 * PAGES * (g + 1))
                        for c in range(PAGES // 4):
                            o = ps[rows, c, :]
                            for k in range(KK):
                                pe.matmul(o, ql[:, k, 2 * g + b], page[:, b, 4 * c:4 * c + 4, k * P:(k + 1) * P], start=k == 0, stop=False)
                            pe.matmul(o, qr[:, 2 * g + b], kr[:, b, 4 * c:4 * c + 4, :], start=False, stop=True)
                        for k in range(KK):
                            pe.matmul(ps[rows, 2, 0:NSMP], ql[:, k, 2 * g + b], cnT[:, k, :], start=k == 0, stop=False)
                        ins = pe.matmul(ps[rows, 2, 0:NSMP], qr[:, 2 * g + b], krn[:], start=False, stop=True)
                    ins.then_inc(s["s_done"], 1)
                    pe.wait_ge(s["p_done"], g + 1)
                    if g:
                        pe.wait_ge(s["tp_read"], g)
                    for j in range(PAGES):
                        pe.transpose(ps[:, 3 + j // 4, (j % 4) * P:(j % 4 + 1) * P], prob[:, j * P:(j + 1) * P], ident[:])
                    pe.transpose(ps[0:NSMP, 5, 0:P], prob[:, PAST:], ident[:]).then_inc(s["tp_done"], 1)
                    pe.wait_ge(s["tp_read"], g + 1)
                    for b in range(2):
                        cols = slice(64 * b, 64 * b + 64)
                        for k in range(KK):
                            o = ps[:, 6 + k, (2 * g + b) * 64:(2 * g + b + 1) * 64]
                            for j in range(PAGES):
                                pe.matmul(o, page[:, b, j, KR + k * P:KR + (k + 1) * P], probT[:, j, cols], start=j == 0, stop=False)
                            ins = pe.matmul(o, cn[:, k * P:(k + 1) * P], probT[0:NSMP, PAGES, cols], start=False, stop=True)
                        ins.then_inc(s["pg_used"], 1)
                pe.wait_ge(s["ol_read"], 1)
                for h in range(HB):
                    for k in range(KK):
                        ins = pe.matmul(ps[(h % 2) * VD:(h % 2 + 1) * VD, 3, (h // 2) * NSMP:(h // 2 + 1) * NSMP],
                                        wuv[:, k, h * VD:(h + 1) * VD], ol[:, k, :, h, :], start=k == 0, stop=k == KK - 1)
                ins.then_inc(s["ob_done"], 1)

            @block.scalar
            def _(act):
                act.wait_ge(s["cn_done"], 1)
                act.activation(cnT[:], ps[:, 2, 0:KK * NSMP].rearrange("p (k n) -> p k n", k=KK), ACT.Copy).then_inc(s["cn_read"], 1)
                act.wait_ge(s["ql_done"], 1)
                for k in range(KK):
                    ins = act.activation(ql[:, k].rearrange("p b h t -> p h b t"),
                                         ps[:, k, :].rearrange("p (h b t) -> p h b t", h=HB, b=NB), ACT.Copy)
                ins.then_inc(s["ql_read"], 1)
                for g in range(NB // 2):
                    act.wait_ge(s["nm_done"], g + 1)
                    act.activation(prob[:, PAST:], prob[:, PAST:], ACT.Exp, bias=nm[:], accum_out=den[:, 1:2])
                    act.activation(prob[:, 0:PAST], ps[:, 0:2, :].rearrange("p a n -> p (a n)"), ACT.Exp, bias=nm[:],
                                   accum_out=den[:, 0:1]).then_inc(s["exp_done"], 1)
                    act.wait_ge(s["tp_done"], g + 1)
                    act.activation(probT[:, 0:PAGES, :].rearrange("p j r -> p (j r)"),
                                   ps[:, 3:5, :].rearrange("p a n -> p (a n)"), ACT.Copy)
                    act.activation(probT[0:NSMP, PAGES, :], ps[0:NSMP, 5, 0:P], ACT.Copy).then_inc(s["tp_read"], 1)
                act.wait_ge(s["pg_used"], 2 + NB)
                act.activation(ol[:].rearrange("p k b h t -> p k (b h t)"), ps[:, 6:8, :], ACT.Copy).then_inc(s["ol_read"], 1)
                act.wait_ge(s["ob_done"], 1)
                act.activation(ob[:], ps[:, 3, 0:HB // 2 * NSMP].rearrange("p (a n) -> p a n", n=NSMP), ACT.Copy)\
                    .then_inc(s["ob_read"], 1)

            @block.vector
            def _(dve):
                dve.wait_ge(s["const"], 16 * (8 + HB))
                for g in range(NB // 2):
                    dve.wait_ge(s["s_done"], g + 1)
                    if g:
                        dve.wait_ge(s["tp_done"], g)
                    dve.tensor_tensor_reduce(prob[:, PAST:], ps[:, 2, 0:NSMP], mask[:, g, :], 1.0, LOWEST, ALU.add, ALU.max,
                                             mx[:, 1:2])
                    dve.tensor_reduce(mx[:, 0:1], ps[:, 0:2, :].rearrange("p a n -> p (a n)"), AX.X, ALU.max)\
                        .then_inc(s["mx_done"], 1)
                    dve.wait_ge(s["mx_done"], g + 1)
                    dve.tensor_reduce(nm[:], mx[:], AX.X, ALU.max, negate=True).then_inc(s["nm_done"], 1)
                    dve.wait_ge(s["exp_done"], g + 1)
                    dve.tensor_reduce(dsum[:], den[:], AX.X, ALU.add).then_inc(s["dsum_done"], 1)
                    dve.wait_ge(s["dsum_done"], g + 1)
                    dve.reciprocal(rden[:], dsum[:]).then_inc(s["rden_done"], 1)
                    dve.wait_ge(s["rden_done"], g + 1)
                    dve.tensor_scalar(prob[:], prob[:], rden[:], None, ALU.mult).then_inc(s["p_done"], 1)


def branch_outputs(nc, io):
    with ExitStack() as ctx:
        m = Mem(nc, ctx, "br")
        K = 512 // P
        ring = WeightRing(m, io["w_o"], K * 2 * P, 4)
        o = m.sb("o", [P, 2, K, N])
        o_hi, o_lo = m.sb("o_hi", [P, K, N], F32R), m.sb("o_lo", [P, K, N], F32R)
        st = m.sb("st", [P, 2, N])
        ps = m.ps("ps", [P, 8, 512])
        s = {n: m.sem(n) for n in ("hi_done", "lo_done", "b_done", "b_read")}
        o_in = [m.sem(f"o_in{i}") for i in range(2)]
        stored = [m.sem(f"stored{i}") for i in range(2)]
        ITS = [(br, c) for br in range(3) for c in range(KD)]

        with nc.Block() as block:
            @block.sync
            def _(sp):
                for br in range(2):
                    sp.dma_start(o[:, br], io["oT_scr"][br].rearrange("(k p) n -> p k n", p=P)).then_inc(o_in[br], 16)
                for br in range(3):
                    for j in range(4):
                        ring.load(sp, 0, 4 * br + j)
                    if br == 0:
                        sp.wait_ge(s["lo_done"], 1)
                        sp.dma_start(o[:, 0], io["oT_scr"][2].rearrange("(k p) n -> p k n", p=P)).then_inc(o_in[0], 16)

            @block.tensor
            def _(pe):
                for i, (br, c) in enumerate(ITS):
                    j = 4 * br + c // 2
                    if c == 0:
                        pe.wait_ge(s["lo_done"], br + 1)
                    if c % 2 == 0:
                        ring.wait(pe, 0, j)
                    if i >= 2:
                        pe.wait_ge(s["b_read"], i - 1)
                    for q, (at, n) in enumerate(COL):
                        for k in range(K):
                            w = slice((2 * k + c % 2) * P, (2 * k + c % 2 + 1) * P)
                            ins = mm3(pe, ps[:, 3 * (i % 2) + q, 0:n], ring.hi[:, j % ring.R, w], ring.lo[:, j % ring.R, w],
                                      o_hi[:, k, at:at + n], o_lo[:, k, at:at + n], k == 0, k == K - 1)
                    ins.then_inc(s["b_done"], 1)

            @block.scalar
            def _(act):
                for br in range(3):
                    if br == 0:
                        for j in range(4):
                            ring.round_hi(act, 0, j, True)
                    act.wait_ge(o_in[br % 2], 16 * (br // 2 + 1))
                    if br:
                        act.wait_ge(s["b_done"], KD * br)
                    act.activation(o_hi[:], o[:, br % 2], ACT.Copy).then_inc(s["hi_done"], 1)
                    for c in range(KD):
                        i = KD * br + c
                        act.wait_ge(s["b_done"], i + 1)
                        if i >= 2:
                            act.wait_ge(stored[i % 2], 16 * (i // 2))
                        for q, (at, n) in enumerate(COL):
                            ins = act.activation(st[:, i % 2, at:at + n], ps[:, 3 * (i % 2) + q, 0:n], ACT.Copy)
                        ins.then_inc(s["b_read"], 1)
                        if c % 2 and br < 2:
                            ring.round_hi(act, 0, 4 * br + 4 + c // 2, True)
                        act.wait_ge(s["b_read"], i + 1)
                        act.dma_start(io["bT_scr"][br, c * P:(c + 1) * P, :], st[:, i % 2, :]).then_inc(stored[i % 2], 16)
                for i in range(2):
                    act.wait_ge(stored[i], 16 * (len(ITS) // 2))

            @block.vector
            def _(dve):
                dve.sem_inc(ring.ready, ring.RAW)
                for br in range(3):
                    if br == 0:
                        for j in range(4):
                            ring.rest_lo(dve, 0, j)
                    dve.wait_ge(s["hi_done"], br + 1)
                    dve.tensor_tensor(o_lo[:], o[:, br % 2], o_hi[:].bitcast(F32), ALU.subtract).then_inc(s["lo_done"], 1)
                    if br < 2:
                        for j in range(4):
                            ring.rest_lo(dve, 0, 4 * br + 4 + j)


def merge(nc, io, hT_hi, hT_lo, mT_hi, mT_lo):
    with ExitStack() as ctx:
        m = Mem(nc, ctx, "mrg")
        ring = WeightRing(m, io["w_gate"], KD * P, 3)
        b_ = m.sb("b", [P, 3, N])
        sig = m.sb("sig", [P, 2, N])
        acc = m.sb("acc", [P, 2, N])
        ps = m.ps("ps", [P, 8, 512])
        s = {n: m.sem(n) for n in ("g_done", "sig_done", "prod_done", "sum_done", "hi_done", "lo_done")}
        b_in = [m.sem(f"b_in{i}") for i in range(3)]
        ITS = [(c, br) for c in range(KD) for br in range(3)]

        with nc.Block() as block:
            @block.sync
            def _(sp):
                for i, (c, br) in enumerate(ITS):
                    ring.load(sp, 0, i)
                    if i >= 3:
                        sp.wait_ge(s["sum_done"], i - 2)
                    sp.dma_start(b_[:, i % 3, :], io["bT_scr"][br, c * P:(c + 1) * P, :]).then_inc(b_in[i % 3], 16)

            @block.tensor
            def _(pe):
                for i, (c, br) in enumerate(ITS):
                    ring.wait(pe, 0, i)
                    if i >= 2:
                        pe.wait_ge(s["sig_done"], i - 1)
                    for q, (at, n) in enumerate(COL):
                        for k in range(KD):
                            w = slice(k * P, (k + 1) * P)
                            ins = mm3(pe, ps[:, 3 * (i % 2) + q, 0:n], ring.hi[:, i % ring.R, w], ring.lo[:, i % ring.R, w],
                                      hT_hi[:, k, at:at + n], hT_lo[:, k, at:at + n], k == 0, k == KD - 1)
                    ins.then_inc(s["g_done"], 1)

            @block.scalar
            def _(act):
                for j in range(3):
                    ring.round_hi(act, 0, j, True)
                for i, (c, br) in enumerate(ITS):
                    act.wait_ge(s["g_done"], i + 1)
                    if i >= 2:
                        act.wait_ge(s["sum_done"], i - 1)
                    for q, (at, n) in enumerate(COL):
                        ins = act.activation(sig[:, i % 2, at:at + n], ps[:, 3 * (i % 2) + q, 0:n], ACT.Sigmoid)
                    ins.then_inc(s["sig_done"], 1)
                    if i + 3 < len(ITS):
                        ring.round_hi(act, 0, i + 3, True)
                    if br == 2:
                        act.wait_ge(s["sum_done"], 3 * c + 3)
                        act.activation(mT_hi[:, c, :], acc[:, c % 2, :], ACT.Copy).then_inc(s["hi_done"], 1)

            @block.vector
            def _(dve):
                dve.sem_inc(ring.ready, ring.RAW)
                for j in range(3):
                    ring.rest_lo(dve, 0, j)

                def rest(c):
                    dve.wait_ge(s["hi_done"], c + 1)
                    dve.tensor_tensor(mT_lo[:, c, :], acc[:, c % 2, :], mT_hi[:, c, :].bitcast(F32), ALU.subtract)\
                        .then_inc(s["lo_done"], 1)

                for i, (c, br) in enumerate(ITS):
                    dve.wait_ge(s["sig_done"], i + 1)
                    dve.wait_ge(b_in[i % 3], 16 * (i // 3 + 1))
                    if br == 0:
                        dve.tensor_tensor(acc[:, c % 2, :], sig[:, i % 2, :], b_[:, i % 3, :], ALU.mult).then_inc(s["sum_done"], 1)
                        if c:
                            rest(c - 1)
                    else:
                        dve.tensor_tensor(sig[:, i % 2, :], sig[:, i % 2, :], b_[:, i % 3, :], ALU.mult).then_inc(s["prod_done"], 1)
                        dve.wait_ge(s["prod_done"], 2 * c + br)
                        dve.wait_ge(s["sum_done"], i)
                        dve.tensor_tensor(acc[:, c % 2, :], acc[:, c % 2, :], sig[:, i % 2, :], ALU.add).then_inc(s["sum_done"], 1)
                    if i + 3 < len(ITS):
                        ring.rest_lo(dve, 0, i + 3)
                rest(KD - 1)


def output_projection(nc, io, mT_hi, mT_lo):
    with ExitStack() as ctx:
        m = Mem(nc, ctx, "out")
        CH, XS = 8, 2
        raw = m.sb("raw", [P, 3, D])
        w_hi, w_lo = m.sb("w_hi", [P, KD, D], F32R), m.sb("w_lo", [P, KD, D], F32R)
        gain = m.sb("gain", [P, D])
        x = m.sb("x", [P, XS, D])
        sq = m.sb("sq", [P, 512])
        y = m.sb("y", [P, 2, D])
        ss = m.sb("ss", [P, TILES, 2])
        mean, rstd, half = m.sb("mean", [P, TILES]), m.sb("rstd", [P, TILES]), m.sb("half", [P, 1])
        ps = m.ps("ps", [P, 8, 512])
        s = {n: m.sem(n) for n in ("const", "rounded", "ready", "y_done", "sq_done", "half_set", "sum_done", "mean_done",
                                   "rstd_done", "scaled", "added")}
        landed = [m.sem(f"landed{i}") for i in range(3)]
        x_in = [m.sem(f"x_in{i}") for i in range(XS)]
        stored = [m.sem(f"stored{i}") for i in range(2)]

        with nc.Block() as block:
            @block.sync
            def _(sp):
                sp.dma_start(gain[:], io["gain_post"][0]).then_inc(s["const"], 16)
                for k in range(KD):
                    if k >= 3:
                        sp.wait_ge(s["ready"], k - 2)
                    sp.dma_start(raw[:, k % 3, :], io["w_out"][k * P:(k + 1) * P, :]).then_inc(landed[k % 3], 16)
                for t in range(TILES):
                    r = rows_of(t)
                    if t >= XS:
                        sp.wait_ge(s["added"], t - XS + 1)
                    src = io["xp"][t * P:(t + 1) * P, :] if t < PT_TILES else io["xs"]
                    sp.dma_start(x[0:r, t % XS, :], src).then_inc(x_in[t % XS], 16)

            @block.tensor
            def _(pe):
                for t in range(TILES):
                    r = rows_of(t)
                    if t >= 4:
                        pe.wait_ge(s["scaled"], t - 3)
                    for k in range(KD):
                        if t == 0:
                            pe.wait_ge(s["ready"], k + 1)
                        x_ = slice(t * P, t * P + r)
                        for w, v in ((w_hi, mT_hi), (w_lo, mT_hi), (w_hi, mT_lo)):
                            for c in range(2):
                                ins = pe.matmul(ps[0:r, 2 * (t % 4) + c, :], v[:, k, x_], w[:, k, c * 512:(c + 1) * 512],
                                                start=k == 0 and w is w_hi and v is mT_hi, stop=k == KD - 1 and v is mT_lo)
                    ins.then_inc(s["y_done"], 1)

            @block.scalar
            def _(act):
                for k in range(KD):
                    act.wait_ge(landed[k % 3], 16 * (k // 3 + 1))
                    act.activation(w_hi[:, k, :], raw[:, k % 3, :], ACT.Copy).then_inc(s["rounded"], 1)

                def store(t):
                    r = rows_of(t)
                    act.wait_ge(s["added"], t + 1)
                    act.dma_start(io["x1_scr"][t * P:t * P + r, :], y[0:r, t % 2, :]).then_inc(stored[t % 2], 16)

                for t in range(TILES):
                    r = rows_of(t)
                    act.wait_ge(s["y_done"], t + 1)
                    for c in range(2):
                        if 2 * t + c:
                            act.wait_ge(s["sq_done"], 2 * t + c)
                        act.activation(sq[0:r, :], ps[0:r, 2 * (t % 4) + c, :], ACT.Square,
                                       accum_out=ss[0:r, t, c:c + 1]).then_inc(s["sq_done"], 1)
                    if t:
                        store(t - 1)
                store(TILES - 1)
                act.wait_ge(stored[0], 16 * (TILES // 2 + 1))
                act.wait_ge(stored[1], 16 * (TILES // 2))

            @block.gpsimd
            def _(pool):
                pool.memset(half[:], -0.5).then_inc(s["half_set"], 1)
                pool.wait_ge(s["half_set"], 1)
                for t in range(TILES):
                    r = rows_of(t)
                    pool.wait_ge(s["sq_done"], 2 * t + 2)
                    pool.tensor_tensor(mean[0:r, t:t + 1], ss[0:r, t, 0:1], ss[0:r, t, 1:2], ALU.add).then_inc(s["sum_done"], 1)
                    pool.wait_ge(s["sum_done"], t + 1)
                    pool.tensor_scalar(mean[0:r, t:t + 1], mean[0:r, t:t + 1], 1.0 / D, EPS, ALU.mult,
                                       ALU.add).then_inc(s["mean_done"], 1)
                    pool.wait_ge(s["mean_done"], t + 1)
                    pool.tensor_tensor(rstd[0:r, t:t + 1], mean[0:r, t:t + 1], half[0:r, :], ALU.pow)\
                        .then_inc(s["rstd_done"], 1)

            @block.vector
            def _(dve):
                for k in range(KD):
                    dve.wait_ge(s["rounded"], k + 1)
                    dve.tensor_tensor(w_lo[:, k, :], raw[:, k % 3, :], w_hi[:, k, :].bitcast(F32), ALU.subtract)\
                        .then_inc(s["ready"], 1)
                dve.wait_ge(s["const"], 16)
                for t in range(TILES):
                    r = rows_of(t)
                    dve.wait_ge(s["rstd_done"], t + 1)
                    if t >= 2:
                        dve.wait_ge(stored[t % 2], 16 * (t // 2))
                    dve.scalar_tensor_tensor(y[0:r, t % 2, :], ps[0:r, 2 * (t % 4):2 * (t % 4) + 2, :].rearrange("p a n -> p (a n)"),
                                             rstd[0:r, t:t + 1], gain[0:r, :], ALU.mult, ALU.mult).then_inc(s["scaled"], 1)
                    dve.wait_ge(s["scaled"], t + 1)
                    dve.wait_ge(x_in[t % XS], 16 * (t // XS + 1))
                    dve.tensor_tensor(y[0:r, t % 2, :], y[0:r, t % 2, :], x[0:r, t % XS, :], ALU.add).then_inc(s["added"], 1)


CONV = 3
CHUNKS = 2 * DFF // P
PAIRS = CHUNKS // 2
BODIES = PAIRS // 2
UW = CONV - 1 + S + NB * (TS + CONV - 1)
CW = UW - (CONV - 1)
SAMP = S + CONV - 1


def ffn(nc, io, hT_hi, hT_lo, acc):
    with ExitStack() as ctx:
        m = Mem(nc, ctx, "ffn")
        ring = WeightRing(m, io["w_ffn"], D, 4)
        ring.turns = lambda base: base // ring.RAW
        ring.RAW = RAW = 2
        prev = m.sb("prev", [P, CHUNKS, NB, CONV - 1])
        coef = m.sb("coef", [P, CHUNKS, CONV + 1])
        last = m.sb("last", [P, CHUNKS, 1 + NB, CONV - 1])
        u = m.sb("u", [P, 2, UW])
        c = m.sb("c", [P, 2, CW])
        prod = m.sb("prod", [P, N])
        a_hi, a_lo = m.sb("a_hi", [P, 2, N], F32R), m.sb("a_lo", [P, 2, N], F32R)
        ps = m.ps("ps", [P, 8, 512])
        s = {n: m.sem(n) for n in ("const", "u_set", "acc_set", "up_done", "up_read", "c0_done", "c1_done", "c_done", "kept", "gelu_done",
                                   "prod_done", "hi_done", "lo_done", "dn_done", "dn_read", "stored")}
        DN = 2 * TILES

        with nc.Block() as block:
            @block.sync
            def _(sp):
                for dst, src in ((prev, "conv_prev"), (coef, "conv_coef")):
                    sp.dma_start(dst[:], io[src]).then_inc(s["const"], 16)
                with sp.Fori(0, FFN_CHUNKS // 4) as g:
                    for j in range(4):
                        ring.load(sp, 4 * g, j)
                sp.wait_ge(s["kept"], CHUNKS + 2)
                sp.dma_start(io["conv_last"], last[:]).then_inc(s["stored"], 16)
                sp.wait_ge(s["stored"], 16)

            @block.tensor
            def _(pe):
                def up(i, base, j, n):
                    ring.wait(pe, base, j)
                    pe.wait_ge(s["up_read"], 4 * i + n + 1)
                    sl = j % ring.R
                    for q, (at, w) in enumerate(COL):
                        for k in range(KD):
                            ins = mm3(pe, ps[:, 3 * (n % 2) + q, 0:w], ring.hi[:, sl, k * P:(k + 1) * P],
                                      ring.lo[:, sl, k * P:(k + 1) * P], hT_hi[:, k, at:at + w], hT_lo[:, k, at:at + w],
                                      k == 0, k == KD - 1)
                    ins.then_inc(s["up_done"], 1)

                def down(i, base, j):
                    ring.wait(pe, base, j + 1)
                    pe.wait_ge(s["lo_done"], 2 * i + 2)
                    for t in range(TILES):
                        for half in range(2):
                            pe.wait_ge(s["dn_read"], DN * i + 2 * t + half + 1)
                            o = ps[0:rows_of(t), 6 + half, :]
                            for f in range(2):
                                a = [x[:, f, t * P:t * P + rows_of(t)] for x in (a_hi, a_lo)]
                                w = [x[:, (j + f) % ring.R, half * 512:(half + 1) * 512] for x in (ring.hi, ring.lo)]
                                pe.matmul(o, a[0], w[0], start=f == 0, stop=False)
                                pe.matmul(o, a[0], w[1], start=False, stop=False)
                                ins = pe.matmul(o, a[1], w[0], start=False, stop=f == 1)
                            ins.then_inc(s["dn_done"], 1)

                def body(i, base, j):
                    up(i, base, j, 0)
                    up(i, base, j + 1, 1)
                    down(i - 1, base, j + 2)
                    up(i, base, j + 4, 2)
                    up(i, base, j + 5, 3)

                for n in range(4):
                    up(0, 0, n, n)
                with pe.Fori(0, (BODIES - 1) // 2) as g:
                    body(2 * g + 1, 4 + 12 * g, 0)
                    body(2 * g + 2, 4 + 12 * g, 6)
                down(BODIES - 1, 4 + 6 * (BODIES - 1), 0)

            @block.scalar
            def _(act):
                act.sem_inc(s["up_read"], 2)

                def round_hi(base, j):
                    act.wait_ge(ring.landed[j % RAW], 16 * ring.turn(base, j) + 16)
                    act.activation(ring.hi[:, j % ring.R, :], ring.raw[:, j % RAW, :], ACT.Copy).then_inc(ring.rounded, 1)

                def copy_u(i, f, n):
                    b, chunk = n % 2, f + (n % 2) * PAIRS
                    act.wait_ge(s["c_done"], 4 * i + n + 1)
                    act.wait_ge(s["kept"], 4 * i + n + 1)
                    samp = u[:, b, S + CONV - 1:].rearrange("p (b t) -> p b t", b=NB)
                    act.activation(samp[:, :, 0:CONV - 1], prev[:, bass.ds(chunk, 1)].rearrange("p a b t -> p (a b) t"), ACT.Copy)
                    act.wait_ge(s["up_done"], 4 * i + n + 1)
                    bank = 3 * b
                    act.activation(u[:, b, CONV - 1:CONV - 1 + 768].rearrange("p (a n) -> p a n", a=2), ps[:, bank:bank + 2, 0:384],
                                   ACT.Copy)
                    act.activation(u[:, b, CONV - 1 + 768:CONV - 1 + S], ps[:, bank + 2, 0:256], ACT.Copy)
                    act.activation(samp[:, :, CONV - 1:], ps[:, bank + 2, 256:320].rearrange("p (b t) -> p b t", b=NB), ACT.Copy)\
                        .then_inc(s["up_read"], 1)
                    act.wait_ge(s["up_read"], 4 * i + n + 3)
                    act.wait_ge(s["prod_done"], 2 * i + n // 2 + 1)
                    act.activation(c[:, b, :], u[:, b, CONV - 1:], ACT.Identity, bias=coef[:, bass.ds(chunk, 1), CONV],
                                   scale=coef[:, bass.ds(chunk, 1), CONV - 1]).then_inc(s["c0_done"], 1)

                def gelu(i, n):
                    act.wait_ge(s["c_done"], 4 * i + n + 2)
                    act.activation(c[:, 0, :], c[:, 0, :], ACT.Gelu_apprx_tanh).then_inc(s["gelu_done"], 1)

                def split(i, n):
                    f = n // 2
                    act.wait_ge(s["prod_done"], 2 * i + f + 2)
                    act.activation(a_hi[:, f, :], prod[:], ACT.Copy).then_inc(s["hi_done"], 1)

                def body(i, base, j, first=False):
                    copy_u(i, 2 * i, 0)
                    round_hi(base, j + 4)
                    gelu(i, 1)
                    copy_u(i, 2 * i, 1)
                    round_hi(base, j + 5)
                    if not first:
                        act.wait_ge(s["dn_done"], DN * i)
                        round_hi(base, j + 6)
                        round_hi(base, j + 7)
                    split(i, 1)
                    copy_u(i, 2 * i + 1, 2)
                    round_hi(base, j + (6 if first else 8))
                    gelu(i, 3)
                    copy_u(i, 2 * i + 1, 3)
                    round_hi(base, j + (7 if first else 9))
                    split(i, 3)

                act.wait_ge(s["const"], 32)
                act.wait_ge(s["u_set"], 1)
                for j in range(4):
                    round_hi(0, j)
                body(0, 0, 0, True)
                with act.Fori(0, (BODIES - 1) // 2) as g:
                    body(2 * g + 1, 4 + 12 * g, 0)
                    body(2 * g + 2, 4 + 12 * g, 6)

            @block.gpsimd
            def _(pool):
                pool.memset(u[:, :, 0:CONV - 1], 0.0).then_inc(s["u_set"], 1)
                pool.sem_inc(s["kept"], 2)

                def keep(i, f, n):
                    b, chunk = n % 2, f + (n % 2) * PAIRS
                    pool.wait_ge(s["up_read"], 4 * i + n + 3)
                    pool.tensor_copy(last[:, bass.ds(chunk, 1), 0, :], u[:, b, S:S + CONV - 1].rearrange("p (a n) -> p a n", a=1))
                    pool.tensor_copy(last[:, bass.ds(chunk, 1), 1:].rearrange("p a b t -> p (a b) t"),
                                     u[:, b, SAMP:].rearrange("p (b t) -> p b t", b=NB)[:, :, TS:]).then_inc(s["kept"], 1)

                with pool.Fori(0, BODIES) as i:
                    for n in range(4):
                        keep(i, 2 * i + n // 2, n)

            @block.vector
            def _(dve):
                dve.sem_inc(ring.ready, RAW)
                dve.sem_inc(s["c_done"], 2)
                dve.sem_inc(s["prod_done"], 1)
                dve.sem_inc(s["dn_read"], 2)

                def conv(i, f, n):
                    b, chunk = n % 2, f + (n % 2) * PAIRS
                    dve.wait_ge(s["c0_done"], 4 * i + n + 1)
                    dve.scalar_tensor_tensor(c[:, b, :], u[:, b, 1:CW + 1], coef[:, bass.ds(chunk, 1), 1], c[:, b, :], ALU.mult,
                                             ALU.add).then_inc(s["c1_done"], 1)
                    dve.wait_ge(s["c1_done"], 4 * i + n + 1)
                    dve.scalar_tensor_tensor(c[:, b, :], u[:, b, 0:CW], coef[:, bass.ds(chunk, 1), 0], c[:, b, :], ALU.mult,
                                             ALU.add).then_inc(s["c_done"], 1)

                def multiply(i, n):
                    dve.wait_ge(s["c_done"], 4 * i + n + 3)
                    dve.wait_ge(s["gelu_done"], 2 * i + n // 2 + 1)
                    dve.tensor_tensor(prod[:, 0:S], c[:, 0, 0:S], c[:, 1, 0:S], ALU.mult)
                    samp = lambda x: x[:, S:].rearrange("p (b t) -> p b t", b=NB)[:, :, CONV - 1:]
                    dve.tensor_tensor(prod[:, S:].rearrange("p (b t) -> p b t", b=NB), samp(c[:, 0]), samp(c[:, 1]), ALU.mult)\
                        .then_inc(s["prod_done"], 1)

                def rest(i, n):
                    f = n // 2
                    dve.wait_ge(s["hi_done"], 2 * i + f + 1)
                    dve.tensor_tensor(a_lo[:, f, :], prod[:], a_hi[:, f, :].bitcast(F32), ALU.subtract)\
                        .then_inc(s["lo_done"], 1)

                def add(i, t, half, first=False):
                    r = rows_of(t)
                    dve.wait_ge(s["dn_done"], DN * i + 2 * t + half + 1)
                    o, a = ps[0:r, 6 + half, :], acc[0:r, t, half * 512:(half + 1) * 512]
                    dve.tensor_tensor(a, o, a, ALU.add).then_inc(s["dn_read"], 1)

                def body(i, base, j, first=False):
                    conv(i, 2 * i, 0)
                    ring.rest_lo(dve, base, j + 4)
                    if not first:
                        for t in range(TILES):
                            for half in range(2):
                                add(i - 1, t, half)
                            if t == 4:
                                ring.rest_lo(dve, base, j + 5)
                    else:
                        ring.rest_lo(dve, base, j + 5)
                    conv(i, 2 * i, 1)
                    multiply(i, 1)
                    if not first:
                        ring.rest_lo(dve, base, j + 6)
                        ring.rest_lo(dve, base, j + 7)
                    rest(i, 1)
                    conv(i, 2 * i + 1, 2)
                    ring.rest_lo(dve, base, j + (6 if first else 8))
                    conv(i, 2 * i + 1, 3)
                    multiply(i, 3)
                    ring.rest_lo(dve, base, j + (7 if first else 9))
                    rest(i, 3)

                dve.memset(acc[:], 0.0).then_inc(s["acc_set"], 1)
                dve.wait_ge(s["acc_set"], 1)
                for j in range(4):
                    ring.rest_lo(dve, 0, j)
                body(0, 0, 0, True)
                with dve.Fori(0, (BODIES - 1) // 2) as g:
                    body(2 * g + 1, 4 + 12 * g, 0)
                    body(2 * g + 2, 4 + 12 * g, 6)
                for t in range(TILES):
                    for half in range(2):
                        add(BODIES - 1, t, half)


FFN_CHUNKS = 4 + 6 * (BODIES - 1) + 2 + 2


def finish(nc, io, acc):
    with ExitStack() as ctx:
        m = Mem(nc, ctx, "fin")
        gain = m.sb("gain", [P, D])
        x = m.sb("x", [P, TILES, D])
        sq = m.sb("sq", [P, D])
        y = m.sb("y", [P, TILES, D])
        ss, mean, rstd = (m.sb(n, [P, TILES]) for n in ("ss", "mean", "rstd"))
        half = m.sb("half", [P, 1])
        s = {n: m.sem(n) for n in ("const", "sq_done", "half_set", "mean_done", "rstd_done", "scaled", "added", "stored")}
        x_in = [m.sem(f"x_in{i}") for i in range(TILES)]

        with nc.Block() as block:
            @block.sync
            def _(sp):
                sp.dma_start(gain[:], io["gain_post"][1]).then_inc(s["const"], 16)
                for t in range(TILES):
                    r = rows_of(t)
                    sp.dma_start(x[0:r, t, :], io["x1_scr"][t * P:t * P + r, :]).then_inc(x_in[t], 16)
                for t in range(TILES):
                    r = rows_of(t)
                    sp.wait_ge(s["added"], t + 1)
                    sp.dma_start(io["y_p"][t * P:(t + 1) * P, :] if t < PT_TILES else io["y_s"], y[0:r, t, :])\
                        .then_inc(s["stored"], 16)
                sp.wait_ge(s["stored"], 16 * TILES)

            @block.scalar
            def _(act):
                for t in range(TILES):
                    r = rows_of(t)
                    if t:
                        act.wait_ge(s["sq_done"], t)
                    act.activation(sq[0:r, :], acc[0:r, t, :], ACT.Square, accum_out=ss[0:r, t:t + 1]).then_inc(s["sq_done"], 1)

            @block.gpsimd
            def _(pool):
                pool.memset(half[:], -0.5).then_inc(s["half_set"], 1)
                pool.wait_ge(s["half_set"], 1)
                for t in range(TILES):
                    r = rows_of(t)
                    pool.wait_ge(s["sq_done"], t + 1)
                    pool.tensor_scalar(mean[0:r, t:t + 1], ss[0:r, t:t + 1], 1.0 / D, EPS, ALU.mult,
                                       ALU.add).then_inc(s["mean_done"], 1)
                    pool.wait_ge(s["mean_done"], t + 1)
                    pool.tensor_tensor(rstd[0:r, t:t + 1], mean[0:r, t:t + 1], half[0:r, :], ALU.pow)\
                        .then_inc(s["rstd_done"], 1)

            @block.vector
            def _(dve):
                dve.wait_ge(s["const"], 16)

                def scale(t):
                    r = rows_of(t)
                    dve.wait_ge(s["rstd_done"], t + 1)
                    dve.scalar_tensor_tensor(y[0:r, t, :], acc[0:r, t, :], rstd[0:r, t:t + 1], gain[0:r, :], ALU.mult,
                                             ALU.mult).then_inc(s["scaled"], 1)

                scale(0)
                for t in range(TILES):
                    r = rows_of(t)
                    if t + 1 < TILES:
                        scale(t + 1)
                    dve.wait_ge(s["scaled"], t + 1)
                    dve.wait_ge(x_in[t], 16)
                    dve.tensor_tensor(y[0:r, t, :], y[0:r, t, :], x[0:r, t, :], ALU.add).then_inc(s["added"], 1)


def build(nc, io):
    top = 229344
    Mem.spent.clear()
    pair = 4 * KD * N
    with ExitStack() as ctx:
        m = Mem(nc, ctx, "h")
        hT_hi = m.sb("hT_hi", [P, KD, N], F32R)
        hT_lo = m.sb("hT_lo", [P, KD, N], F32R)
        with ExitStack() as early:
            e = Mem(nc, early, "mem")
            mT_hi = e.sb("mT_hi", [P, KD, NMEM], F32R)
            mT_lo = e.sb("mT_lo", [P, KD, NMEM], F32R)
            items = [(io["xp"][t * P:(t + 1) * P, :], P, 0, hT_hi, hT_lo, t * P) for t in range(PT_TILES)]
            items += [(io["xs"], NSMP, 0, hT_hi, hT_lo, S)]
            items += [(io["mem"][t * P:(t + 1) * P, :], P, 1, mT_hi, mT_lo, t * P) for t in range(NMEM // P)]
            normalise(nc, io, "nrm", items)
            memory_attention(nc, io, hT_hi, hT_lo, mT_hi, mT_lo)
        window_attention(nc, io, hT_hi, hT_lo)
        latent_projections(nc, io, hT_hi, hT_lo)
        latent_attention(nc, io)
        over = list(Mem.spent)
        sample_attention(nc, io)
        sample_latent(nc, io, over)
        branch_outputs(nc, io)
        mix_hi = nc.alloc_sbuf_tensor_at("mix_hi", [P, KD, N], F32R, offset=top - 2 * pair)
        mix_lo = nc.alloc_sbuf_tensor_at("mix_lo", [P, KD, N], F32R, offset=top - pair)
        merge(nc, io, hT_hi, hT_lo, mix_hi, mix_lo)
    output_projection(nc, io, mix_hi, mix_lo)
    with ExitStack() as ctx:
        m = Mem(nc, ctx, "x")
        acc = m.sb("acc", [P, TILES, D])
        with ExitStack() as late:
            e = Mem(nc, late, "x2")
            xT_hi = e.sb("xT_hi", [P, KD, N], F32R)
            xT_lo = e.sb("xT_lo", [P, KD, N], F32R)
            normalise(nc, io, "nrm2", [(io["x1_scr"][t * P:t * P + rows_of(t), :], rows_of(t), 2, xT_hi, xT_lo, t * P)
                                       for t in range(TILES)])
            ffn(nc, io, xT_hi, xT_lo, acc)
        finish(nc, io, acc)


def rotary(dim, pos):
    inv = np.float32(10000.0) ** (-np.arange(dim // 2, dtype=np.float32) * np.float32(2.0 / dim))
    ang = pos.astype(np.float32)[:, None] * inv[None, :].astype(np.float32)
    return np.cos(ang).astype(np.float32), np.sin(ang).astype(np.float32)


def tiled(a, pad):
    a = np.concatenate([a, np.zeros((TILES * P - N,) + a.shape[1:], a.dtype)])
    return np.ascontiguousarray(np.moveaxis(a.reshape((TILES, P) + a.shape[1:]), 0, 1))


def constants():
    pos = np.concatenate([np.arange(S), np.tile(PAST + np.arange(TS), NB)])
    ca, sa = rotary(HD, pos)
    cb, sb = rotary(RB, pos)
    out = {"ident": np.eye(P, dtype=np.float32),
           "cos_a": tiled(ca, 0), "sin_a": tiled(np.stack([-sa, sa], 1), 0),
           "cos_b": tiled(cb, 0), "sin_b": tiled(np.stack([-sb, sb], 1), 0)}
    q = np.arange(P)[:, None]
    blocks = []
    for (win, dil), reach in zip(GROUPS, MASK_BACK):
        for back in range(reach, -1, -1):
            dist = q - np.arange(P)[None, :] + back * P
            blocks.append(np.where((dist >= 0) & (dist <= win) & (dist % dil == 0), 0.0, -1e30))
    out["mask_p"] = np.concatenate(blocks, 1).astype(np.float32)
    causal = np.where(q >= np.arange(P)[None, :], 0.0, -1e30)
    out["mask_c"] = np.concatenate([np.zeros((P, S - P)), causal], 1).astype(np.float32)
    t = np.tile(np.arange(TS), 4 * H)[:, None]
    p = [np.arange(CK[0])[None, :], np.arange(CK[1])[None, :]]
    old = [p[0] >= t, (p[1] >= t) & ((CK[1] + t - p[1]) % GROUPS[1][1] == 0),
           (np.arange(CK[2]) // (PAST // GROUPS[2][1]))[None, :] == t]
    smp = np.repeat(np.arange(4), H * TS)[:, None]
    b, u = np.repeat(np.arange(NB), TS)[None, :], np.tile(np.arange(TS), NB)[None, :]
    halves = []
    for half in range(2):
        new = [(b == 4 * half + smp) & (u <= t) & ((t - u) % dil == 0) for _, dil in GROUPS]
        halves.append(np.concatenate([np.where(v, 0.0, -1e30) for v in old + new], 1))
    out["mask_s"] = np.stack(halves).astype(np.float32)
    t, smp = np.tile(np.arange(TS), 2 * HB)[:, None, None], np.repeat(np.arange(2), HB * TS)[:, None, None]
    two = np.arange(NB // 2)[None, :, None]
    out["mask_l"] = np.where((b[None] == 2 * two + smp) & (u[None] <= t), 0.0, -1e30).astype(np.float32)
    return out


def padded(a, width):
    return np.concatenate([a, np.zeros(a.shape[:-1] + (width - a.shape[-1],), a.dtype)], -1)


def slabs(w, n):
    k, c = w.shape
    return w.reshape(k // P // n, n, P, c).transpose(0, 2, 1, 3).reshape(-1, P, n * c)


OFF_Q = G * 3 * H * HD


def kernel(**inputs):
    import concourse.bacc as bacc
    from concourse.bass_utils import run_bass_kernel_spmd as run

    x = {k: np.asarray(v) for k, v in inputs.items()}
    w_in = x["w_in"][0]
    feed = constants()
    feed["xp"] = x["x_prompt"][0]
    feed["xs"] = x["x_sample"].reshape(NSMP, D)
    feed["mem"] = x["mem_prompt"][0]
    gain = lambda w: np.asarray(w)[0].reshape(-1, P).T
    feed["gains_pre"] = np.stack([gain(x["norm_attn_pre"]), gain(x["norm_mem"]), gain(x["norm_ffn_pre"])], 1)
    feed["gain_post"] = np.stack([np.tile(x["norm_attn_post"][0], (P, 1)), np.tile(x["norm_ffn_post"][0], (P, 1))])
    swa = w_in[:, :OFF_Q].reshape(D, G, 3, H, HD).transpose(3, 1, 0, 2, 4).reshape(H * G, D, 3 * HD)
    feed["w_swa"] = np.concatenate([slabs(u, 2) for u in swa])

    o0, o1, o2, o3 = OFF_Q, OFF_Q + QR, OFF_Q + QR + KR + RB, OFF_Q + QR + KR + RB + H * HD
    wide = 2 * QR
    feed["w_lat"] = np.concatenate(
        [padded(w, wide) for w in (slabs(w_in[:, o0:o1], 2), slabs(w_in[:, o1:o2], 2), slabs(x["w_uq"][0], 1),
                                   slabs(x["w_uk"][0].reshape(KR, HB * NOPE), 1),
                                   slabs(x["w_uv"][0].reshape(KR, HB * VD), 1))])
    feed["gain_lat"] = np.tile(np.concatenate([x["norm_cq"][0], x["norm_ckv"][0]]), (P, 1))
    kvw = x["w_mem_kv"][0]
    by_head = lambda w, n: w.reshape(D, -1, n).transpose(1, 0, 2)
    feed["w_mem"] = np.concatenate([slabs(kvw[:, :H * HD], 2), slabs(kvw[:, H * HD:], 2)]
                                   + [slabs(w, KD) for w in by_head(w_in[:, o2:o3], P)])

    cache = [x[f"cache_swa_g{g}"][0] for g in range(G)]
    for g in range(G):
        feed[f"cache{g}"] = cache[g]
    dil = GROUPS[2][1]
    wide2 = cache[2].reshape(NB, PAST // dil, dil, 2, H, HD)[:, :, :TS].transpose(0, 2, 1, 3, 4, 5)
    seen = np.concatenate([cache[0], cache[1], wide2.reshape(NB, CK[2], 2, H, HD), x["cache_mem_kv"][0]], 1)
    feed["k_smp"] = seen[:, :, 0].transpose(0, 3, 2, 1)
    feed["v_smp"] = seen[:, :, 1].reshape(NB, VBLK, P, 2, 2 * HD).transpose(0, 3, 2, 1, 4).reshape(2 * NB, P, VBLK, 2 * HD)
    feed["page_table"] = x["page_table"].reshape(1, -1)
    ckv, kr = x["cache_mla_ckv"][0], x["cache_mla_krope"][0]
    n_pool = ckv.shape[0]
    ckvT = ckv.transpose(0, 2, 1).reshape(n_pool, KR // P, P, P).transpose(0, 2, 1, 3).reshape(n_pool, P, KR)
    feed["pool"] = np.concatenate([ckvT, ckv], 2)
    feed["pool_kr"] = kr.transpose(0, 2, 1)
    feed["w_ukT"] = x["w_uk"][0].transpose(2, 1, 0)
    feed["w_uv"] = x["w_uv"][0].reshape(KR // P, P, HB * VD).transpose(1, 0, 2)
    by_cols = lambda w: w.reshape(512 // P, P, 4, 2 * P).transpose(2, 1, 0, 3).reshape(4, P, -1)
    feed["w_o"] = np.concatenate([by_cols(x[n][0]) for n in ("w_o_a", "w_o_b", "w_o_m")])
    blocks = lambda w: w.reshape(KD, P, -1, P).transpose(2, 1, 0, 3).reshape(-1, P, KD * P)
    feed["w_gate"] = blocks(w_in[:, o3:].reshape(D, 3, KD, P).transpose(0, 2, 1, 3).reshape(D, -1))
    feed["w_out"] = x["w_out"][0]
    up, down = blocks(x["w_up"][0]), x["w_down"][0].reshape(PAIRS, P, D)
    chunks = []
    for i in range(BODIES):
        f = 2 * i
        chunks += [up[f], up[f + PAIRS]] + ([down[f - 2], down[f - 1]] if i else []) + [up[f + 1], up[f + 1 + PAIRS]]
    chunks += [down[PAIRS - 2], down[PAIRS - 1]] * 2
    feed["w_ffn"] = np.stack(chunks)
    by_channel = lambda a: a.reshape(a.shape[:-1] + (CHUNKS, P)).transpose((a.ndim, a.ndim - 1) + tuple(range(a.ndim - 1)))
    feed["conv_prev"] = by_channel(x["state_ffn_conv"][0])
    feed["conv_coef"] = by_channel(np.concatenate([x["conv_w"][0], x["conv_b"]]))

    nc = bacc.Bacc("TRN2", target_bir_lowering=False, num_devices=1)
    io, arrays = {}, {}
    for name, a in feed.items():
        arrays[f"in_{name}"] = np.ascontiguousarray(a)
        io[name] = nc.dram_tensor(f"in_{name}", a.shape, mybir.dt.from_np(a.dtype), kind="ExternalInput").ap()
    outs = {}

    def output(name, shape):
        outs[name] = shape
        io[name] = nc.dram_tensor(f"out_{name}", shape, F32, kind="ExternalOutput").ap()
        return io[name]

    io["p_swa"] = [output(f"p_swa{g}", (min(w, S), 2, H, HD)) for g, (w, _) in enumerate(GROUPS)]
    ring_len = [min(w, PAST + TS) for w, _ in GROUPS]
    io["s_swa"] = [output(f"s_swa{g}", (NB, n, 2, H, HD)) for g, n in enumerate(ring_len)]
    io["s_swa_new"] = [a[:, n - TS:n] for a, n in zip(io["s_swa"], ring_len)]
    scratch = lambda name, shape: nc.dram_tensor(name, shape, F32).ap()
    io["smp_qk"] = scratch("smp_qk", (H, P, 2 * G, NSMP))
    io["smp_kv"] = scratch("smp_kv", (H, NSMP, G, 2, HD))
    io["smp_qm"] = scratch("smp_qm", (H, P, NSMP))
    io["bT_scr"] = scratch("bT_scr", (3, D, N))
    io["x1_scr"] = scratch("x1_scr", (N, D))
    output("y_p", (S, D))
    output("y_s", (NSMP, D))
    output("conv_last", (P, CHUNKS, 1 + NB, CONV - 1))
    io["qT_scr"] = scratch("qT_scr", (HB, NOPE + RB, N))
    io["kT_scr"] = scratch("kT_scr", (HB * NOPE, S))
    io["krT_scr"] = scratch("krT_scr", (RB, N))
    io["v_scr"] = scratch("v_scr", (S, HB * VD))
    output("p_ckv", (S, KR))
    output("p_kr", (S, RB))
    output("s_ckv", (NSMP, KR))
    output("s_kr", (NSMP, RB))
    output("p_mem", (NMEM, 2, H * HD))
    io["oT_scr"] = scratch("oT_scr", (3, 512, N))
    build(nc, io)
    r = run(nc, [arrays], core_ids=[0])
    got = {n: r.results[0][f"out_{n}"] for n in outs}
    conv = got["conv_last"].transpose(2, 3, 1, 0).reshape(1 + NB, CONV - 1, 2 * DFF)
    kept = lambda g: got[f"p_swa{g}"].reshape((1, 1) + got[f"p_swa{g}"].shape)
    return (got["y_p"].reshape(1, S, D), got["y_s"].reshape(NB, TS, D), kept(0), kept(1), kept(2),
            got["p_ckv"].reshape(1, 1, S, KR), got["p_kr"].reshape(1, 1, S, RB),
            got["p_mem"].reshape(1, 1, NMEM, 2, H, HD), conv[0:1].reshape(1, 1, CONV - 1, 2 * DFF),
            got["s_swa0"][None], got["s_swa1"][None], got["s_swa2"][None],
            got["s_ckv"].reshape(1, NB, TS, KR), got["s_kr"].reshape(1, NB, TS, RB), conv[1:][None])
```

```python
from contextlib import ExitStack

import numpy as np

import concourse.bass as bass
from concourse import mybir

ALU = mybir.AluOpType
ACT = mybir.ActivationFunctionType
AX = mybir.AxisListType
F32 = mybir.dt.float32
F32R = mybir.dt.float32r
I32 = mybir.dt.int32

P = 128
D = 1024
KD = D // P
S = 1024
NB, TS = 8, 8
NSMP = NB * TS
N = S + NSMP
PT_TILES = S // P
TILES = PT_TILES + 1
PAST = 1024
GROUPS = ((128, 1), (512, 4), (2048, 16))
G = len(GROUPS)
H = 4
HD = 128
HB, NOPE, RB, VD = 8, 64, 32, 64
QR, KR = 384, 256
NMEM = 256
DFF = 2816
EPS = 1e-6
SCALE_A = HD ** -0.5
SCALE_B = (NOPE + RB) ** -0.5
LOWEST = -3.0e38
COL = [(0, 384), (384, 384), (768, 320)]


def rows_of(t):
    return P if t < PT_TILES else NSMP


class Mem:

    spent = []

    def __init__(self, nc, ctx, name):
        self.nc, self.ctx, self.name = nc, ctx, name

    def sb(self, name, shape, dt=F32):
        return self.ctx.enter_context(self.nc.sbuf_tensor(f"{self.name}_{name}", shape, dt))

    def ps(self, name, shape):
        return self.ctx.enter_context(self.nc.psum_tensor(f"{self.name}_{name}", shape, F32))

    def sem(self, name):
        sem = self.ctx.enter_context(self.nc.semaphore(f"{self.name}_{name}"))
        Mem.spent.append(sem.num)
        return sem


def clear_spent(pool, numbers):
    first = None
    for n in sorted(numbers):
        if first is None or n != last + 1:
            if first is not None:
                pool.sem_clear(range(first, last + 1))
            first = n
        last = n
    pool.sem_clear(range(first, last + 1))


def mm3(pe, out, w_hi, w_lo, x_hi, x_lo, start, stop):
    pe.matmul(out, w_hi, x_hi, start=start, stop=False)
    pe.matmul(out, w_hi, x_lo, start=False, stop=False)
    return pe.matmul(out, w_lo, x_hi, start=False, stop=stop)


class WeightRing:

    RAW = 3

    def __init__(self, m, src, width, slots):
        self.src, self.width, self.R = src, width, slots
        self.raw = m.sb("w_raw", [P, self.RAW, width])
        self.hi = m.sb("w_hi", [P, slots, width], F32R)
        self.lo = m.sb("w_lo", [P, slots, width], F32R)
        self.landed = [m.sem(f"w_landed{i}") for i in range(self.RAW)]
        self.rounded = m.sem("w_rounded")
        self.ready = m.sem("w_ready")
        self.used = m.sem("w_used")

    def load(self, sp, base, j):
        sp.wait_ge(self.ready, base + j + 1)
        sp.dma_start(self.raw[:, j % self.RAW, :], self.src[base + j]).then_inc(self.landed[j % self.RAW], 16)

    def round_hi(self, act, base, j, free=False):
        act.wait_ge(self.landed[j % self.RAW], 16 * self.turn(base, j) + 16)
        if not free:
            act.wait_ge(self.used, base + j + 1)
        act.activation(self.hi[:, j % self.R, :], self.raw[:, j % self.RAW, :], ACT.Copy).then_inc(self.rounded, 1)

    def rest_lo(self, dve, base, j):
        dve.wait_ge(self.rounded, base + j + 1)
        dve.tensor_tensor(self.lo[:, j % self.R, :], self.raw[:, j % self.RAW, :],
                          self.hi[:, j % self.R, :].bitcast(F32), ALU.subtract).then_inc(self.ready, 1)

    def turn(self, base, j):
        if isinstance(base, int):
            return (base + j) // self.RAW
        return self.turns(base) + j // self.RAW

    def credit(self, dve, pe):
        if dve is not None:
            dve.sem_inc(self.ready, self.RAW)
        if pe is not None:
            pe.sem_inc(self.used, self.R)

    def wait(self, pe, base, j):
        pe.wait_ge(self.ready, base + j + 1 + self.RAW)


def normalise(nc, io, name, items):
    with ExitStack() as ctx:
        m = Mem(nc, ctx, name)
        XS = 4
        xs = m.sb("x", [P, XS, D])
        sq = m.sb("sq", [P, D])
        ss = m.sb("ss", [P, 16])
        rstd = m.sb("rstd", [P, 16])
        half = m.sb("half", [P, 1])
        ident = m.sb("ident", [P, P])
        gains = m.sb("gains", [P, 3, KD])
        h = m.sb("h", [P, 2, D])
        h32 = m.sb("h32", [P, 2, KD, P])
        ps = m.ps("t", [P, 2, KD, P])
        landed = [m.sem(f"landed{i}") for i in range(XS)]
        const = m.sem("const")
        sq_done, mean_done, rstd_done = m.sem("sq_done"), m.sem("mean_done"), m.sem("rstd_done")
        h_done, turned, gained, hi_done, lo_done, half_set = (m.sem(x) for x in
            ("h_done", "turned", "gained", "hi_done", "lo_done", "half_set"))
        with nc.Block() as block:
            @block.sync
            def _(sp):
                sp.dma_start(ident[:], io["ident"]).then_inc(const, 16)
                sp.dma_start(gains[:], io["gains_pre"]).then_inc(const, 16)
                for i, (src, r, *_) in enumerate(items):
                    if i >= XS:
                        sp.wait_ge(h_done, i - XS + 1)
                    sp.dma_start(xs[0:r, i % XS, :], src).then_inc(landed[i % XS], 16)

            @block.scalar
            def _(act):
                def square(i):
                    r = items[i][1]
                    act.wait_ge(landed[i % XS], 16 * (i // XS + 1))
                    if i:
                        act.wait_ge(sq_done, i)
                    act.activation(sq[0:r, :], xs[0:r, i % XS, :], ACT.Square,
                                   accum_out=ss[0:r, i:i + 1]).then_inc(sq_done, 1)

                square(0)
                square(1)
                for i, (_, r, _, hi, _, c) in enumerate(items):
                    if i + 2 < len(items):
                        square(i + 2)
                    act.wait_ge(gained, i + 1)
                    act.activation(hi[:, :, c:c + r], h32[:, i % 2, :, 0:r], ACT.Copy).then_inc(hi_done, 1)

            @block.gpsimd
            def _(pool):
                pool.memset(half[:], -0.5).then_inc(half_set, 1)
                pool.wait_ge(half_set, 1)
                for i, (_, r, *_) in enumerate(items):
                    pool.wait_ge(sq_done, i + 1)
                    pool.tensor_scalar(ss[0:r, i:i + 1], ss[0:r, i:i + 1], 1.0 / D, EPS, ALU.mult,
                                       ALU.add).then_inc(mean_done, 1)
                    pool.wait_ge(mean_done, i + 1)
                    pool.tensor_tensor(rstd[0:r, i:i + 1], ss[0:r, i:i + 1], half[0:r, :], ALU.pow)\
                        .then_inc(rstd_done, 1)

            @block.tensor
            def _(pe):
                pe.wait_ge(const, 32)
                for i, (_, r, *_) in enumerate(items):
                    pe.wait_ge(h_done, i + 1)
                    if i >= 2:
                        pe.wait_ge(gained, i - 1)
                    for k in range(KD):
                        ins = pe.transpose(ps[:, i % 2, k, 0:r], h[0:r, i % 2, k * P:(k + 1) * P], ident[0:r, 0:r])
                    ins.then_inc(turned, 1)

            @block.vector
            def _(dve):
                dve.wait_ge(const, 32)
                def scale(i):
                    r = items[i][1]
                    dve.wait_ge(rstd_done, i + 1)
                    if i >= 2:
                        dve.wait_ge(turned, i - 1)
                    dve.tensor_scalar(h[0:r, i % 2, :], xs[0:r, i % XS, :], rstd[0:r, i:i + 1], None,
                                      ALU.mult).then_inc(h_done, 1)

                def rest(i):
                    _, r, _, hi, lo, c = items[i]
                    dve.wait_ge(hi_done, i + 1)
                    dve.tensor_tensor(lo[:, :, c:c + r], h32[:, i % 2, :, 0:r], hi[:, :, c:c + r].bitcast(F32),
                                      ALU.subtract).then_inc(lo_done, 1)

                scale(0)
                for i, (_, r, g, *_) in enumerate(items):
                    if i + 1 < len(items):
                        scale(i + 1)
                    dve.wait_ge(turned, i + 1)
                    if i >= 2:
                        dve.wait_ge(lo_done, i - 1)
                    gain = gains[:, g, :].rearrange("p (k a) -> p k a", a=1).broadcast_to([P, KD, r])
                    dve.tensor_tensor(h32[:, i % 2, :, 0:r], ps[:, i % 2, :, 0:r], gain, ALU.mult).then_inc(gained, 1)
                    if i:
                        rest(i - 1)
                rest(len(items) - 1)


PARTS = 2
ITS = [(part, t) for part in range(PARTS) for t in range(PT_TILES)]
HALFT = PT_TILES // 2


def blocks_of(part, t):
    if part == 0:
        return [(0, kt) for kt in range(max(0, t - 1), t + 1)]
    return [(1, t % HALFT), (1, t % HALFT + HALFT), (2, t)]


MOST = 3
MASK_BLOCKS = 2 + 2 * MOST


def mask_at(part, t):
    return (1 if t == 0 else 0) if part == 0 else 2 + MOST * (t // HALFT)


def tile_of(x, g, k, t):
    if t == PT_TILES:
        return x[:, k, S:N]
    return x[:, k, t * P:(t + 1) * P] if g == 0 else x[:, k, t:S:PT_TILES]


def window_attention(nc, io, hT_hi, hT_lo):
    with ExitStack() as ctx:
        m = Mem(nc, ctx, "win")
        ring = WeightRing(m, io["w_swa"], 2 * 3 * P, 6)
        CH = 12
        PR = G * TILES
        NI = len(ITS)
        NO = 2 + 2 * PARTS
        NST = 2 * G + 2
        ident = m.sb("ident", [P, P])
        mask = m.sb("mask", [P, MASK_BLOCKS * P])
        cosb = m.sb("cos", [P, 2, TILES, HD // 2])
        sinb = m.sb("sin", [P, 2, TILES, 2, HD // 2])
        qkT = m.sb("qkT", [P, G, 2, N])
        kv = m.sb("kv", [P, G, TILES, 2, HD])
        qrot = m.sb("qrot", [P, 2, HD])
        ra = m.sb("ra", [P, 2, 2, 2, HD // 2])
        rb = m.sb("rb", [P, 2, 2, 2, HD // 2])
        prob = m.sb("prob", [P, 3, MOST * P])
        spare = m.sb("spare", [P, 1])
        mx = m.sb("mx", [P, 2])
        nm = m.sb("nm", [P, PARTS, PT_TILES])
        den = m.sb("den", [P, PARTS, PT_TILES])
        rden = m.sb("rden", [P, 2])
        probT = m.sb("probT", [P, 2, MOST * P])
        oT = m.sb("oT", [P, PARTS, S])
        ps = m.ps("ps", [P, 8, 512])
        names = ("const", "pj_done", "ab_done", "rotated", "v_done", "tq_done", "tq_read", "s_done", "mx_read",
                 "nm_done", "exp_done", "rden_done", "p_done", "tp_done", "tp_read", "o_done", "o_read", "stored",
                 "o_stored", "kept")
        s = {n: m.sem(n) for n in names}

        ring.turns = lambda base: (base // ring.RAW)

        with nc.Block() as block:
            @block.sync
            def _(sp):
                with sp.Fori(0, H) as h:
                    for j in range(CH):
                        ring.load(sp, CH * h, j)
                        if j % 6 == 5:
                            b = 2 * h + j // 6
                            for g, (win, _) in enumerate(GROUPS):
                                first, n = max(0, PAST + TS - win) - max(0, PAST - win), min(win, PAST + TS) - TS
                                sp.dma_start(io["s_swa"][g][b, 0:n], io[f"cache{g}"][b, first:first + n])\
                                    .then_inc(s["kept"], 16)
                    sp.wait_ge(s["tq_read"], PR * h + PR + 2)
                    sp.wait_ge(s["v_done"], PR * h + PR + 2)
                    for g, (win, _) in enumerate(GROUPS):
                        keep = min(win, S)
                        for c in range(2):
                            if g == 0:
                                dst, src = io["p_swa"][g].rearrange("p c h d -> c h p d")[c, h], kv[:, g, PT_TILES - 1, c, :]
                            else:
                                dst = io["p_swa"][g].rearrange("(m t) c h d -> c h m t d", t=PT_TILES)[c, h]
                                src = kv[P - keep // PT_TILES:P, g, 0:PT_TILES, c, :]
                            sp.dma_start(dst, src).then_inc(s["stored"], 16)
                    sp.dma_start(io["smp_kv"][h], kv[0:NSMP, :, TILES - 1]).then_inc(s["stored"], 16)
                    sp.dma_start(io["smp_qk"][h], qkT[:, :, :, S:N].rearrange("p g c n -> p (g c) n"))\
                        .then_inc(s["stored"], 16)
                sp.wait_ge(s["stored"], 16 * NST * (H + 1))
                sp.wait_ge(s["o_stored"], 16 * NO * (H + 1))
                sp.wait_ge(s["kept"], 16 * G * NB)

            @block.tensor
            def _(pe):
                pe.sem_inc(ring.used, ring.R)

                def turn_qk(h, p, last_chunk=False):
                    g, t = divmod(p, TILES)
                    r = rows_of(t)
                    pe.wait_ge(s["rotated"], PR * h + p + 3)
                    pe.wait_ge(s["tq_read"], PR * h + (2 if p == 0 else p + 1))
                    if p == 0:
                        pe.wait_ge(s["const"], 64)
                    ins = pe.transpose(ps[:, 2 + p % 2, 0:P], qrot[:, p % 2, :], ident[:])
                    if last_chunk:
                        ins.then_inc(ring.used, 1)
                    pe.transpose(ps[:, 2 + p % 2, P:2 * P], kv[:, g, t, 0, :], ident[:]).then_inc(s["tq_done"], 1)

                def scores(h, i):
                    part, t = ITS[i]
                    pe.wait_ge(s["mx_read"], NI * h + i + 1)
                    for j, (g, kt) in enumerate(blocks_of(part, t)):
                        ins = pe.matmul(ps[:, i % 4, j * P:(j + 1) * P], qkT[:, g, 0, t * P:(t + 1) * P],
                                        qkT[:, g, 1, kt * P:(kt + 1) * P], start=True, stop=True)
                    ins.then_inc(s["s_done"], 1)

                def turn_p(h, i):
                    pe.wait_ge(s["p_done"], NI * h + i + 1)
                    pe.wait_ge(s["tp_read"], NI * h + i + 1)
                    for j in range(len(blocks_of(*ITS[i]))):
                        ins = pe.transpose(ps[:, 4 + i % 2, j * P:(j + 1) * P], prob[:, i % 3, j * P:(j + 1) * P], ident[:])
                    ins.then_inc(s["tp_done"], 1)

                def values(h, i):
                    pe.wait_ge(s["o_read"], NI * h + i + 1)
                    pe.wait_ge(s["tp_read"], NI * h + i + 3)
                    bl = blocks_of(*ITS[i])
                    for j, (g, kt) in enumerate(bl):
                        ins = pe.matmul(ps[:, 6 + i % 2, 0:P], kv[:, g, kt, 1, :], probT[:, i % 2, j * P:(j + 1) * P],
                                        start=j == 0, stop=j == len(bl) - 1)
                    ins.then_inc(s["o_done"], 1)

                with pe.Fori(0, H) as h:
                    for p in range(PR):
                        g, t = divmod(p, TILES)
                        r = rows_of(t)
                        pe.wait_ge(s["ab_done"], PR * h + (2 if p == 0 else p + 1))
                        pe.wait_ge(s["v_done"], PR * h + (2 if p == 0 else p + 1))
                        for c in range(4):
                            j = 4 * g + c
                            if t == 0:
                                ring.wait(pe, CH * h, j)
                            for i in range(2):
                                k = 2 * c + i
                                w = slice(i * 3 * P, (i + 1) * 3 * P)
                                ins = mm3(pe, ps[0:r, p % 2, 0:3 * P], tile_of(hT_hi, g, k, t), tile_of(hT_lo, g, k, t),
                                          ring.hi[:, j % ring.R, w], ring.lo[:, j % ring.R, w], k == 0, k == KD - 1)
                            if t == TILES - 1 and c < 3:
                                ins.then_inc(ring.used, 1)
                        ins.then_inc(s["pj_done"], 1)
                        if p:
                            turn_qk(h, p - 1, t == TILES - 1)
                    turn_qk(h, PR - 1)
                    pe.wait_ge(s["tq_read"], PR * h + PR + 2)
                    pe.wait_ge(s["v_done"], PR * h + PR + 2)
                    scores(h, 0)
                    scores(h, 1)
                    for i in range(NI):
                        if i + 2 < NI:
                            scores(h, i + 2)
                        turn_p(h, i)
                        if i:
                            values(h, i - 1)
                    values(h, NI - 1)

            @block.scalar
            def _(act):
                for dst, src in ((cosb, "cos_a"), (sinb, "sin_a"), (ident, "ident"), (mask, "mask_p")):
                    act.dma_start(dst[:], io[src]).then_inc(s["const"], 16)
                act.sem_inc(s["v_done"], 2)
                act.sem_inc(s["tq_read"], 2)
                act.sem_inc(s["tp_read"], 2)
                act.sem_inc(s["o_read"], 2)
                act.sem_inc(s["stored"], 16 * NST)
                act.sem_inc(s["o_stored"], 16 * NO)

                def turned_qk(h, p):
                    g, t = divmod(p, TILES)
                    r = rows_of(t)
                    act.wait_ge(s["tq_done"], PR * h + p + 1)
                    act.activation(qkT[:, g, :, t * P:t * P + r],
                                   ps[:, 2 + p % 2, 0:2 * P].rearrange("p (a b) -> p a b", a=2)[:, :, 0:r],
                                   ACT.Copy).then_inc(s["tq_read"], 1)

                def keep_o(h, i):
                    part, t = ITS[i]
                    act.wait_ge(s["o_done"], NI * h + i + 1)
                    dst = oT[:, 0, t * P:(t + 1) * P] if part == 0 else oT[:, 1, t:S:PT_TILES]
                    act.activation(dst, ps[:, 6 + i % 2, 0:P], ACT.Copy).then_inc(s["o_read"], 1)

                def exps(h, i):
                    part, t = ITS[i]
                    w = len(blocks_of(part, t)) * P
                    act.wait_ge(s["nm_done"], NI * h + i + 1)
                    act.activation(prob[:, i % 3, 0:w], prob[:, i % 3, 0:w], ACT.Exp, bias=nm[:, part, t:t + 1],
                                   accum_out=den[:, part, t:t + 1]).then_inc(s["exp_done"], 1)

                with act.Fori(0, H) as h:
                    for j in range(6):
                        ring.round_hi(act, CH * h, j)
                    act.wait_ge(s["stored"], 16 * NST * h + 16 * NST)
                    for p in range(PR):
                        g, t = divmod(p, TILES)
                        r = rows_of(t)
                        act.wait_ge(s["pj_done"], PR * h + p + 1)
                        act.activation(kv[0:r, g, t, 1, :], ps[0:r, p % 2, 2 * P:3 * P], ACT.Copy)\
                            .then_inc(s["v_done"], 1)
                        if t == TILES - 1:
                            for j in ((6, 7, 8, 9), (10, 11), ())[g]:
                                ring.round_hi(act, CH * h, j)
                        if p:
                            turned_qk(h, p - 1)
                    turned_qk(h, PR - 1)
                    act.wait_ge(s["o_stored"], 16 * NO * h + 16 * NO)
                    exps(h, 0)
                    exps(h, 1)
                    for i, (part, t) in enumerate(ITS):
                        w = len(blocks_of(part, t)) * P
                        act.wait_ge(s["tp_done"], NI * h + i + 1)
                        act.activation(probT[:, i % 2, 0:w], ps[:, 4 + i % 2, 0:w], ACT.Copy).then_inc(s["tp_read"], 1)
                        if i + 2 < NI:
                            exps(h, i + 2)
                        if i:
                            keep_o(h, i - 1)
                    keep_o(h, NI - 1)
                    act.wait_ge(s["o_read"], NI * h + NI + 2)
                    act.dma_start(io["oA_scr"][bass.ts(h, P), :], oT[:, 0]).then_inc(s["o_stored"], 16)
                    act.dma_start(io["oT_scr"][0, bass.ts(h, P), 0:S], oT[:, 1]).then_inc(s["o_stored"], 16)
                    for n, x in enumerate((nm, den)):
                        act.dma_start(io["stat_scr"][h, 0, n].rearrange("(t p) -> p t", p=P), x[:, 0],
                                      allow_slow_non_contiguous=True).then_inc(s["o_stored"], 16)
                        act.dma_start(io["stat_scr"][h, 1, n].rearrange("(p t) -> p t", p=P), x[:, 1]).then_inc(s["o_stored"], 16)

            @block.vector
            def _(dve):
                dve.sem_inc(ring.ready, ring.RAW)
                dve.sem_inc(s["ab_done"], 2)
                dve.sem_inc(s["mx_read"], 4)
                dve.memset(kv[NSMP:P, :, TILES - 1], 0.0)
                def rotate(h, p):
                    g, t = divmod(p, TILES)
                    r = rows_of(t)
                    if p == 0:
                        dve.wait_ge(s["const"], 64)
                    dve.wait_ge(s["v_done"], PR * h + p + 3)
                    dve.wait_ge(s["rotated"], PR * h + (2 if p == 0 else p + 1))
                    x = ps[0:r, p % 2, 0:2 * HD].rearrange("p (a b c) -> p a b c", a=2, b=2)
                    co = cosb[0:r, min(g, 1), t, :].rearrange("p (a b c) -> p a b c", a=1, b=1).broadcast_to([r, 2, 2, HD // 2])
                    dve.tensor_tensor(ra[0:r, p % 2], x, co, ALU.mult)
                    for i in range(2):
                        si = sinb[0:r, min(g, 1), t, i, :].rearrange("p (a c) -> p a c", a=1).broadcast_to([r, 2, HD // 2])
                        ins = dve.tensor_tensor(rb[0:r, p % 2, :, i, :], x[:, :, 1 - i, :], si, ALU.mult)
                        if i:
                            ins.then_inc(s["ab_done"], 1)

                def mask_max(h, i):
                    part, t = ITS[i]
                    w, at = len(blocks_of(part, t)) * P, mask_at(part, t) * P
                    dve.wait_ge(s["s_done"], NI * h + i + 1)
                    dve.tensor_scalar(spare[:], ident[:, 0:1], 1.0, None, ALU.mult)
                    dve.tensor_tensor_reduce(prob[:, i % 3, 0:w], ps[:, i % 4, 0:w], mask[:, at:at + w], SCALE_A, LOWEST,
                                             ALU.add, ALU.max, mx[:, i % 2:i % 2 + 1]).then_inc(s["mx_read"], 1)
                    dve.wait_ge(s["mx_read"], NI * h + i + 5)
                    dve.tensor_scalar(nm[:, part, t:t + 1], mx[:, i % 2:i % 2 + 1], -1.0, None, ALU.mult)\
                        .then_inc(s["nm_done"], 1)

                with dve.Fori(0, H) as h:
                    for j in range(6):
                        ring.rest_lo(dve, CH * h, j)
                    for p in range(PR):
                        g, t = divmod(p, TILES)
                        rotate(h, p)
                        if t == TILES - 1:
                            for j in ((6, 7, 8, 9), (10, 11), ())[g]:
                                ring.rest_lo(dve, CH * h, j)
                    dve.wait_ge(s["o_stored"], 16 * NO * h + 16 * NO)
                    mask_max(h, 0)
                    mask_max(h, 1)
                    for i, (part, t) in enumerate(ITS):
                        w = len(blocks_of(part, t)) * P
                        dve.wait_ge(s["exp_done"], NI * h + i + 1)
                        dve.reciprocal(rden[:, i % 2:i % 2 + 1], den[:, part, t:t + 1]).then_inc(s["rden_done"], 1)
                        dve.wait_ge(s["rden_done"], NI * h + i + 1)
                        dve.tensor_scalar(prob[:, i % 3, 0:w], prob[:, i % 3, 0:w], rden[:, i % 2:i % 2 + 1], None,
                                          ALU.mult).then_inc(s["p_done"], 1)
                        if i + 2 < NI:
                            mask_max(h, i + 2)

            @block.gpsimd
            def _(pool):
                pool.sem_inc(s["rotated"], 2)
                with pool.Fori(0, H) as h:
                    pool.wait_ge(s["stored"], 16 * NST * h + 16 * NST)
                    for p in range(PR):
                        g, t = divmod(p, TILES)
                        r = rows_of(t)
                        pool.wait_ge(s["ab_done"], PR * h + p + 3)
                        if p >= 2:
                            pool.wait_ge(s["tq_done"], PR * h + p - 1)
                        pool.tensor_tensor(qrot[0:r, p % 2, :].rearrange("p (a c) -> p a c", a=2), ra[0:r, p % 2, 0],
                                           rb[0:r, p % 2, 0], ALU.add)
                        pool.tensor_tensor(kv[0:r, g, t, 0, :].rearrange("p (a c) -> p a c", a=2), ra[0:r, p % 2, 1],
                                           rb[0:r, p % 2, 1], ALU.add).then_inc(s["rotated"], 1)

def memory_attention(nc, io, hT_hi, hT_lo, mT_hi, mT_lo):
    with ExitStack() as ctx:
        m = Mem(nc, ctx, "mem")
        ring = WeightRing(m, io["w_mem"], KD * P, 6)
        MT = NMEM // P
        KV_CH = 2 * 4
        CHUNKS = KV_CH + H
        ident = m.sb("ident", [P, P])
        kv = m.sb("kv", [P, MT, 2, H * HD])
        kT = m.sb("kT", [P, H, NMEM])
        qT = m.sb("qT", [P, H, N])
        prob = m.sb("prob", [P, 4, NMEM])
        probT = m.sb("probT", [P, 2, NMEM])
        oT = m.sb("oT", [P, H, S])
        nm, den, rden = m.sb("nm", [P, 4]), m.sb("den", [P, 4]), m.sb("rden", [P, 4])
        ps = m.ps("ps", [P, 8, 512])
        s = {n: m.sem(n) for n in ("const", "pj_done", "pj_read", "tk_done", "tk_read", "s_done", "nm_done",
                                   "exp_done", "rden_done", "p_done", "tp_done", "tp_read", "o_done", "o_read",
                                   "stored")}
        UNITS = 2 * MT + 3 * H
        ITS = [(h, t) for h in range(H) for t in range(PT_TILES)]
        ring.turns = None

        with nc.Block() as block:
            @block.sync
            def _(sp):
                sp.dma_start(ident[:], io["ident"]).then_inc(s["const"], 16)
                for j in range(CHUNKS):
                    ring.load(sp, 0, j)
                sp.wait_ge(s["pj_read"], 2 * MT)
                sp.dma_start(io["p_mem"].rearrange("(t p) c n -> p t c n", p=P), kv[:]).then_inc(s["stored"], 16)
                sp.wait_ge(s["pj_read"], UNITS)
                sp.dma_start(io["smp_qm"].rearrange("h p n -> p h n"), qT[:, :, S:N]).then_inc(s["stored"], 16)
                for h in range(H):
                    sp.wait_ge(s["o_read"], PT_TILES * (h + 1))
                    sp.dma_start(io["oT_scr"][2, h * P:(h + 1) * P, 0:S], oT[:, h]).then_inc(s["stored"], 16)
                sp.wait_ge(s["stored"], 16 * (2 + H))

            @block.tensor
            def _(pe):
                pe.sem_inc(ring.used, ring.R)
                pe.wait_ge(s["const"], 16)
                u = 0
                for c in range(2):
                    for t in range(MT):
                        if u >= 4:
                            pe.wait_ge(s["pj_read"], u - 3)
                        for k in range(KD):
                            j = 4 * c + k // 2
                            if t == 0:
                                ring.wait(pe, 0, j)
                            w = slice(k % 2 * 512, k % 2 * 512 + 512)
                            ins = mm3(pe, ps[:, u % 4, :], mT_hi[:, k, t * P:(t + 1) * P], mT_lo[:, k, t * P:(t + 1) * P],
                                      ring.hi[:, j % ring.R, w], ring.lo[:, j % ring.R, w], k == 0, k == KD - 1)
                            if t == MT - 1 and k % 2 and k < KD - 1:
                                ins.then_inc(ring.used, 1)
                        ins.then_inc(s["pj_done"], 1)
                        u += 1
                    pe.wait_ge(s["pj_done"], u)
                    pe.sem_inc(ring.used, 1)
                for t in range(MT):
                    pe.wait_ge(s["pj_read"], t + 1)
                    for h in range(H):
                        ins = pe.transpose(ps[:, 4 + t, h * P:(h + 1) * P], kv[:, t, 0, h * P:(h + 1) * P], ident[:])
                    ins.then_inc(s["tk_done"], 1)
                for h in range(H):
                    j = KV_CH + h
                    ring.wait(pe, 0, j)
                    for c, (at, n) in enumerate(COL):
                        pe.wait_ge(s["pj_read"], u - 3)
                        for k in range(KD):
                            w = slice(k * P, (k + 1) * P)
                            ins = mm3(pe, ps[:, u % 4, 0:n], ring.hi[:, j % ring.R, w], ring.lo[:, j % ring.R, w],
                                      hT_hi[:, k, at:at + n], hT_lo[:, k, at:at + n], k == 0, k == KD - 1)
                        ins.then_inc(s["pj_done"], 1)
                        u += 1
                pe.wait_ge(s["pj_read"], UNITS)
                pe.wait_ge(s["tk_read"], MT)

                def scores(i):
                    h, t = ITS[i]
                    if i >= 4:
                        pe.wait_ge(s["exp_done"], i - 3)
                    pe.matmul(ps[:, i % 4, 0:NMEM], qT[:, h, t * P:(t + 1) * P], kT[:, h, :], start=True,
                              stop=True).then_inc(s["s_done"], 1)

                def turn(i):
                    pe.wait_ge(s["p_done"], i + 1)
                    if i >= 2:
                        pe.wait_ge(s["tp_read"], i - 1)
                    for b in range(MT):
                        ins = pe.transpose(ps[:, 4 + i % 2, b * P:(b + 1) * P], prob[:, i % 4, b * P:(b + 1) * P], ident[:])
                    ins.then_inc(s["tp_done"], 1)

                def values(i):
                    h, t = ITS[i]
                    pe.wait_ge(s["tp_read"], i + 1)
                    if i >= 2:
                        pe.wait_ge(s["o_read"], i - 1)
                    for b in range(MT):
                        ins = pe.matmul(ps[:, 6 + i % 2, 0:P], kv[:, b, 1, h * P:(h + 1) * P],
                                        probT[:, i % 2, b * P:(b + 1) * P], start=b == 0, stop=b == MT - 1)
                    ins.then_inc(s["o_done"], 1)

                n = len(ITS)
                for i in range(n + 3):
                    if i < n:
                        scores(i)
                    if 2 <= i < n + 2:
                        turn(i - 2)
                    if i >= 3:
                        values(i - 3)

            @block.scalar
            def _(act):
                u = 0

                def read(dst, src, scale=1.0):
                    nonlocal u
                    act.wait_ge(s["pj_done"], u + 1)
                    act.activation(dst, src, ACT.Copy, scale=scale).then_inc(s["pj_read"], 1)
                    u += 1

                for j in range(4):
                    ring.round_hi(act, 0, j)
                for j in range(4, 6):
                    ring.round_hi(act, 0, j)
                for c in range(2):
                    for t in range(MT):
                        read(kv[:, t, c, :], ps[:, u % 4, :])
                    if c == 0:
                        for j in (6, 7, 8, 9):
                            ring.round_hi(act, 0, j)
                for j in (10, 11):
                    ring.round_hi(act, 0, j)
                for t in range(MT):
                    act.wait_ge(s["tk_done"], t + 1)
                    act.activation(kT[:, :, t * P:(t + 1) * P], ps[:, 4 + t, :].rearrange("p (h n) -> p h n", h=H),
                                   ACT.Copy).then_inc(s["tk_read"], 1)
                for h in range(H):
                    for at, n in COL:
                        read(qT[:, h, at:at + n], ps[:, u % 4, 0:n], SCALE_A)

                def exps(i):
                    act.wait_ge(s["nm_done"], i + 1)
                    act.activation(prob[:, i % 4, :], ps[:, i % 4, 0:NMEM], ACT.Exp, bias=nm[:, i % 4:i % 4 + 1],
                                   accum_out=den[:, i % 4:i % 4 + 1]).then_inc(s["exp_done"], 1)

                n = len(ITS)
                for i in range(n + 3):
                    if i < n:
                        exps(i)
                    if 2 <= i < n + 2:
                        b = (i - 2) % 2
                        act.wait_ge(s["tp_done"], i - 1)
                        act.activation(probT[:, b, :], ps[:, 4 + b, 0:NMEM], ACT.Copy).then_inc(s["tp_read"], 1)
                    if i >= 3:
                        h, t = ITS[i - 3]
                        act.wait_ge(s["o_done"], i - 2)
                        act.activation(oT[:, h, t * P:(t + 1) * P], ps[:, 6 + (i - 3) % 2, 0:P], ACT.Copy)\
                            .then_inc(s["o_read"], 1)

            @block.vector
            def _(dve):
                dve.sem_inc(ring.ready, ring.RAW)
                for j in range(CHUNKS):
                    ring.rest_lo(dve, 0, j)
                n = len(ITS)
                for i in range(n + 1):
                    if i < n:
                        dve.wait_ge(s["s_done"], i + 1)
                        dve.tensor_reduce(nm[:, i % 4:i % 4 + 1], ps[:, i % 4, 0:NMEM], AX.X, ALU.max,
                                          negate=True).then_inc(s["nm_done"], 1)
                    if i >= 1:
                        b = (i - 1) % 4
                        dve.wait_ge(s["exp_done"], i)
                        dve.reciprocal(rden[:, b:b + 1], den[:, b:b + 1]).then_inc(s["rden_done"], 1)
                        dve.wait_ge(s["rden_done"], i)
                        dve.tensor_scalar(prob[:, b, :], prob[:, b, :], rden[:, b:b + 1], None, ALU.mult)\
                            .then_inc(s["p_done"], 1)


def latent_projections(nc, io, hT_hi, hT_lo):
    with ExitStack() as ctx:
        m = Mem(nc, ctx, "lat")
        ring = WeightRing(m, io["w_lat"], 2 * QR, 6)
        KQ, KK = QR // P, KR // P
        UNIT = ((QR, KQ), (KR + RB, KK))
        ident = m.sb("ident", [P, P])
        gain = m.sb("gain", [P, QR + KR])
        cosb = m.sb("cos", [P, TILES, RB // 2])
        sinb = m.sb("sin", [P, TILES, 2, RB // 2])
        raw = m.sb("raw", [P, 2, QR])
        sq = m.sb("sq", [P, QR])
        ss = m.sb("ss", [P, 2 * TILES])
        rstd = m.sb("rstd", [P, 2 * TILES])
        half = m.sb("half", [P, 1])
        xq = m.sb("xq", [P, 2, QR])
        xk = m.sb("xk", [P, TILES, KR + RB])
        ra, rb = m.sb("ra", [P, 2, HB, RB]), m.sb("rb", [P, 2, HB, RB])
        qT_hi, qT_lo = m.sb("qT_hi", [P, KQ, N], F32R), m.sb("qT_lo", [P, KQ, N], F32R)
        cT_hi, cT_lo = m.sb("cT_hi", [P, KK, N], F32R), m.sb("cT_lo", [P, KK, N], F32R)
        krT = m.sb("krT", [RB, N])
        q = m.sb("q", [P, 2, HB, NOPE + RB])
        qTs = m.sb("qTs", [NOPE + RB, 2, HB, P])
        st = m.sb("st", [P, 2, 512])
        ps = m.ps("ps", [P, 8, 512])
        s = {n: m.sem(n) for n in ("const", "half", "pj_done", "pj_read", "sq_done", "mean_done", "rstd_done",
                                   "x_done", "ra_done", "rot_done", "t_done", "hi_done", "lo_done", "qp_done", "qp_read",
                                   "qa_done", "q_done", "qt_done", "qt_read", "e_done", "e_read", "kstored", "kr_read")}
        q_stored = [m.sem(f"q_stored{i}") for i in range(2)]
        e_stored = [m.sem(f"e_stored{i}") for i in range(2)]
        STEPS = [(u, t) for u in range(2) for t in range(TILES)]
        CHUNKS = 8 + KQ + KK + KK
        EK = [(pair, c) for pair in range(HB // 2) for c in range(S // 512)]
        EV = list(range(PT_TILES))
        NE = len(EK) + len(EV)

        with nc.Block() as block:
            @block.sync
            def _(sp):
                for dst, src in ((ident, "ident"), (gain, "gain_lat"), (cosb, "cos_b"), (sinb, "sin_b")):
                    sp.dma_start(dst[:], io[src]).then_inc(s["const"], 16)
                for j in range(CHUNKS):
                    ring.load(sp, 0, j)
                sp.wait_ge(s["x_done"], 2 * TILES)
                sp.wait_ge(s["rot_done"], TILES)
                for t0, t1, r, ckv, kr in ((0, PT_TILES, P, "p_ckv", "p_kr"), (PT_TILES, TILES, NSMP, "s_ckv", "s_kr")):
                    sp.dma_start(io[ckv].rearrange("(t p) c -> p t c", p=r), xk[0:r, t0:t1, 0:KR]).then_inc(s["kstored"], 16)
                    sp.dma_start(io[kr].rearrange("(t p) c -> p t c", p=r), xk[0:r, t0:t1, KR:KR + RB])\
                        .then_inc(s["kstored"], 16)
                sp.wait_ge(s["kr_read"], TILES)
                sp.dma_start(io["krT_scr"], krT[:]).then_inc(s["kstored"], 16)
                for t in range(TILES):
                    r = rows_of(t)
                    sp.wait_ge(s["qt_read"], t + 1)
                    sp.dma_start(io["qT_scr"].rearrange("h c n -> c h n")[:, :, t * P:t * P + r], qTs[:, t % 2, :, 0:r])\
                        .then_inc(q_stored[t % 2], 16)
                for i in range(NE):
                    sp.wait_ge(s["e_read"], i + 1)
                    if i < len(EK):
                        pair, c = EK[i]
                        dst = io["kT_scr"][pair * P:(pair + 1) * P, c * 512:(c + 1) * 512]
                    else:
                        t = EV[i - len(EK)]
                        dst = io["v_scr"][t * P:(t + 1) * P, :]
                    sp.dma_start(dst, st[:, i % 2, :]).then_inc(e_stored[i % 2], 16)
                sp.wait_ge(s["kstored"], 16 * 5)
                for i in range(2):
                    sp.wait_ge(q_stored[i], 16 * ((TILES + 1 - i) // 2))
                    sp.wait_ge(e_stored[i], 16 * (NE // 2))

            @block.tensor
            def _(pe):
                pe.sem_inc(ring.used, ring.R)
                pe.wait_ge(s["const"], 64)

                def turn(i):
                    u, t = STEPS[i]
                    r, nb = rows_of(t), UNIT[u][1]
                    pe.wait_ge(s["x_done"], i + 1)
                    if i >= 2:
                        pe.wait_ge(s["lo_done"], i - 1)
                    src = xk[0:r, t, :] if u else xq[0:r, t % 2, :]
                    if u:
                        pe.wait_ge(s["rot_done"], t + 1)
                        if t >= 2:
                            pe.wait_ge(s["kr_read"], t - 1)
                        pe.transpose(ps[0:RB, 4 + i % 2, 3 * P:3 * P + r], src[:, KR:KR + RB], ident[0:r, 0:r])
                    for b in range(nb):
                        ins = pe.transpose(ps[:, 4 + i % 2, b * P:b * P + r], src[:, b * P:(b + 1) * P], ident[0:r, 0:r])
                    ins.then_inc(s["t_done"], 1)

                for i, (u, t) in enumerate(STEPS):
                    r, (cols, _) = rows_of(t), UNIT[u]
                    if i >= 2:
                        pe.wait_ge(s["pj_read"], i - 1)
                    for k in range(KD):
                        j = 4 * u + k // 2
                        if t == 0:
                            ring.wait(pe, 0, j)
                        w = slice(k % 2 * cols, (k % 2 + 1) * cols)
                        x = slice(t * P, t * P + r)
                        ins = mm3(pe, ps[0:r, i % 2, 0:cols], hT_hi[:, k, x], hT_lo[:, k, x], ring.hi[:, j % ring.R, w],
                                  ring.lo[:, j % ring.R, w], k == 0, k == KD - 1)
                        if t == TILES - 1 and k % 2 and k < KD - 1:
                            ins.then_inc(ring.used, 1)
                    ins.then_inc(s["pj_done"], 1)
                    if t == TILES - 1:
                        pe.wait_ge(s["pj_done"], i + 1)
                        pe.sem_inc(ring.used, 1)
                    if i:
                        turn(i - 1)
                turn(len(STEPS) - 1)

                def turn_q(t):
                    r = rows_of(t)
                    pe.wait_ge(s["q_done"], t + 1)
                    if t >= 2:
                        pe.wait_ge(s["qt_read"], t - 1)
                    bank = 4 + 2 * (t % 2)
                    for h in range(HB):
                        ins = pe.transpose(ps[0:NOPE + RB, bank + h // 4, (h % 4) * P:(h % 4) * P + r], q[0:r, t % 2, h, :],
                                           ident[0:r, 0:r])
                    ins.then_inc(s["qt_done"], 1)

                pe.wait_ge(s["lo_done"], 2 * TILES)
                pe.wait_ge(s["kr_read"], TILES)
                for t in range(TILES):
                    r = rows_of(t)
                    if t >= 2:
                        pe.wait_ge(s["qp_read"], t - 1)
                    for c in range(2):
                        for k in range(KQ):
                            j = 8 + k
                            if t == 0 and c == 0:
                                ring.wait(pe, 0, j)
                            w = slice(c * QR, (c + 1) * QR)
                            x = slice(t * P, t * P + r)
                            ins = mm3(pe, ps[0:r, 2 * (t % 2) + c, 0:QR], qT_hi[:, k, x], qT_lo[:, k, x],
                                      ring.hi[:, j % ring.R, w], ring.lo[:, j % ring.R, w], k == 0, k == KQ - 1)
                    ins.then_inc(s["qp_done"], 1)
                    if t:
                        turn_q(t - 1)
                turn_q(TILES - 1)
                pe.wait_ge(s["qp_done"], TILES)
                pe.sem_inc(ring.used, KQ)
                pe.wait_ge(s["qp_read"], TILES)
                for i in range(NE):
                    if i >= 2:
                        pe.wait_ge(s["e_read"], i - 1)
                    for k in range(KK):
                        if i < len(EK):
                            pair, c = EK[i]
                            j = 8 + KQ + k
                            w = slice(pair * P, (pair + 1) * P)
                            x = slice(c * 512, (c + 1) * 512)
                            a = ring.hi[:, j % ring.R, w], ring.lo[:, j % ring.R, w], cT_hi[:, k, x], cT_lo[:, k, x]
                        else:
                            t = EV[i - len(EK)]
                            j = 8 + KQ + KK + k
                            x = slice(t * P, (t + 1) * P)
                            a = cT_hi[:, k, x], cT_lo[:, k, x], ring.hi[:, j % ring.R, 0:512], ring.lo[:, j % ring.R, 0:512]
                        if i in (0, len(EK)):
                            ring.wait(pe, 0, j)
                        ins = mm3(pe, ps[:, i % 2, :], *a, k == 0, k == KK - 1)
                    ins.then_inc(s["e_done"], 1)

            def read_q(act, t):
                r = rows_of(t)
                act.wait_ge(s["qt_done"], t + 1)
                if t >= 2:
                    act.wait_ge(q_stored[t % 2], 16 * (t // 2))
                bank = 4 + 2 * (t % 2)
                act.activation(qTs[:, t % 2, :, 0:r].rearrange("p (a h) n -> p a h n", a=2),
                               ps[0:NOPE + RB, bank:bank + 2, :].rearrange("p a (h n) -> p a h n", h=4)[:, :, :, 0:r],
                               ACT.Copy).then_inc(s["qt_read"], 1)

            @block.scalar
            def _(act):
                for j in range(6):
                    ring.round_hi(act, 0, j)

                def split(i):
                    u, t = STEPS[i]
                    r, nb = rows_of(t), UNIT[u][1]
                    act.wait_ge(s["t_done"], i + 1)
                    if u:
                        act.activation(krT[:, t * P:t * P + r], ps[0:RB, 4 + i % 2, 3 * P:3 * P + r], ACT.Copy)\
                            .then_inc(s["kr_read"], 1)
                    hi = cT_hi if u else qT_hi
                    act.activation(hi[:, 0:nb, t * P:t * P + r],
                                   ps[:, 4 + i % 2, 0:nb * P].rearrange("p (b n) -> p b n", b=nb)[:, :, 0:r],
                                   ACT.Copy).then_inc(s["hi_done"], 1)

                for i, (u, t) in enumerate(STEPS):
                    r, (cols, nb) = rows_of(t), UNIT[u]
                    act.wait_ge(s["pj_done"], i + 1)
                    if i:
                        act.wait_ge(s["sq_done"], i)
                    act.activation(sq[0:r, 0:nb * P], ps[0:r, i % 2, 0:nb * P], ACT.Square, accum_out=ss[0:r, i:i + 1])\
                        .then_inc(s["sq_done"], 1)
                    if i >= 2:
                        act.wait_ge(s["x_done"], i - 1)
                        if u and t >= 2:
                            act.wait_ge(s["ra_done"], 2 * (t - 1))
                    act.activation(raw[0:r, i % 2, 0:cols], ps[0:r, i % 2, 0:cols], ACT.Copy).then_inc(s["pj_read"], 1)
                    if t == TILES - 1:
                        for j in ((6, 7, 8, 9), (10, 11, 12, 13))[u]:
                            ring.round_hi(act, 0, j)
                    if i:
                        split(i - 1)
                split(len(STEPS) - 1)
                for t in range(TILES):
                    r = rows_of(t)
                    act.wait_ge(s["qp_done"], t + 1)
                    if t >= 2:
                        act.wait_ge(s["qt_done"], t - 1)
                    act.activation(q[0:r, t % 2].rearrange("p h c -> p (h c)").rearrange("p (a c) -> p a c", a=2),
                                   ps[0:r, 2 * (t % 2):2 * (t % 2) + 2, 0:QR], ACT.Copy, scale=SCALE_B)\
                        .then_inc(s["qp_read"], 1)
                    if t:
                        turned_q = t - 1
                        read_q(act, turned_q)
                read_q(act, TILES - 1)
                ring.round_hi(act, 0, CHUNKS - 1)
                for i in range(NE):
                    act.wait_ge(s["e_done"], i + 1)
                    if i >= 2:
                        act.wait_ge(e_stored[i % 2], 16 * (i // 2))
                    act.activation(st[:, i % 2, :], ps[:, i % 2, :], ACT.Copy).then_inc(s["e_read"], 1)

            @block.gpsimd
            def _(pool):
                pool.memset(half[:], -0.5).then_inc(s["half"], 1)
                pool.wait_ge(s["half"], 1)
                for i, (u, t) in enumerate(STEPS):
                    r = rows_of(t)
                    pool.wait_ge(s["sq_done"], i + 1)
                    pool.tensor_scalar(ss[0:r, i:i + 1], ss[0:r, i:i + 1], 1.0 / (UNIT[u][1] * P), EPS, ALU.mult,
                                       ALU.add).then_inc(s["mean_done"], 1)
                    pool.wait_ge(s["mean_done"], i + 1)
                    pool.tensor_tensor(rstd[0:r, i:i + 1], ss[0:r, i:i + 1], half[0:r, :], ALU.pow)\
                        .then_inc(s["rstd_done"], 1)

            @block.vector
            def _(dve):
                dve.sem_inc(ring.ready, ring.RAW)
                for j in range(6):
                    ring.rest_lo(dve, 0, j)
                dve.wait_ge(s["const"], 64)

                def rotate(dst, src, t, heads, b, count, done):
                    r = rows_of(t)
                    half_ = RB // 2
                    co = cosb[0:r, t, :].rearrange("p (a b c) -> p a b c", a=1, b=1).broadcast_to([r, heads, 2, half_])
                    a = ra[0:r, b, 0:heads, :].rearrange("p h (i c) -> p h i c", i=2)
                    c = rb[0:r, b, 0:heads, :].rearrange("p h (i c) -> p h i c", i=2)
                    dve.tensor_tensor(a, src, co, ALU.mult)
                    for i in range(2):
                        si = sinb[0:r, t, i, :].rearrange("p (a c) -> p a c", a=1).broadcast_to([r, heads, half_])
                        dve.tensor_tensor(c[:, :, i, :], src[:, :, 1 - i, :], si, ALU.mult).then_inc(s["ra_done"], 1)
                    dve.wait_ge(s["ra_done"], count + 2)
                    dve.tensor_tensor(dst, a, c, ALU.add).then_inc(done, 1)

                def rest(i):
                    u, t = STEPS[i]
                    r, nb = rows_of(t), UNIT[u][1]
                    hi, lo = (cT_hi, cT_lo) if u else (qT_hi, qT_lo)
                    dve.wait_ge(s["hi_done"], i + 1)
                    x = slice(t * P, t * P + r)
                    dve.tensor_tensor(lo[:, 0:nb, x], ps[:, 4 + i % 2, 0:nb * P].rearrange("p (b n) -> p b n", b=nb)[:, :, 0:r],
                                      hi[:, 0:nb, x].bitcast(F32), ALU.subtract).then_inc(s["lo_done"], 1)

                for i, (u, t) in enumerate(STEPS):
                    r, nb = rows_of(t), UNIT[u][1]
                    dve.wait_ge(s["rstd_done"], i + 1)
                    dve.wait_ge(s["pj_read"], i + 1)
                    if i >= 2:
                        dve.wait_ge(s["t_done"], i - 1)
                    dst = xk[0:r, t, 0:KR] if u else xq[0:r, t % 2, :]
                    dve.scalar_tensor_tensor(dst, raw[0:r, i % 2, 0:nb * P], rstd[0:r, i:i + 1],
                                             gain[0:r, u * QR:u * QR + nb * P], ALU.mult, ALU.mult).then_inc(s["x_done"], 1)
                    if u:
                        rotate(xk[0:r, t, KR:].rearrange("p (a i c) -> p a i c", a=1, i=2),
                               raw[0:r, i % 2, KR:KR + RB].rearrange("p (a i c) -> p a i c", a=1, i=2), t, 1, t % 2,
                               2 * t, s["rot_done"])
                    if t == TILES - 1:
                        for j in ((6, 7, 8, 9), (10, 11, 12, 13))[u]:
                            ring.rest_lo(dve, 0, j)
                    if i:
                        rest(i - 1)
                rest(len(STEPS) - 1)
                for t in range(TILES):
                    r = rows_of(t)
                    dve.wait_ge(s["qp_read"], t + 1)
                    v = q[0:r, t % 2, :, NOPE:].rearrange("p h (i c) -> p h i c", i=2)
                    rotate(v, v, t, HB, t % 2, 2 * TILES + 2 * t, s["q_done"])
                ring.rest_lo(dve, 0, CHUNKS - 1)


def latent_attention(nc, io):
    with ExitStack() as ctx:
        m = Mem(nc, ctx, "la")
        C = NOPE + RB
        PAIRS = HB // 2
        ident = m.sb("ident", [P, P])
        mask = m.sb("mask", [P, S])
        qT = m.sb("qT", [C, 2, 2, S])
        kT = m.sb("kT", [C, 2, 2, S])
        v = m.sb("v", [P, 2, PT_TILES, 2 * VD])
        prob = m.sb("prob", [P, 2, S])
        probT = m.sb("probT", [P, 2, 2, 512])
        oT = m.sb("oT", [P, 2, S])
        spare = m.sb("spare", [P, 1])
        mx, nm, den, rden = (m.sb(n, [P, 2]) for n in ("mx", "nm", "den", "rden"))
        ps = m.ps("ps", [P, 8, 512])
        s = {n: m.sem(n) for n in ("const", "s_done", "mx_read", "nm_done", "exp_done", "rden_done", "p_done", "tp_done",
                                   "tp_read", "o_done", "o_read", "pair_used")}
        landed = [m.sem(f"landed{i}") for i in range(2)]
        o_stored = [m.sem(f"o_stored{i}") for i in range(2)]
        ITS = [(b, a, t) for b in range(2) for a in range(2) for t in range(PT_TILES)]
        NI = len(ITS)
        QB = [0]
        for _, _, t in ITS:
            QB.append(QB[-1] + t // 4 + 1)
        NQ = QB[-1]
        assert NQ % 2 == 0

        with nc.Block() as block:
            @block.sync
            def _(sp):
                sp.dma_start(ident[:], io["ident"]).then_inc(s["const"], 16)
                sp.dma_start(mask[:], io["mask_c"]).then_inc(s["const"], 16)
                with sp.Fori(0, PAIRS // 2) as g:
                    for b in range(2):
                        pair = 2 * g + b
                        sp.wait_ge(s["pair_used"], 2 * g + b + 1)
                        sp.dma_start(qT[:, b], io["qT_scr"].rearrange("(a h) c n -> a c h n", h=2)[pair][:, :, 0:S])\
                            .then_inc(landed[b], 16)
                        sp.dma_start(kT[0:NOPE, b], io["kT_scr"].rearrange("(a h c) n -> a c h n", h=2, c=NOPE)[pair])\
                            .then_inc(landed[b], 16)
                        for a in range(2):
                            sp.dma_start(kT[NOPE:C, b, a], io["krT_scr"][:, 0:S]).then_inc(landed[b], 16)
                        sp.dma_start(v[:, b], io["v_scr"].rearrange("(t p) (a c) -> a p t c", p=P, c=2 * VD)[pair])\
                            .then_inc(landed[b], 16)

            @block.tensor
            def _(pe):
                pe.sem_inc(s["pair_used"], 2)
                pe.wait_ge(s["const"], 32)

                def scores(g, i):
                    b, a, t = ITS[i]
                    if a == 0 and t == 0:
                        pe.wait_ge(landed[b], 80 * g + 80)
                    pe.wait_ge(s["mx_read"], NI * g + i + 1)
                    w = (t + 1) * P
                    for c in range(0, w, 512):
                        n = min(512, w - c)
                        ins = pe.matmul(ps[:, 2 * (i % 2) + c // 512, 0:n], qT[:, b, a, t * P:(t + 1) * P],
                                        kT[:, b, a, c:c + n], start=True, stop=True)
                    ins.then_inc(s["s_done"], 1)

                def turn(g, i, q):
                    b, a, t = ITS[i]
                    n = QB[i] + q
                    pe.wait_ge(s["tp_read"], NQ * g + n + 1)
                    for j in range(4 * q, min(4 * q + 4, t + 1)):
                        ins = pe.transpose(ps[:, 4 + n % 2, (j % 4) * P:(j % 4 + 1) * P], prob[:, i % 2, j * P:(j + 1) * P],
                                           ident[:])
                    ins.then_inc(s["tp_done"], 1)

                def values(g, i):
                    b, a, t = ITS[i]
                    pe.wait_ge(s["o_read"], NI * g + i + 1)
                    for q in range(t // 4 + 1):
                        pe.wait_ge(s["tp_read"], NQ * g + QB[i] + q + 3)
                        for j in range(4 * q, min(4 * q + 4, t + 1)):
                            ins = pe.matmul(ps[a * VD:(a + 1) * VD, 6 + i % 2, 0:P], v[:, b, j, a * VD:(a + 1) * VD],
                                            probT[:, i % 2, q, (j % 4) * P:(j % 4 + 1) * P], start=j == 0, stop=j == t)
                    ins.then_inc(s["o_done"], 1)
                    if a == 1 and t == PT_TILES - 1:
                        pe.wait_ge(s["o_done"], NI * g + i + 1)
                        pe.sem_inc(s["pair_used"], 1)

                with pe.Fori(0, PAIRS // 2) as g:
                    scores(g, 0)
                    for i, (b, a, t) in enumerate(ITS):
                        if i + 1 < NI:
                            scores(g, i + 1)
                        pe.wait_ge(s["p_done"], NI * g + i + 1)
                        for q in range(t // 4 + 1):
                            turn(g, i, q)
                        if i:
                            values(g, i - 1)
                    values(g, NI - 1)

            @block.scalar
            def _(act):
                act.sem_inc(s["tp_read"], 2)
                act.sem_inc(s["o_read"], 2)
                for b in range(2):
                    act.sem_inc(o_stored[b], 16)

                def exps(g, i):
                    w = (ITS[i][2] + 1) * P
                    act.wait_ge(s["nm_done"], NI * g + i + 1)
                    act.activation(prob[:, i % 2, 0:w], prob[:, i % 2, 0:w], ACT.Exp, bias=nm[:, i % 2:i % 2 + 1],
                                   accum_out=den[:, i % 2:i % 2 + 1]).then_inc(s["exp_done"], 1)

                def keep_o(g, i):
                    b, a, t = ITS[i]
                    if a == 0 and t == 0:
                        act.wait_ge(o_stored[b], 16 * g + 16)
                    act.wait_ge(s["o_done"], NI * g + i + 1)
                    act.activation(oT[a * VD:(a + 1) * VD, b, t * P:(t + 1) * P],
                                   ps[a * VD:(a + 1) * VD, 6 + i % 2, 0:P], ACT.Copy).then_inc(s["o_read"], 1)
                    if a == 1 and t == PT_TILES - 1:
                        act.wait_ge(s["o_read"], NI * g + i + 3)
                        act.dma_start(io["oT_scr"][1].rearrange("(a p) n -> a p n", p=P)[2 * g + b][:, 0:S], oT[:, b])\
                            .then_inc(o_stored[b], 16)

                with act.Fori(0, PAIRS // 2) as g:
                    exps(g, 0)
                    for i, (b, a, t) in enumerate(ITS):
                        if i + 1 < NI:
                            exps(g, i + 1)
                        for q in range(t // 4 + 1):
                            n = QB[i] + q
                            w = (min(4 * q + 4, t + 1) - 4 * q) * P
                            act.wait_ge(s["tp_done"], NQ * g + n + 1)
                            act.activation(probT[:, i % 2, q, 0:w], ps[:, 4 + n % 2, 0:w], ACT.Copy).then_inc(s["tp_read"], 1)
                        if i:
                            keep_o(g, i - 1)
                    keep_o(g, NI - 1)
                for b in range(2):
                    act.wait_ge(o_stored[b], 16 * (PAIRS // 2) + 16)

            @block.vector
            def _(dve):
                dve.sem_inc(s["mx_read"], 2)
                dve.wait_ge(s["const"], 32)

                def mask_max(g, i):
                    b, a, t = ITS[i]
                    w = (t + 1) * P
                    dve.wait_ge(s["s_done"], NI * g + i + 1)
                    dve.tensor_scalar(spare[:], ident[:, 0:1], 1.0, None, ALU.mult)
                    sc = ps[:, 2 * (i % 2):2 * (i % 2) + 2, :].rearrange("p a n -> p (a n)")
                    dve.tensor_tensor_reduce(prob[:, i % 2, 0:w], sc[:, 0:w], mask[:, S - w:S], 1.0, LOWEST, ALU.add,
                                             ALU.max, mx[:, i % 2:i % 2 + 1]).then_inc(s["mx_read"], 1)
                    dve.wait_ge(s["mx_read"], NI * g + i + 3)
                    dve.tensor_scalar(nm[:, i % 2:i % 2 + 1], mx[:, i % 2:i % 2 + 1], -1.0, None, ALU.mult)\
                        .then_inc(s["nm_done"], 1)

                with dve.Fori(0, PAIRS // 2) as g:
                    mask_max(g, 0)
                    for i, (b, a, t) in enumerate(ITS):
                        w = (t + 1) * P
                        dve.wait_ge(s["exp_done"], NI * g + i + 1)
                        dve.reciprocal(rden[:, i % 2:i % 2 + 1], den[:, i % 2:i % 2 + 1]).then_inc(s["rden_done"], 1)
                        dve.wait_ge(s["rden_done"], NI * g + i + 1)
                        dve.tensor_scalar(prob[:, i % 2, 0:w], prob[:, i % 2, 0:w], rden[:, i % 2:i % 2 + 1], None,
                                          ALU.mult).then_inc(s["p_done"], 1)
                        if i + 1 < NI:
                            mask_max(g, i + 1)



CK = [128, 512, 512]
KEYS = sum(CK)
VBLK = (KEYS + NMEM) // P
VLOT = (VBLK + 1) // 2, VBLK // 2
WIN = KEYS + G * NSMP


def sample_attention(nc, io, spent):
    with ExitStack() as ctx:
        m = Mem(nc, ctx, "sa")
        BH = 4
        R = BH * H * TS
        ident = m.sb("ident", [P, P])
        mask = m.sb("mask", [P, WIN])
        qk = m.sb("qk", [P, H, 2 * G, NSMP])
        qm = m.sb("qm", [P, H, NSMP])
        vnew = m.sb("vnew", [NSMP, G, H * HD])
        qz = m.sb("qz", [P, NB, G + 1, H, H * TS])
        kc = m.sb("kc", [P, 2, H, KEYS + NMEM])
        vc = m.sb("vc", [P, 3, VLOT[0], H * HD])
        prob = m.sb("prob", [P, WIN + NMEM])
        probT = m.sb("probT", [P, VBLK + G, P])
        o = m.sb("o", [P, 2, H * HD])
        out = m.sb("out", [P, 2, H, NSMP])
        mx, nm, den, rden = m.sb("mx", [P, 4]), m.sb("nm", [P, 2]), m.sb("den", [P, 2]), m.sb("rden", [P, 2])
        ps = m.ps("ps", [P, 8, 512])
        s = {n: m.sem(n) for n in ("const", "vnew_in", "zeroed", "spread", "k_used", "v_used", "s_done", "mx_done", "nm_done",
                                   "exp_done", "rden_done", "p_done", "tp_done", "tp_read", "o_copied", "ot_done", "o_read",
                                   "stored",
                                   "mask_used", "masked")}
        k_in = [[m.sem(f"k_in{i}_{e}") for e in range(4)] for i in range(2)]
        v_in = [m.sem(f"v_in{i}") for i in range(3)]
        PB = [(P * i, P) for i in range(KEYS // P)] + [(WIN + P * i, P) for i in range(NMEM // P)]
        PB += [(KEYS + NSMP * g, NSMP) for g in range(G)]
        NQ = -(-len(PB) // 4)

        REGIONS = ((0, 1, CK[0], CK[1]), (1, 2, CK[0] + CK[1], CK[2]), (2, 0, 0, CK[0]), (3, G, KEYS, NMEM))

        with nc.Block() as block:
            @block.gpsimd
            def _(pool):
                clear_spent(pool, spent)

            @block.sync
            def _(sp):
                for dst, src in ((ident[:], io["ident"]), (qk[:], io["smp_qk"].rearrange("h p c n -> p h c n")),
                                 (qm[:], io["smp_qm"].rearrange("h p n -> p h n"))):
                    sp.dma_start(dst, src).then_inc(s["const"], 16)

                def load_k(b):
                    if b >= 2:
                        sp.wait_ge(s["k_used"], b - 1)
                    for e, (_, _, at, n) in enumerate(REGIONS):
                        sp.dma_start(kc[:, b % 2, :, at:at + n], io["k_smp"][b, :, :, at:at + n]).then_inc(k_in[b % 2][e], 16)

                def load_v(i):
                    if i >= 3:
                        sp.wait_ge(s["v_used"], i - 2)
                    first, n = (0, VLOT[0])[i % 2], VLOT[i % 2]
                    sp.dma_start(vc[:, i % 3, 0:n], io["v_smp"][i // 2, :, first:first + n]).then_inc(v_in[i % 3], 16)

                for b in range(2):
                    load_k(b)
                sp.dma_start(mask[:], io["mask_s"][0]).then_inc(s["masked"], 16)
                for i in range(3):
                    load_v(i)
                for b in range(2, NB):
                    load_k(b)
                sp.wait_ge(s["mask_used"], 1)
                sp.dma_start(mask[:], io["mask_s"][1]).then_inc(s["masked"], 16)
                for g in range(G):
                    for h in range(H):
                        for c in range(2):
                            sp.dma_start(io["s_swa_new"][g].rearrange("b t c h d -> c h b t d")[c, h],
                                         io["smp_kv"].rearrange("h (b t) g c d -> g c h b t d", b=NB)[g, c, h])\
                                .then_inc(s["stored"], 16)
                for i in range(3, 2 * NB):
                    load_v(i)
                sp.wait_ge(s["o_read"], 2)
                for i, br in enumerate((0, 2)):
                    sp.dma_start(io["oT_scr"][br].rearrange("(h p) n -> p h n", p=P)[:, :, S:N],
                                 out[:, i]).then_inc(s["stored"], 16)
                sp.wait_ge(s["stored"], 16 * (G * H * 2 + 2))

            @block.tensor
            def _(pe):
                pe.wait_ge(s["const"], 16 * 3)
                pe.wait_ge(s["spread"], 1)

                def scores(half):
                    if half:
                        pe.wait_ge(s["exp_done"], 1)
                    for i in range(BH):
                        b = BH * half + i
                        for e, (bank, g, at, n) in enumerate(REGIONS):
                            pe.wait_ge(k_in[b % 2][e], 16 * (b // 2 + 1))
                            for h in range(H):
                                ins = pe.matmul(ps[32 * i:32 * i + 32, bank, 0:n], qz[:, b, g, h, :],
                                                kc[:, b % 2, h, at:at + n], start=h == 0, stop=h == H - 1)
                        ins.then_inc(s["k_used"], 1)
                        for g in range(G):
                            for h in range(H):
                                ins = pe.matmul(ps[32 * i:32 * i + 32, 2, CK[0] + g * NSMP:CK[0] + (g + 1) * NSMP],
                                                qz[:, b, g, h, :], qk[:, h, 2 * g + 1, :], start=h == 0, stop=h == H - 1)
                    ins.then_inc(s["s_done"], 1)

                def turn(half, q):
                    n = NQ * half + q
                    if n >= 2:
                        pe.wait_ge(s["tp_read"], n - 1)
                    if half and q == 0:
                        pe.wait_ge(s["o_read"], 1)
                    for j in range(4 * q, min(4 * q + 4, len(PB))):
                        at, w = PB[j]
                        ins = pe.transpose(ps[0:w, 4 + n % 2, (j % 4) * P:(j % 4 + 1) * P], prob[:, at:at + w], ident[:])
                    ins.then_inc(s["tp_done"], 1)

                def values(half):
                    pe.wait_ge(s["tp_read"], NQ * (half + 1))
                    pe.wait_ge(s["vnew_in"], 16 * G)
                    if half:
                        pe.wait_ge(s["o_copied"], 1)
                    for i in range(BH):
                        rows = slice(i * H * TS, (i + 1) * H * TS)
                        for part in range(2):
                            lot = 2 * (BH * half + i) + part
                            pe.wait_ge(v_in[lot % 3], 16 * (lot // 3 + 1))
                            if part == 0:
                                for g in range(G):
                                    pe.matmul(ps[rows, 6, :], probT[0:NSMP, VBLK + g, rows], vnew[:, g, :], start=g == 0,
                                              stop=False)
                            for n in range(VLOT[part]):
                                j = part * VLOT[0] + n
                                ins = pe.matmul(ps[rows, 6 if j < KEYS // P else 7, :], probT[:, j, rows], vc[:, lot % 3, n, :],
                                                start=j == KEYS // P, stop=j in (KEYS // P - 1, VBLK - 1))
                            ins.then_inc(s["v_used"], 1)

                def turn_o(half):
                    pe.wait_ge(s["o_copied"], half + 1)
                    for br in range(2):
                        for h in range(H):
                            ins = pe.transpose(ps[:, 4 + br, h * HD:(h + 1) * HD], o[:, br, h * HD:(h + 1) * HD], ident[:])
                    ins.then_inc(s["ot_done"], 1)

                scores(0)
                scores(1)
                for half in range(2):
                    pe.wait_ge(s["p_done"], half + 1)
                    for q in range(NQ):
                        turn(half, q)
                    values(half)
                    turn_o(half)

            @block.scalar
            def _(act):
                for g in range(G):
                    act.dma_start(vnew[:, g].rearrange("n (h d) -> n h d", h=H), io["smp_kv"].rearrange("h n g c d -> c g n h d")[1, g])\
                        .then_inc(s["vnew_in"], 16)

                def exps(half):
                    act.wait_ge(s["nm_done"], half + 1)
                    act.activation(prob[:, 0:WIN], prob[:, 0:WIN], ACT.Exp, bias=nm[:, 0:1], accum_out=den[:, 0:1])
                    act.activation(prob[:, WIN:WIN + NMEM], ps[:, 3, 0:NMEM], ACT.Exp, bias=nm[:, 1:2],
                                   accum_out=den[:, 1:2]).then_inc(s["exp_done"], 1)

                def read_turned(half):
                    for q in range(NQ):
                        n = NQ * half + q
                        blocks = PB[4 * q:4 * q + 4]
                        act.wait_ge(s["tp_done"], n + 1)
                        groups = [[j for j, (_, w) in enumerate(blocks) if w == width] for width in (P, NSMP)]
                        for js in groups:
                            if js:
                                w = blocks[js[0]][1]
                                ins = act.activation(
                                    probT[0:w, 4 * q + js[0]:4 * q + js[-1] + 1, :],
                                    ps[0:w, 4 + n % 2, js[0] * P:(js[-1] + 1) * P].rearrange("p (j r) -> p j r", r=P), ACT.Copy)
                        ins.then_inc(s["tp_read"], 1)

                def copy_o(half):
                    act.wait_ge(s["v_used"], 2 * BH * (half + 1))
                    act.activation(o[:], ps[:, 6:8, :], ACT.Copy).then_inc(s["o_copied"], 1)

                def keep_own(half):
                    act.wait_ge(s["ot_done"], half + 1)
                    for br in range(2):
                        for h in range(H):
                            ins = act.activation(
                                out[:, br, h, half * BH * TS:(half + 1) * BH * TS].rearrange("p (b t) -> p b t", b=BH),
                                ps[:, 4 + br, h * HD:(h + 1) * HD].rearrange("p (b h t) -> p b h t", b=BH, h=H)[:, :, h, :], ACT.Copy)
                    ins.then_inc(s["o_read"], 1)

                exps(0)
                read_turned(0)
                exps(1)
                copy_o(0)
                keep_own(0)
                read_turned(1)
                copy_o(1)
                keep_own(1)

            @block.vector
            def _(dve):
                dve.memset(qz[:], 0.0).then_inc(s["zeroed"], 1)
                dve.wait_ge(s["zeroed"], 1)
                dve.wait_ge(s["const"], 16 * 3)
                for h in range(H):
                    for g in range(G + 1):
                        src = qk[:, h, 2 * g, :] if g < G else qm[:, h, :]
                        ins = dve.tensor_scalar(qz[:, :, g, h, h * TS:(h + 1) * TS], src.rearrange("p (b t) -> p b t", b=NB),
                                                SCALE_A if g < G else 1.0, None, ALU.mult)
                ins.then_inc(s["spread"], 1)
                for half in range(2):
                    dve.wait_ge(s["s_done"], half + 1)
                    dve.wait_ge(s["masked"], 16 * (half + 1))
                    parts = ((0, 0, CK[0], CK[1]), (1, 0, CK[0] + CK[1], CK[2]), (2, 0, 0, CK[0]),
                             (2, CK[0], KEYS, G * NSMP))
                    if half:
                        dve.wait_ge(s["tp_done"], NQ)
                    for i, (bank, c, at, n) in enumerate(parts):
                        ins = dve.tensor_tensor_reduce(prob[:, at:at + n], ps[:, bank, c:c + n], mask[:, at:at + n], 1.0,
                                                       LOWEST, ALU.add, ALU.max, mx[:, i:i + 1])
                    ins.then_inc(s["mx_done"], 1)
                    dve.tensor_reduce(nm[:, 1:2], ps[:, 3, 0:NMEM], AX.X, ALU.max, negate=True)
                    dve.wait_ge(s["mx_done"], half + 1)
                    dve.sem_inc(s["mask_used"], 1)
                    dve.tensor_reduce(nm[:, 0:1], mx[:], AX.X, ALU.max, negate=True).then_inc(s["nm_done"], 1)
                    dve.wait_ge(s["exp_done"], half + 1)
                    dve.reciprocal(rden[:], den[:]).then_inc(s["rden_done"], 1)
                    dve.wait_ge(s["rden_done"], half + 1)
                    dve.tensor_scalar(prob[:, 0:WIN], prob[:, 0:WIN], rden[:, 0:1], None, ALU.mult)
                    dve.tensor_scalar(prob[:, WIN:], prob[:, WIN:], rden[:, 1:2], None, ALU.mult).then_inc(s["p_done"], 1)


def sample_latent(nc, io):
    with ExitStack() as ctx:
        m = Mem(nc, ctx, "sl")
        KK = KR // P
        PAGES = PAST // P
        ident = m.sb("ident", [P, P])
        mask = m.sb("mask", [P, NB // 2, NSMP])
        table = m.sb("table", [1, NB * PAGES], I32)
        wukT = m.sb("wukT", [NOPE, HB, KR])
        wuv = m.sb("wuv", [P, KK, HB * VD])
        qn = m.sb("qn", [NOPE, HB, NSMP])
        qr = m.sb("qr", [RB, NB, HB, TS])
        krn = m.sb("krn", [RB, NSMP])
        cn = m.sb("cn", [NSMP, KR])
        cnT = m.sb("cnT", [P, KK, NSMP])
        ql = m.sb("ql", [P, KK, NB, HB, TS])
        page = m.sb("page", [P, 4, PAGES, 2 * KR])
        kr = m.sb("kr", [RB, 4, PAGES, P])
        prob = m.sb("prob", [P, 2, PAST + NSMP])
        probT = m.sb("probT", [P, PAGES + 1, P])
        ol = m.sb("ol", [P, KK, NB, HB, TS])
        ob = m.sb("ob", [P, HB // 2, NSMP])
        mx, nm, den, dsum, rden = m.sb("mx", [P, 2]), m.sb("nm", [P, 1]), m.sb("den", [P, 2]), m.sb("dsum", [P, 1]), m.sb("rden", [P, 1])
        ps = m.ps("ps", [P, 8, 512])
        s = {n: m.sem(n) for n in ("const", "table_in", "cn_done", "cn_read", "ql_done", "ql_read", "pg_used", "s_done", "mx_done", "nm_done",
                                   "exp_done", "dsum_done", "rden_done", "p_done", "tp_done", "tp_read",
                                   "ol_read", "ob_done", "ob_read", "stored")}
        pg_in = [m.sem(f"pg_in{i}") for i in range(4)]
        kr_in = [m.sem(f"kr_in{i}") for i in range(4)]

        with nc.Block() as block:
            @block.gpsimd
            def _(pool):
                pool.wait_ge(s["table_in"], 16)
                with pool.Fori(0, NB // 4) as g:
                    for b in range(4):
                        pool.wait_ge(s["pg_used"], 4 * g + b + 1)
                        for j in range(PAGES):
                            at = (4 * g + b) * PAGES + j
                            n = pool.value_load(table[0:1, bass.ds(at, 1)], min_val=0, max_val=io["pool"].shape[0] - 1)
                            pool.dma_start(kr[:, b, j, :], io["pool_kr"][n]).then_inc(kr_in[b], 16)

            @block.sync
            def _(sp):
                sp.dma_start(table[:], io["page_table"]).then_inc(s["table_in"], 16)
                sp.wait_ge(s["table_in"], 16)
                with sp.Fori(0, NB // 4) as g:
                    for b in range(4):
                        sp.wait_ge(s["pg_used"], 4 * g + b + 1)
                        for j in range(PAGES):
                            at = (4 * g + b) * PAGES + j
                            n = sp.value_load(table[0:1, bass.ds(at, 1)], min_val=0, max_val=io["pool"].shape[0] - 1)
                            sp.dma_start(page[:, b, j, :], io["pool"][n]).then_inc(pg_in[b], 16)
                sp.wait_ge(s["ob_read"], 1)
                sp.dma_start(io["oT_scr"][1].rearrange("(a p) n -> p a n", p=P)[:, :, S:N], ob[:]).then_inc(s["stored"], 16)
                sp.wait_ge(s["stored"], 16)

            @block.tensor
            def _(pe):
                pe.sem_inc(s["pg_used"], 4)
                pe.wait_ge(s["const"], 16 * (7 + HB))
                for k in range(KK):
                    ins = pe.transpose(ps[:, 2, k * NSMP:(k + 1) * NSMP], cn[:, k * P:(k + 1) * P], ident[0:NSMP, 0:NSMP])
                ins.then_inc(s["cn_done"], 1)
                for k in range(KK):
                    for h in range(HB):
                        ins = pe.matmul(ps[:, k, h * NSMP:(h + 1) * NSMP], wukT[:, h, k * P:(k + 1) * P], qn[:, h, :],
                                        start=True, stop=True)
                ins.then_inc(s["ql_done"], 1)
                pe.wait_ge(s["cn_read"], 1)
                pe.wait_ge(s["ql_read"], 1)
                def scores(g):
                    if g:
                        pe.wait_ge(s["exp_done"], g)
                    for b in range(2):
                        rows, sl = slice(64 * b, 64 * b + 64), (2 * g + b) % 4
                        pe.wait_ge(pg_in[sl], 16 * PAGES * (g // 2 + 1))
                        pe.wait_ge(kr_in[sl], 16 * PAGES * (g // 2 + 1))
                        for c in range(PAGES // 4):
                            o = ps[rows, c, :]
                            for k in range(KK):
                                pe.matmul(o, ql[:, k, 2 * g + b], page[:, sl, 4 * c:4 * c + 4, k * P:(k + 1) * P], start=k == 0,
                                          stop=False)
                            pe.matmul(o, qr[:, 2 * g + b], kr[:, sl, 4 * c:4 * c + 4, :], start=False, stop=True)
                        for k in range(KK):
                            pe.matmul(ps[rows, 2, 0:NSMP], ql[:, k, 2 * g + b], cnT[:, k, :], start=k == 0, stop=False)
                        ins = pe.matmul(ps[rows, 2, 0:NSMP], qr[:, 2 * g + b], krn[:], start=False, stop=True)
                    ins.then_inc(s["s_done"], 1)

                scores(0)
                for g in range(NB // 2):
                    if g + 1 < NB // 2:
                        scores(g + 1)
                    pe.wait_ge(s["p_done"], g + 1)
                    if g:
                        pe.wait_ge(s["tp_read"], g)
                    for j in range(PAGES):
                        pe.transpose(ps[:, 3 + j // 4, (j % 4) * P:(j % 4 + 1) * P], prob[:, g % 2, j * P:(j + 1) * P], ident[:])
                    pe.transpose(ps[0:NSMP, 5, 0:P], prob[:, g % 2, PAST:], ident[:]).then_inc(s["tp_done"], 1)
                    pe.wait_ge(s["tp_read"], g + 1)
                    for b in range(2):
                        cols, sl = slice(64 * b, 64 * b + 64), (2 * g + b) % 4
                        for k in range(KK):
                            o = ps[:, 6 + k, (2 * g + b) * 64:(2 * g + b + 1) * 64]
                            for j in range(PAGES):
                                pe.matmul(o, page[:, sl, j, KR + k * P:KR + (k + 1) * P], probT[:, j, cols], start=j == 0, stop=False)
                            ins = pe.matmul(o, cn[:, k * P:(k + 1) * P], probT[0:NSMP, PAGES, cols], start=False, stop=True)
                        ins.then_inc(s["pg_used"], 1)
                pe.wait_ge(s["ol_read"], 1)
                for h in range(HB):
                    for k in range(KK):
                        ins = pe.matmul(ps[(h % 2) * VD:(h % 2 + 1) * VD, 3, (h // 2) * NSMP:(h // 2 + 1) * NSMP],
                                        wuv[:, k, h * VD:(h + 1) * VD], ol[:, k, :, h, :], start=k == 0, stop=k == KK - 1)
                ins.then_inc(s["ob_done"], 1)

            @block.scalar
            def _(act):
                for dst, src in ((ident, "ident"), (mask, "mask_l"), (wukT, "w_ukT"), (wuv, "w_uv"), (cn, "s_ckv")):
                    act.dma_start(dst[:], io[src]).then_inc(s["const"], 16)
                act.dma_start(qn[:], io["qT_scr"].rearrange("h c n -> c h n")[0:NOPE, :, S:N]).then_inc(s["const"], 16)
                for h in range(HB):
                    act.dma_start(qr[:, :, h, :], io["qT_scr"][h, NOPE:NOPE + RB, S:N].rearrange("c (b t) -> c b t", b=NB))\
                        .then_inc(s["const"], 16)
                act.dma_start(krn[:], io["krT_scr"][:, S:N]).then_inc(s["const"], 16)

                act.wait_ge(s["cn_done"], 1)
                act.activation(cnT[:], ps[:, 2, 0:KK * NSMP].rearrange("p (k n) -> p k n", k=KK), ACT.Copy).then_inc(s["cn_read"], 1)
                act.wait_ge(s["ql_done"], 1)
                for k in range(KK):
                    ins = act.activation(ql[:, k].rearrange("p b h t -> p h b t"),
                                         ps[:, k, :].rearrange("p (h b t) -> p h b t", h=HB, b=NB), ACT.Copy)
                ins.then_inc(s["ql_read"], 1)
                def exps(g):
                    act.wait_ge(s["nm_done"], g + 1)
                    act.activation(prob[:, g % 2, PAST:], prob[:, g % 2, PAST:], ACT.Exp, bias=nm[:], accum_out=den[:, 1:2])
                    act.activation(prob[:, g % 2, 0:PAST], ps[:, 0:2, :].rearrange("p a n -> p (a n)"), ACT.Exp, bias=nm[:],
                                   accum_out=den[:, 0:1]).then_inc(s["exp_done"], 1)

                exps(0)
                for g in range(NB // 2):
                    if g:
                        act.wait_ge(s["pg_used"], 4 + 2 * g)
                    act.wait_ge(s["tp_done"], g + 1)
                    act.activation(probT[:, 0:PAGES, :].rearrange("p j r -> p (j r)"),
                                   ps[:, 3:5, :].rearrange("p a n -> p (a n)"), ACT.Copy)
                    act.activation(probT[0:NSMP, PAGES, :], ps[0:NSMP, 5, 0:P], ACT.Copy).then_inc(s["tp_read"], 1)
                    if g + 1 < NB // 2:
                        exps(g + 1)
                act.wait_ge(s["pg_used"], 4 + NB)
                act.activation(ol[:].rearrange("p k b h t -> p k (b h t)"), ps[:, 6:8, :], ACT.Copy).then_inc(s["ol_read"], 1)
                act.wait_ge(s["ob_done"], 1)
                act.activation(ob[:], ps[:, 3, 0:HB // 2 * NSMP].rearrange("p (a n) -> p a n", n=NSMP), ACT.Copy)\
                    .then_inc(s["ob_read"], 1)

            @block.vector
            def _(dve):
                dve.wait_ge(s["const"], 16 * (7 + HB))
                for g in range(NB // 2):
                    pr = prob[:, g % 2]
                    dve.wait_ge(s["s_done"], g + 1)
                    if g >= 2:
                        dve.wait_ge(s["tp_done"], g - 1)
                    dve.tensor_tensor_reduce(pr[:, PAST:], ps[:, 2, 0:NSMP], mask[:, g, :], 1.0, LOWEST, ALU.add, ALU.max,
                                             mx[:, 1:2])
                    dve.tensor_reduce(mx[:, 0:1], ps[:, 0:2, :].rearrange("p a n -> p (a n)"), AX.X, ALU.max)\
                        .then_inc(s["mx_done"], 1)
                    dve.wait_ge(s["mx_done"], g + 1)
                    dve.tensor_reduce(nm[:], mx[:], AX.X, ALU.max, negate=True).then_inc(s["nm_done"], 1)
                    dve.wait_ge(s["exp_done"], g + 1)
                    dve.tensor_reduce(dsum[:], den[:], AX.X, ALU.add).then_inc(s["dsum_done"], 1)
                    dve.wait_ge(s["dsum_done"], g + 1)
                    dve.reciprocal(rden[:], dsum[:]).then_inc(s["rden_done"], 1)
                    dve.wait_ge(s["rden_done"], g + 1)
                    dve.tensor_scalar(pr, pr, rden[:], None, ALU.mult).then_inc(s["p_done"], 1)


def branch_outputs(nc, io):
    with ExitStack() as ctx:
        m = Mem(nc, ctx, "br")
        K = 512 // P
        ring = WeightRing(m, io["w_o"], K * 2 * P, 3)
        BR, CH = 3, 4
        BRANCH = (1, 2, 0)
        o = m.sb("o", [P, K, N])
        o_hi, o_lo = m.sb("o_hi", [P, 2, K, N], F32R), m.sb("o_lo", [P, 2, K, N], F32R)
        st = m.sb("st", [P, 2, N])
        oA, wb = m.sb("oA", [P, S]), m.sb("wb", [P, S])
        stat = m.sb("stat", [P, 2, 2, H, PT_TILES])
        low, expo, wt = m.sb("low", [P, H, PT_TILES]), m.sb("expo", [P, 2, H, PT_TILES]), m.sb("wt", [P, 2, H, PT_TILES])
        ps = m.ps("ps", [P, 8, 512])
        s = {n: m.sem(n) for n in ("hi_done", "lo_done", "b_done", "b_read", "stat_in", "low_done", "diff_done",
                                   "exp_done", "mass_done", "total_done", "inv_done", "w_done", "w_stored", "head_in", "gap_done",
                                   "part_done", "head_done")}
        o_in = [m.sem(f"o_in{i}") for i in range(len(COL))]
        stored = [m.sem(f"stored{i}") for i in range(2)]
        ITS = [(br, c) for br in range(BR) for c in range(KD)]
        Q = len(COL)

        with nc.Block() as block:
            @block.sync
            def _(sp):
                for br in range(BR):
                    if br:
                        sp.wait_ge(s["lo_done"], Q * br)
                    for q, (at, n) in enumerate(COL):
                        sp.dma_start(o[:, :, at:at + n], io["oT_scr"][BRANCH[br]].rearrange("(k p) n -> p k n", p=P)[:, :, at:at + n])\
                            .then_inc(o_in[q], 16)
                        if q == 0:
                            ring.load(sp, 0, CH * br)
                    for j in range(CH * br + 1, CH * br + CH):
                        ring.load(sp, 0, j)
                    if br == 0:
                        for part in range(2):
                            for n in range(2):
                                sp.dma_start(stat[:, part, n], io["stat_scr"].rearrange("h a n (p t) -> a n p h t", p=P)[part, n])\
                                    .then_inc(s["stat_in"], 16)

            @block.tensor
            def _(pe):
                for i, (br, c) in enumerate(ITS):
                    j = CH * br + c // 2
                    if c % 2 == 0:
                        ring.wait(pe, 0, j)
                    if i >= 2:
                        pe.wait_ge(s["b_read"], i - 1)
                    for q, (at, n) in enumerate(COL):
                        if c == 0:
                            pe.wait_ge(s["lo_done"], Q * br + q + 1)
                        for k in range(K):
                            w = slice((2 * k + c % 2) * P, (2 * k + c % 2 + 1) * P)
                            ins = mm3(pe, ps[:, 3 * (i % 2) + q, 0:n], ring.hi[:, j % ring.R, w], ring.lo[:, j % ring.R, w],
                                      o_hi[:, br % 2, k, at:at + n], o_lo[:, br % 2, k, at:at + n], k == 0, k == K - 1)
                    ins.then_inc(s["b_done"], 1)

            @block.scalar
            def _(act):
                def split(br):
                    if BRANCH[br] == 0:
                        act.wait_ge(s["head_done"], H)
                    for q, (at, n) in enumerate(COL):
                        act.wait_ge(o_in[q], 16 * br + 16)
                        act.activation(o_hi[:, br % 2, :, at:at + n], o[:, :, at:at + n], ACT.Copy).then_inc(s["hi_done"], 1)

                ring.round_hi(act, 0, 0, True)
                split(0)
                for j in (1, 2):
                    ring.round_hi(act, 0, j, True)
                for i, (br, c) in enumerate(ITS):
                    act.wait_ge(s["b_done"], i + 1)
                    if i >= 2:
                        act.wait_ge(stored[i % 2], 16 * (i // 2))
                    for q, (at, n) in enumerate(COL):
                        ins = act.activation(st[:, i % 2, at:at + n], ps[:, 3 * (i % 2) + q, 0:n], ACT.Copy)
                    ins.then_inc(s["b_read"], 1)
                    if c % 2 and i // 2 + 3 < BR * CH:
                        ring.round_hi(act, 0, i // 2 + 3, True)
                    if i == 3:
                        act.wait_ge(s["diff_done"], 1)
                        act.activation(expo[:], expo[:], ACT.Exp).then_inc(s["exp_done"], 1)
                    if c == (3 if br == 0 else 5) and br + 1 < BR:
                        split(br + 1)
                    act.wait_ge(s["b_read"], i + 1)
                    act.dma_start(io["bT_scr"][BRANCH[br], c * P:(c + 1) * P, :], st[:, i % 2, :]).then_inc(stored[i % 2], 16)
                for i in range(2):
                    act.wait_ge(stored[i], 16 * (len(ITS) // 2))

            @block.vector
            def _(dve):
                dve.sem_inc(ring.ready, ring.RAW)

                def rest(br):
                    for q, (at, n) in enumerate(COL):
                        dve.wait_ge(s["hi_done"], Q * br + q + 1)
                        dve.tensor_tensor(o_lo[:, br % 2, :, at:at + n], o[:, :, at:at + n],
                                          o_hi[:, br % 2, :, at:at + n].bitcast(F32), ALU.subtract).then_inc(s["lo_done"], 1)

                ring.rest_lo(dve, 0, 0)
                rest(0)
                for j in (1, 2):
                    ring.rest_lo(dve, 0, j)
                dve.wait_ge(s["stat_in"], 64)
                dve.tensor_tensor(low[:], stat[:, 0, 0], stat[:, 1, 0], ALU.min).then_inc(s["low_done"], 1)
                dve.wait_ge(s["low_done"], 1)
                for part in range(2):
                    ins = dve.tensor_tensor(expo[:, part], low[:], stat[:, part, 0], ALU.subtract)
                ins.then_inc(s["diff_done"], 1)
                for br in range(BR):
                    for n in range(CH):
                        j = CH * br + n + 3
                        if j < BR * CH:
                            ring.rest_lo(dve, 0, j)
                        if br == 0 and n == 1:
                            dve.wait_ge(s["exp_done"], 1)
                            dve.tensor_tensor(wt[:], expo[:], stat[:, :, 1], ALU.mult).then_inc(s["mass_done"], 1)
                            dve.wait_ge(s["mass_done"], 1)
                            dve.tensor_tensor(low[:], wt[:, 0], wt[:, 1], ALU.add).then_inc(s["total_done"], 1)
                            dve.wait_ge(s["total_done"], 1)
                            dve.reciprocal(expo[:, 0], low[:]).then_inc(s["inv_done"], 1)
                            dve.wait_ge(s["inv_done"], 1)
                            dve.tensor_tensor(wt[:, 0], wt[:, 0], expo[:, 0], ALU.mult).then_inc(s["w_done"], 1)
                            rest(1)
                        for k in {(0, 3): (0,), (1, 0): (1, 2), (1, 1): (3,)}.get((br, n), ()):
                            for q in range(Q):
                                dve.wait_ge(o_in[q], 16 * BR)
                            dve.wait_ge(s["head_in"], 32 * k + 32)
                            dve.tensor_tensor(oA[:], oA[:], o[:, k, 0:S], ALU.subtract).then_inc(s["gap_done"], 1)
                            dve.wait_ge(s["gap_done"], k + 1)
                            dve.tensor_tensor(oA[:], oA[:], wb[:], ALU.mult).then_inc(s["part_done"], 1)
                            dve.wait_ge(s["part_done"], k + 1)
                            dve.tensor_tensor(o[:, k, 0:S], o[:, k, 0:S], oA[:], ALU.add).then_inc(s["head_done"], 1)
                        if (br, n) == (1, 1):
                            rest(2)

            @block.gpsimd
            def _(pool):
                pool.wait_ge(s["w_done"], 1)
                pool.dma_start(io["w_scr"].rearrange("h (p t) -> p h t", p=P), wt[:, 0]).then_inc(s["w_stored"], 16)
                pool.wait_ge(s["w_stored"], 16)
                for k in range(H):
                    if k:
                        pool.wait_ge(s["head_done"], k)
                    pool.dma_start(oA[:], io["oA_scr"][k * P:(k + 1) * P, :]).then_inc(s["head_in"], 16)
                    pool.dma_start(wb[:], io["w_scr"][k:k + 1, :].broadcast_to([P, S])).then_inc(s["head_in"], 16)


def merge(nc, io, hT_hi, hT_lo, mT_hi, mT_lo):
    with ExitStack() as ctx:
        m = Mem(nc, ctx, "mrg")
        ring = WeightRing(m, io["w_gate"], KD * P, 3)
        b_ = m.sb("b", [P, 3, N])
        sig = m.sb("sig", [P, 2, N])
        acc = m.sb("acc", [P, 2, N])
        ps = m.ps("ps", [P, 8, 512])
        s = {n: m.sem(n) for n in ("g_done", "sig_done", "prod_done", "sum_done", "hi_done", "lo_done")}
        b_in = [m.sem(f"b_in{i}") for i in range(3)]
        ITS = [(c, br) for c in range(KD) for br in range(3)]

        with nc.Block() as block:
            @block.sync
            def _(sp):
                for i, (c, br) in enumerate(ITS):
                    ring.load(sp, 0, i)
                    if i >= 3:
                        sp.wait_ge(s["sum_done"], i - 2)
                    sp.dma_start(b_[:, i % 3, :], io["bT_scr"][br, c * P:(c + 1) * P, :]).then_inc(b_in[i % 3], 16)

            @block.tensor
            def _(pe):
                for i, (c, br) in enumerate(ITS):
                    ring.wait(pe, 0, i)
                    if i >= 2:
                        pe.wait_ge(s["sig_done"], i - 1)
                    for q, (at, n) in enumerate(COL):
                        for k in range(KD):
                            w = slice(k * P, (k + 1) * P)
                            ins = mm3(pe, ps[:, 3 * (i % 2) + q, 0:n], ring.hi[:, i % ring.R, w], ring.lo[:, i % ring.R, w],
                                      hT_hi[:, k, at:at + n], hT_lo[:, k, at:at + n], k == 0, k == KD - 1)
                    ins.then_inc(s["g_done"], 1)

            @block.scalar
            def _(act):
                for j in range(3):
                    ring.round_hi(act, 0, j, True)
                for i, (c, br) in enumerate(ITS):
                    act.wait_ge(s["g_done"], i + 1)
                    if i >= 2:
                        act.wait_ge(s["sum_done"], i - 1)
                    for q, (at, n) in enumerate(COL):
                        ins = act.activation(sig[:, i % 2, at:at + n], ps[:, 3 * (i % 2) + q, 0:n], ACT.Sigmoid)
                    ins.then_inc(s["sig_done"], 1)
                    if i + 3 < len(ITS):
                        ring.round_hi(act, 0, i + 3, True)
                    if br == 2:
                        act.wait_ge(s["sum_done"], 3 * c + 3)
                        act.activation(mT_hi[:, c, :], acc[:, c % 2, :], ACT.Copy).then_inc(s["hi_done"], 1)

            @block.vector
            def _(dve):
                dve.sem_inc(ring.ready, ring.RAW)
                for j in range(3):
                    ring.rest_lo(dve, 0, j)

                def rest(c):
                    dve.wait_ge(s["hi_done"], c + 1)
                    dve.tensor_tensor(mT_lo[:, c, :], acc[:, c % 2, :], mT_hi[:, c, :].bitcast(F32), ALU.subtract)\
                        .then_inc(s["lo_done"], 1)

                for i, (c, br) in enumerate(ITS):
                    dve.wait_ge(s["sig_done"], i + 1)
                    dve.wait_ge(b_in[i % 3], 16 * (i // 3 + 1))
                    if br == 0:
                        dve.tensor_tensor(acc[:, c % 2, :], sig[:, i % 2, :], b_[:, i % 3, :], ALU.mult).then_inc(s["sum_done"], 1)
                        if c:
                            rest(c - 1)
                    else:
                        dve.tensor_tensor(sig[:, i % 2, :], sig[:, i % 2, :], b_[:, i % 3, :], ALU.mult).then_inc(s["prod_done"], 1)
                        dve.wait_ge(s["prod_done"], 2 * c + br)
                        dve.wait_ge(s["sum_done"], i)
                        dve.tensor_tensor(acc[:, c % 2, :], acc[:, c % 2, :], sig[:, i % 2, :], ALU.add).then_inc(s["sum_done"], 1)
                    if i + 3 < len(ITS):
                        ring.rest_lo(dve, 0, i + 3)
                rest(KD - 1)


def output_projection(nc, io, mT_hi, mT_lo):
    with ExitStack() as ctx:
        m = Mem(nc, ctx, "out")
        XS = 2
        raw = m.sb("raw", [P, 2, D])
        w_hi, w_lo = m.sb("w_hi", [P, KD, D], F32R), m.sb("w_lo", [P, KD, D], F32R)
        gain = m.sb("gain", [P, D])
        gains = m.sb("gains", [P, 3, KD])
        ident = m.sb("ident", [P, P])
        x = m.sb("x", [P, XS, D])
        sq = m.sb("sq", [P, D])
        y = m.sb("y", [P, 2, D])
        h = m.sb("h", [P, D])
        h32 = m.sb("h32", [P, KD, P])
        ss = m.sb("ss", [P, TILES, 2])
        mean, rstd, half = m.sb("mean", [P, TILES, 2]), m.sb("rstd", [P, TILES, 2]), m.sb("half", [P, 1])
        ps = m.ps("ps", [P, 8, 512])
        s = {n: m.sem(n) for n in ("const", "rounded", "ready", "y_done", "sq_done", "half_set", "mean_done",
                                   "rstd_done", "scaled", "added", "h_done", "turned", "gained", "hi_done", "lo_done")}
        landed = [m.sem(f"landed{i}") for i in range(2)]
        x_in = [m.sem(f"x_in{i}") for i in range(XS)]
        stored = [m.sem(f"stored{i}") for i in range(2)]
        flat = lambda t: ps[0:rows_of(t), 2 * (t % 3):2 * (t % 3) + 2, :].rearrange("p a n -> p (a n)")

        ORDER = [(0, 0)]
        for t in range(1, TILES):
            ORDER += [(t, 0), (t - 1, 1)]
        ORDER += [(TILES - 1, 1)]
        AT = {x: n for n, x in enumerate(ORDER)}

        with nc.Block() as block:
            @block.sync
            def _(sp):
                def store(t):
                    r = rows_of(t)
                    sp.wait_ge(s["added"], t + 1)
                    sp.dma_start(io["x1_scr"][t * P:t * P + r, :], y[0:r, t % 2, :]).then_inc(stored[t % 2], 16)

                for k in range(KD):
                    if k >= 2:
                        sp.wait_ge(s["ready"], k - 1)
                    sp.dma_start(raw[:, k % 2, :], io["w_out"][k * P:(k + 1) * P, :]).then_inc(landed[k % 2], 16)
                for dst, src in ((gain, io["gain_post"][0]), (gains, io["gains_pre"]), (ident, io["ident"])):
                    sp.dma_start(dst[:], src).then_inc(s["const"], 16)
                for t in range(TILES):
                    r = rows_of(t)
                    if t >= XS:
                        sp.wait_ge(s["added"], t - XS + 1)
                    src = io["xp"][t * P:(t + 1) * P, :] if t < PT_TILES else io["xs"]
                    sp.dma_start(x[0:r, t % XS, :], src).then_inc(x_in[t % XS], 16)
                    if t:
                        store(t - 1)
                store(TILES - 1)
                sp.wait_ge(stored[0], 16 * (TILES // 2 + 1))
                sp.wait_ge(stored[1], 16 * (TILES // 2))

            @block.tensor
            def _(pe):
                def turn(t):
                    r = rows_of(t)
                    pe.wait_ge(s["const"], 48)
                    pe.wait_ge(s["h_done"], t + 1)
                    if t:
                        pe.wait_ge(s["gained"], t)
                    for k in range(KD):
                        ins = pe.transpose(ps[:, 6 + k // 4, (k % 4) * P:(k % 4) * P + r], h[0:r, k * P:(k + 1) * P],
                                           ident[0:r, 0:r])
                    ins.then_inc(s["turned"], 1)

                for t in range(TILES):
                    r = rows_of(t)
                    if t >= 3:
                        pe.wait_ge(s["scaled"], t - 2)
                    for k in range(KD):
                        if t == 0:
                            pe.wait_ge(s["ready"], k + 1)
                        x_ = slice(t * P, t * P + r)
                        for w, v in ((w_hi, mT_hi), (w_lo, mT_hi), (w_hi, mT_lo)):
                            for c in range(2):
                                ins = pe.matmul(ps[0:r, 2 * (t % 3) + c, :], v[:, k, x_], w[:, k, c * 512:(c + 1) * 512],
                                                start=k == 0 and w is w_hi and v is mT_hi, stop=k == KD - 1 and v is mT_lo)
                    ins.then_inc(s["y_done"], 1)
                    if t >= 2:
                        turn(t - 2)
                turn(TILES - 2)
                turn(TILES - 1)

            @block.scalar
            def _(act):
                for k in range(KD):
                    act.wait_ge(landed[k % 2], 16 * (k // 2 + 1))
                    act.activation(w_hi[:, k, :], raw[:, k % 2, :], ACT.Copy).then_inc(s["rounded"], 1)

                def square(t, second):
                    r, n = rows_of(t), AT[(t, second)]
                    act.wait_ge(s["added"] if second else s["y_done"], t + 1)
                    if n:
                        act.wait_ge(s["sq_done"], n)
                    act.activation(sq[0:r, :], y[0:r, t % 2, :] if second else flat(t), ACT.Square,
                                   accum_out=ss[0:r, t, second:second + 1]).then_inc(s["sq_done"], 1)

                def split(t):
                    r = rows_of(t)
                    act.wait_ge(s["gained"], t + 1)
                    act.activation(mT_hi[:, :, t * P:t * P + r], h32[:, :, 0:r], ACT.Copy).then_inc(s["hi_done"], 1)

                for t, second in ORDER:
                    square(t, second)
                    if second and t >= 1:
                        split(t - 1)
                split(TILES - 1)

            @block.gpsimd
            def _(pool):
                pool.memset(half[:], -0.5).then_inc(s["half_set"], 1)
                pool.wait_ge(s["half_set"], 1)
                for n, (t, e) in enumerate(ORDER):
                    r = rows_of(t)
                    pool.wait_ge(s["sq_done"], n + 1)
                    pool.tensor_scalar(mean[0:r, t, e:e + 1], ss[0:r, t, e:e + 1], 1.0 / D, EPS, ALU.mult,
                                       ALU.add).then_inc(s["mean_done"], 1)
                    pool.wait_ge(s["mean_done"], n + 1)
                    pool.tensor_tensor(rstd[0:r, t, e:e + 1], mean[0:r, t, e:e + 1], half[0:r, :], ALU.pow)\
                        .then_inc(s["rstd_done"], 1)

            @block.vector
            def _(dve):
                for k in range(KD):
                    dve.wait_ge(s["rounded"], k + 1)
                    dve.tensor_tensor(w_lo[:, k, :], raw[:, k % 2, :], w_hi[:, k, :].bitcast(F32), ALU.subtract)\
                        .then_inc(s["ready"], 1)
                dve.wait_ge(s["const"], 48)

                def finish_tile(t):
                    r = rows_of(t)
                    dve.wait_ge(s["turned"], t + 1)
                    if t:
                        dve.wait_ge(s["lo_done"], t)
                    fg = gains[:, 2, :].rearrange("p (k a) -> p k a", a=1).broadcast_to([P, KD, r])
                    dve.tensor_tensor(h32[:, :, 0:r], ps[:, 6:8, :].rearrange("p a (k n) -> p (a k) n", n=P)[:, :, 0:r], fg,
                                      ALU.mult).then_inc(s["gained"], 1)
                    dve.wait_ge(s["hi_done"], t + 1)
                    dve.tensor_tensor(mT_lo[:, :, t * P:t * P + r], h32[:, :, 0:r], mT_hi[:, :, t * P:t * P + r].bitcast(F32),
                                      ALU.subtract).then_inc(s["lo_done"], 1)

                for t, second in ORDER:
                    r, n = rows_of(t), AT[(t, second)]
                    dve.wait_ge(s["rstd_done"], n + 1)
                    if second:
                        if t:
                            dve.wait_ge(s["turned"], t)
                        dve.tensor_scalar(h[0:r, :], y[0:r, t % 2, :], rstd[0:r, t, 1:2], None, ALU.mult).then_inc(s["h_done"], 1)
                        if t:
                            finish_tile(t - 1)
                    else:
                        if t >= 2:
                            dve.wait_ge(stored[t % 2], 16 * (t // 2))
                            dve.wait_ge(s["h_done"], t - 1)
                        dve.scalar_tensor_tensor(y[0:r, t % 2, :], flat(t), rstd[0:r, t, 0:1], gain[0:r, :], ALU.mult,
                                                 ALU.mult).then_inc(s["scaled"], 1)
                        dve.wait_ge(s["scaled"], t + 1)
                        dve.wait_ge(x_in[t % XS], 16 * (t // XS + 1))
                        dve.tensor_tensor(y[0:r, t % 2, :], y[0:r, t % 2, :], x[0:r, t % XS, :], ALU.add).then_inc(s["added"], 1)
                finish_tile(TILES - 1)


CONV = 3
CHUNKS = 2 * DFF // P
PAIRS = CHUNKS // 2
BODIES = PAIRS // 2
UW = CONV - 1 + S + NB * (TS + CONV - 1)
CW = UW - (CONV - 1)
SAMP = S + CONV - 1


def ffn(nc, io, hT_hi, hT_lo, acc):
    with ExitStack() as ctx:
        m = Mem(nc, ctx, "ffn")
        ring = WeightRing(m, io["w_ffn"], D, 4)
        ring.turns = lambda base: base // ring.RAW
        ring.RAW = RAW = 2
        prev = m.sb("prev", [P, CHUNKS, NB, CONV - 1])
        coef = m.sb("coef", [P, CHUNKS, CONV + 1])
        last = m.sb("last", [P, CHUNKS, 1 + NB, CONV - 1])
        u = m.sb("u", [P, 2, UW])
        c = m.sb("c", [P, 2, CW])
        prod = m.sb("prod", [P, N])
        a_hi, a_lo = m.sb("a_hi", [P, 2, N], F32R), m.sb("a_lo", [P, 2, N], F32R)
        ps = m.ps("ps", [P, 8, 512])
        s = {n: m.sem(n) for n in ("const", "u_set", "acc_set", "up_done", "up_read", "c0_done", "c1_done", "c_done", "kept", "gelu_done",
                                   "prod_done", "hi_done", "lo_done", "dn_done", "dn_read", "stored")}
        DN = 2 * TILES

        with nc.Block() as block:
            @block.sync
            def _(sp):
                with sp.Fori(0, FFN_CHUNKS // 4) as g:
                    for j in range(4):
                        ring.load(sp, 4 * g, j)
                sp.wait_ge(s["kept"], CHUNKS + 2)
                sp.dma_start(io["conv_last"], last[:]).then_inc(s["stored"], 16)
                sp.wait_ge(s["stored"], 16)

            @block.tensor
            def _(pe):
                def up(i, base, j, n):
                    ring.wait(pe, base, j)
                    pe.wait_ge(s["up_read"], 4 * i + n + 1)
                    sl = j % ring.R
                    for q, (at, w) in enumerate(COL):
                        for k in range(KD):
                            ins = mm3(pe, ps[:, 3 * (n % 2) + q, 0:w], ring.hi[:, sl, k * P:(k + 1) * P],
                                      ring.lo[:, sl, k * P:(k + 1) * P], hT_hi[:, k, at:at + w], hT_lo[:, k, at:at + w],
                                      k == 0, k == KD - 1)
                    ins.then_inc(s["up_done"], 1)

                def down(i, base, j):
                    ring.wait(pe, base, j + 1)
                    pe.wait_ge(s["lo_done"], 2 * i + 2)
                    for t in range(TILES):
                        for half in range(2):
                            pe.wait_ge(s["dn_read"], DN * i + 2 * t + half + 1)
                            o = ps[0:rows_of(t), 6 + half, :]
                            for f in range(2):
                                a = [x[:, f, t * P:t * P + rows_of(t)] for x in (a_hi, a_lo)]
                                w = [x[:, (j + f) % ring.R, half * 512:(half + 1) * 512] for x in (ring.hi, ring.lo)]
                                pe.matmul(o, a[0], w[0], start=f == 0, stop=False)
                                pe.matmul(o, a[0], w[1], start=False, stop=False)
                                ins = pe.matmul(o, a[1], w[0], start=False, stop=f == 1)
                            ins.then_inc(s["dn_done"], 1)

                def body(i, base, j):
                    up(i, base, j, 0)
                    up(i, base, j + 1, 1)
                    down(i - 1, base, j + 2)
                    up(i, base, j + 4, 2)
                    up(i, base, j + 5, 3)

                for n in range(4):
                    up(0, 0, n, n)
                with pe.Fori(0, (BODIES - 1) // 2) as g:
                    body(2 * g + 1, 4 + 12 * g, 0)
                    body(2 * g + 2, 4 + 12 * g, 6)
                down(BODIES - 1, 4 + 6 * (BODIES - 1), 0)

            @block.scalar
            def _(act):
                act.sem_inc(s["up_read"], 2)

                def round_hi(base, j):
                    act.wait_ge(ring.landed[j % RAW], 16 * ring.turn(base, j) + 16)
                    act.activation(ring.hi[:, j % ring.R, :], ring.raw[:, j % RAW, :], ACT.Copy).then_inc(ring.rounded, 1)

                def copy_u(i, f, n):
                    b, chunk = n % 2, f + (n % 2) * PAIRS
                    act.wait_ge(s["c_done"], 4 * i + n + 1)
                    act.wait_ge(s["kept"], 4 * i + n + 1)
                    samp = u[:, b, S + CONV - 1:].rearrange("p (b t) -> p b t", b=NB)
                    act.activation(samp[:, :, 0:CONV - 1], prev[:, bass.ds(chunk, 1)].rearrange("p a b t -> p (a b) t"), ACT.Copy)
                    act.wait_ge(s["up_done"], 4 * i + n + 1)
                    bank = 3 * b
                    act.activation(u[:, b, CONV - 1:CONV - 1 + 768].rearrange("p (a n) -> p a n", a=2), ps[:, bank:bank + 2, 0:384],
                                   ACT.Copy)
                    act.activation(u[:, b, CONV - 1 + 768:CONV - 1 + S], ps[:, bank + 2, 0:256], ACT.Copy)
                    act.activation(samp[:, :, CONV - 1:], ps[:, bank + 2, 256:320].rearrange("p (b t) -> p b t", b=NB), ACT.Copy)\
                        .then_inc(s["up_read"], 1)
                    act.wait_ge(s["up_read"], 4 * i + n + 3)
                    act.wait_ge(s["prod_done"], 2 * i + n // 2 + 1)
                    act.activation(c[:, b, :], u[:, b, CONV - 1:], ACT.Identity, bias=coef[:, bass.ds(chunk, 1), CONV],
                                   scale=coef[:, bass.ds(chunk, 1), CONV - 1]).then_inc(s["c0_done"], 1)

                def gelu(i, n):
                    act.wait_ge(s["c_done"], 4 * i + n + 2)
                    act.activation(c[:, 0, :], c[:, 0, :], ACT.Gelu_apprx_tanh).then_inc(s["gelu_done"], 1)

                def split(i, n):
                    f = n // 2
                    act.wait_ge(s["prod_done"], 2 * i + f + 2)
                    act.activation(a_hi[:, f, :], prod[:], ACT.Copy).then_inc(s["hi_done"], 1)

                def body(i, base, j, first=False):
                    copy_u(i, 2 * i, 0)
                    round_hi(base, j + 4)
                    gelu(i, 1)
                    copy_u(i, 2 * i, 1)
                    round_hi(base, j + 5)
                    if not first:
                        act.wait_ge(s["dn_done"], DN * i)
                        round_hi(base, j + 6)
                        round_hi(base, j + 7)
                    split(i, 1)
                    copy_u(i, 2 * i + 1, 2)
                    round_hi(base, j + (6 if first else 8))
                    gelu(i, 3)
                    copy_u(i, 2 * i + 1, 3)
                    round_hi(base, j + (7 if first else 9))
                    split(i, 3)

                for j in range(4):
                    round_hi(0, j)
                act.wait_ge(s["const"], 32)
                act.wait_ge(s["u_set"], 1)
                body(0, 0, 0, True)
                with act.Fori(0, (BODIES - 1) // 2) as g:
                    body(2 * g + 1, 4 + 12 * g, 0)
                    body(2 * g + 2, 4 + 12 * g, 6)

            @block.gpsimd
            def _(pool):
                for dst, src in ((prev, "conv_prev"), (coef, "conv_coef")):
                    pool.dma_start(dst[:], io[src]).then_inc(s["const"], 16)
                pool.memset(u[:, :, 0:CONV - 1], 0.0).then_inc(s["u_set"], 1)
                pool.memset(acc[:], 0.0).then_inc(s["acc_set"], 1)
                pool.sem_inc(s["kept"], 2)

                def keep(i, f, n):
                    b, chunk = n % 2, f + (n % 2) * PAIRS
                    pool.wait_ge(s["up_read"], 4 * i + n + 3)
                    pool.tensor_copy(last[:, bass.ds(chunk, 1), 0, :], u[:, b, S:S + CONV - 1].rearrange("p (a n) -> p a n", a=1))
                    pool.tensor_copy(last[:, bass.ds(chunk, 1), 1:].rearrange("p a b t -> p (a b) t"),
                                     u[:, b, SAMP:].rearrange("p (b t) -> p b t", b=NB)[:, :, TS:]).then_inc(s["kept"], 1)

                with pool.Fori(0, BODIES) as i:
                    for n in range(4):
                        keep(i, 2 * i + n // 2, n)

            @block.vector
            def _(dve):
                dve.sem_inc(ring.ready, RAW)
                dve.sem_inc(s["c_done"], 2)
                dve.sem_inc(s["prod_done"], 1)
                dve.sem_inc(s["dn_read"], 2)

                def conv(i, f, n):
                    b, chunk = n % 2, f + (n % 2) * PAIRS
                    dve.wait_ge(s["c0_done"], 4 * i + n + 1)
                    dve.scalar_tensor_tensor(c[:, b, :], u[:, b, 1:CW + 1], coef[:, bass.ds(chunk, 1), 1], c[:, b, :], ALU.mult,
                                             ALU.add).then_inc(s["c1_done"], 1)
                    dve.wait_ge(s["c1_done"], 4 * i + n + 1)
                    dve.scalar_tensor_tensor(c[:, b, :], u[:, b, 0:CW], coef[:, bass.ds(chunk, 1), 0], c[:, b, :], ALU.mult,
                                             ALU.add).then_inc(s["c_done"], 1)

                def multiply(i, n):
                    dve.wait_ge(s["c_done"], 4 * i + n + 3)
                    dve.wait_ge(s["gelu_done"], 2 * i + n // 2 + 1)
                    dve.tensor_tensor(prod[:, 0:S], c[:, 0, 0:S], c[:, 1, 0:S], ALU.mult)
                    samp = lambda x: x[:, S:].rearrange("p (b t) -> p b t", b=NB)[:, :, CONV - 1:]
                    dve.tensor_tensor(prod[:, S:].rearrange("p (b t) -> p b t", b=NB), samp(c[:, 0]), samp(c[:, 1]), ALU.mult)\
                        .then_inc(s["prod_done"], 1)

                def rest(i, n):
                    f = n // 2
                    dve.wait_ge(s["hi_done"], 2 * i + f + 1)
                    dve.tensor_tensor(a_lo[:, f, :], prod[:], a_hi[:, f, :].bitcast(F32), ALU.subtract)\
                        .then_inc(s["lo_done"], 1)

                def add(i, t, half, first=False):
                    r = rows_of(t)
                    dve.wait_ge(s["dn_done"], DN * i + 2 * t + half + 1)
                    o, a = ps[0:r, 6 + half, :], acc[0:r, t, half * 512:(half + 1) * 512]
                    dve.tensor_tensor(a, o, a, ALU.add).then_inc(s["dn_read"], 1)

                def body(i, base, j, first=False):
                    conv(i, 2 * i, 0)
                    ring.rest_lo(dve, base, j + 4)
                    if not first:
                        for t in range(TILES):
                            for half in range(2):
                                add(i - 1, t, half)
                            if t == 4:
                                ring.rest_lo(dve, base, j + 5)
                    else:
                        ring.rest_lo(dve, base, j + 5)
                    conv(i, 2 * i, 1)
                    multiply(i, 1)
                    if not first:
                        ring.rest_lo(dve, base, j + 6)
                        ring.rest_lo(dve, base, j + 7)
                    rest(i, 1)
                    conv(i, 2 * i + 1, 2)
                    ring.rest_lo(dve, base, j + (6 if first else 8))
                    conv(i, 2 * i + 1, 3)
                    multiply(i, 3)
                    ring.rest_lo(dve, base, j + (7 if first else 9))
                    rest(i, 3)

                for j in range(4):
                    ring.rest_lo(dve, 0, j)
                body(0, 0, 0, True)
                dve.wait_ge(s["acc_set"], 1)
                with dve.Fori(0, (BODIES - 1) // 2) as g:
                    body(2 * g + 1, 4 + 12 * g, 0)
                    body(2 * g + 2, 4 + 12 * g, 6)
                for t in range(TILES):
                    for half in range(2):
                        add(BODIES - 1, t, half)


FFN_CHUNKS = 4 + 6 * (BODIES - 1) + 2 + 2


def finish(nc, io, acc):
    with ExitStack() as ctx:
        m = Mem(nc, ctx, "fin")
        gain = m.sb("gain", [P, D])
        x = m.sb("x", [P, TILES, D])
        sq = m.sb("sq", [P, D])
        y = m.sb("y", [P, TILES, D])
        ss, mean, rstd = (m.sb(n, [P, TILES]) for n in ("ss", "mean", "rstd"))
        half = m.sb("half", [P, 1])
        s = {n: m.sem(n) for n in ("const", "sq_done", "half_set", "mean_done", "rstd_done", "scaled", "added", "stored")}
        x_in = [m.sem(f"x_in{i}") for i in range(TILES // 4 + 1)]

        with nc.Block() as block:
            @block.sync
            def _(sp):
                sp.dma_start(gain[:], io["gain_post"][1]).then_inc(s["const"], 16)
                for t in range(0, PT_TILES, 4):
                    sp.dma_start(x[:, t:t + 4, :], io["x1_scr"][t * P:(t + 4) * P, :].rearrange("(t p) c -> p t c", p=P))\
                        .then_inc(x_in[t // 4], 16)
                sp.dma_start(x[0:NSMP, PT_TILES, :], io["x1_scr"][S:N, :]).then_inc(x_in[-1], 16)
                for t in range(TILES):
                    r = rows_of(t)
                    sp.wait_ge(s["added"], t + 1)
                    sp.dma_start(io["y_p"][t * P:(t + 1) * P, :] if t < PT_TILES else io["y_s"], y[0:r, t, :])\
                        .then_inc(s["stored"], 16)
                sp.wait_ge(s["stored"], 16 * TILES)

            @block.scalar
            def _(act):
                for t in range(TILES):
                    r = rows_of(t)
                    if t:
                        act.wait_ge(s["sq_done"], t)
                    act.activation(sq[0:r, :], acc[0:r, t, :], ACT.Square, accum_out=ss[0:r, t:t + 1]).then_inc(s["sq_done"], 1)

            @block.gpsimd
            def _(pool):
                pool.memset(half[:], -0.5).then_inc(s["half_set"], 1)
                pool.wait_ge(s["half_set"], 1)
                for t in range(TILES):
                    r = rows_of(t)
                    pool.wait_ge(s["sq_done"], t + 1)
                    pool.tensor_scalar(mean[0:r, t:t + 1], ss[0:r, t:t + 1], 1.0 / D, EPS, ALU.mult,
                                       ALU.add).then_inc(s["mean_done"], 1)
                    pool.wait_ge(s["mean_done"], t + 1)
                    pool.tensor_tensor(rstd[0:r, t:t + 1], mean[0:r, t:t + 1], half[0:r, :], ALU.pow)\
                        .then_inc(s["rstd_done"], 1)

            @block.vector
            def _(dve):
                dve.wait_ge(s["const"], 16)

                def scale(t):
                    r = rows_of(t)
                    dve.wait_ge(s["rstd_done"], t + 1)
                    dve.scalar_tensor_tensor(y[0:r, t, :], acc[0:r, t, :], rstd[0:r, t:t + 1], gain[0:r, :], ALU.mult,
                                             ALU.mult).then_inc(s["scaled"], 1)

                scale(0)
                for t in range(TILES):
                    r = rows_of(t)
                    if t + 1 < TILES:
                        scale(t + 1)
                    dve.wait_ge(s["scaled"], t + 1)
                    dve.wait_ge(x_in[t // 4], 16)
                    dve.tensor_tensor(y[0:r, t, :], y[0:r, t, :], x[0:r, t, :], ALU.add).then_inc(s["added"], 1)


def build(nc, io):
    top = 229344
    Mem.spent.clear()
    pair = 4 * KD * N
    with ExitStack() as ctx:
        m = Mem(nc, ctx, "h")
        hT_hi = m.sb("hT_hi", [P, KD, N], F32R)
        hT_lo = m.sb("hT_lo", [P, KD, N], F32R)
        with ExitStack() as early:
            e = Mem(nc, early, "mem")
            mT_hi = e.sb("mT_hi", [P, KD, NMEM], F32R)
            mT_lo = e.sb("mT_lo", [P, KD, NMEM], F32R)
            items = [(io["xp"][t * P:(t + 1) * P, :], P, 0, hT_hi, hT_lo, t * P) for t in range(PT_TILES)]
            items += [(io["xs"], NSMP, 0, hT_hi, hT_lo, S)]
            items += [(io["mem"][t * P:(t + 1) * P, :], P, 1, mT_hi, mT_lo, t * P) for t in range(NMEM // P)]
            normalise(nc, io, "nrm", items)
            memory_attention(nc, io, hT_hi, hT_lo, mT_hi, mT_lo)
        window_attention(nc, io, hT_hi, hT_lo)
        latent_projections(nc, io, hT_hi, hT_lo)
        latent_attention(nc, io)
        sample_attention(nc, io, list(Mem.spent))
        sample_latent(nc, io)
        branch_outputs(nc, io)
        mix_hi = nc.alloc_sbuf_tensor_at("mix_hi", [P, KD, N], F32R, offset=top - 2 * pair)
        mix_lo = nc.alloc_sbuf_tensor_at("mix_lo", [P, KD, N], F32R, offset=top - pair)
        merge(nc, io, hT_hi, hT_lo, mix_hi, mix_lo)
    output_projection(nc, io, mix_hi, mix_lo)
    with ExitStack() as ctx:
        m = Mem(nc, ctx, "x")
        acc = m.sb("acc", [P, TILES, D])
        ffn(nc, io, mix_hi, mix_lo, acc)
        finish(nc, io, acc)


def rotary(dim, pos):
    inv = np.float32(10000.0) ** (-np.arange(dim // 2, dtype=np.float32) * np.float32(2.0 / dim))
    ang = pos.astype(np.float32)[:, None] * inv[None, :].astype(np.float32)
    return np.cos(ang).astype(np.float32), np.sin(ang).astype(np.float32)


def tiled(a, pad):
    a = np.concatenate([a, np.zeros((TILES * P - N,) + a.shape[1:], a.dtype)])
    return np.ascontiguousarray(np.moveaxis(a.reshape((TILES, P) + a.shape[1:]), 0, 1))


def constants():
    pos = np.concatenate([np.arange(S), np.tile(PAST + np.arange(TS), NB)])
    ca, sa = rotary(HD, pos)
    cb, sb = rotary(RB, pos)
    spread = np.concatenate([np.arange(S).reshape(P, PT_TILES).T.reshape(-1), np.arange(S, N)])
    both = lambda a: np.stack([tiled(a, 0), tiled(a[spread], 0)], 1)
    out = {"ident": np.eye(P, dtype=np.float32), "cos_a": both(ca), "sin_a": both(np.stack([-sa, sa], 1)),
           "cos_b": tiled(cb, 0), "sin_b": tiled(np.stack([-sb, sb], 1), 0)}
    q = np.arange(P)[:, None]
    step = q - np.arange(P)[None, :]
    dists = [(0, step + P), (0, step)]
    for later in range(2):
        dists += [(1, PT_TILES * step + HALFT * (later - x)) for x in range(2)] + [(2, PT_TILES * step)]
    blocks = [np.where((d >= 0) & (d <= GROUPS[g][0]) & (d % GROUPS[g][1] == 0), 0.0, -1e30) for g, d in dists]
    out["mask_p"] = np.concatenate(blocks, 1).astype(np.float32)
    causal = np.where(q >= np.arange(P)[None, :], 0.0, -1e30)
    out["mask_c"] = np.concatenate([np.zeros((P, S - P)), causal], 1).astype(np.float32)
    t = np.tile(np.arange(TS), 4 * H)[:, None]
    p = [np.arange(CK[0])[None, :], np.arange(CK[1])[None, :]]
    old = [p[0] >= t, (p[1] >= t) & ((CK[1] + t - p[1]) % GROUPS[1][1] == 0),
           (np.arange(CK[2]) // (PAST // GROUPS[2][1]))[None, :] == t]
    smp = np.repeat(np.arange(4), H * TS)[:, None]
    b, u = np.repeat(np.arange(NB), TS)[None, :], np.tile(np.arange(TS), NB)[None, :]
    halves = []
    for half in range(2):
        new = [(b == 4 * half + smp) & (u <= t) & ((t - u) % dil == 0) for _, dil in GROUPS]
        halves.append(np.concatenate([np.where(v, 0.0, -1e30) for v in old + new], 1))
    out["mask_s"] = np.stack(halves).astype(np.float32)
    t, smp = np.tile(np.arange(TS), 2 * HB)[:, None, None], np.repeat(np.arange(2), HB * TS)[:, None, None]
    two = np.arange(NB // 2)[None, :, None]
    out["mask_l"] = np.where((b[None] == 2 * two + smp) & (u[None] <= t), 0.0, -1e30).astype(np.float32)
    return out


def padded(a, width):
    return np.concatenate([a, np.zeros(a.shape[:-1] + (width - a.shape[-1],), a.dtype)], -1)


def slabs(w, n):
    k, c = w.shape
    return w.reshape(k // P // n, n, P, c).transpose(0, 2, 1, 3).reshape(-1, P, n * c)


OFF_Q = G * 3 * H * HD


def kernel(**inputs):
    import concourse.bacc as bacc
    from concourse.bass_utils import run_bass_kernel_spmd as run

    x = {k: np.asarray(v) for k, v in inputs.items()}
    w_in = x["w_in"][0]
    feed = constants()
    feed["xp"] = x["x_prompt"][0]
    feed["xs"] = x["x_sample"].reshape(NSMP, D)
    feed["mem"] = x["mem_prompt"][0]
    gain = lambda w: np.asarray(w)[0].reshape(-1, P).T
    feed["gains_pre"] = np.stack([gain(x["norm_attn_pre"]), gain(x["norm_mem"]), gain(x["norm_ffn_pre"])], 1)
    feed["gain_post"] = np.stack([np.tile(x["norm_attn_post"][0], (P, 1)), np.tile(x["norm_ffn_post"][0], (P, 1))])
    swa = w_in[:, :OFF_Q].reshape(D, G, 3, H, HD).transpose(3, 1, 0, 2, 4).reshape(H * G, D, 3 * HD)
    feed["w_swa"] = np.concatenate([slabs(u, 2) for u in swa])

    o0, o1, o2, o3 = OFF_Q, OFF_Q + QR, OFF_Q + QR + KR + RB, OFF_Q + QR + KR + RB + H * HD
    wide = 2 * QR
    feed["w_lat"] = np.concatenate(
        [padded(w, wide) for w in (slabs(w_in[:, o0:o1], 2), slabs(w_in[:, o1:o2], 2), slabs(x["w_uq"][0], 1),
                                   slabs(x["w_uk"][0].reshape(KR, HB * NOPE), 1),
                                   slabs(x["w_uv"][0].reshape(KR, HB * VD), 1))])
    feed["gain_lat"] = np.tile(np.concatenate([x["norm_cq"][0], x["norm_ckv"][0]]), (P, 1))
    kvw = x["w_mem_kv"][0]
    by_head = lambda w, n: w.reshape(D, -1, n).transpose(1, 0, 2)
    feed["w_mem"] = np.concatenate([slabs(kvw[:, :H * HD], 2), slabs(kvw[:, H * HD:], 2)]
                                   + [slabs(w, KD) for w in by_head(w_in[:, o2:o3], P)])

    cache = [x[f"cache_swa_g{g}"][0] for g in range(G)]
    for g in range(G):
        feed[f"cache{g}"] = cache[g]
    dil = GROUPS[2][1]
    wide2 = cache[2].reshape(NB, PAST // dil, dil, 2, H, HD)[:, :, :TS].transpose(0, 2, 1, 3, 4, 5)
    seen = np.concatenate([cache[0], cache[1], wide2.reshape(NB, CK[2], 2, H, HD), x["cache_mem_kv"][0]], 1)
    feed["k_smp"] = seen[:, :, 0].transpose(0, 3, 2, 1)
    feed["v_smp"] = seen[:, :, 1].reshape(NB, VBLK, P, H * HD).transpose(0, 2, 1, 3)
    feed["page_table"] = x["page_table"].reshape(1, -1)
    ckv, kr = x["cache_mla_ckv"][0], x["cache_mla_krope"][0]
    n_pool = ckv.shape[0]
    ckvT = ckv.transpose(0, 2, 1).reshape(n_pool, KR // P, P, P).transpose(0, 2, 1, 3).reshape(n_pool, P, KR)
    feed["pool"] = np.concatenate([ckvT, ckv], 2)
    feed["pool_kr"] = kr.transpose(0, 2, 1)
    feed["w_ukT"] = x["w_uk"][0].transpose(2, 1, 0)
    feed["w_uv"] = x["w_uv"][0].reshape(KR // P, P, HB * VD).transpose(1, 0, 2)
    by_cols = lambda w: w.reshape(512 // P, P, 4, 2 * P).transpose(2, 1, 0, 3).reshape(4, P, -1)
    feed["w_o"] = np.concatenate([by_cols(x[n][0]) for n in ("w_o_b", "w_o_m", "w_o_a")])
    blocks = lambda w: w.reshape(KD, P, -1, P).transpose(2, 1, 0, 3).reshape(-1, P, KD * P)
    feed["w_gate"] = blocks(w_in[:, o3:].reshape(D, 3, KD, P).transpose(0, 2, 1, 3).reshape(D, -1))
    feed["w_out"] = x["w_out"][0]
    up, down = blocks(x["w_up"][0]), x["w_down"][0].reshape(PAIRS, P, D)
    chunks = []
    for i in range(BODIES):
        f = 2 * i
        chunks += [up[f], up[f + PAIRS]] + ([down[f - 2], down[f - 1]] if i else []) + [up[f + 1], up[f + 1 + PAIRS]]
    chunks += [down[PAIRS - 2], down[PAIRS - 1]] * 2
    feed["w_ffn"] = np.stack(chunks)
    by_channel = lambda a: a.reshape(a.shape[:-1] + (CHUNKS, P)).transpose((a.ndim, a.ndim - 1) + tuple(range(a.ndim - 1)))
    feed["conv_prev"] = by_channel(x["state_ffn_conv"][0])
    feed["conv_coef"] = by_channel(np.concatenate([x["conv_w"][0], x["conv_b"]]))

    nc = bacc.Bacc("TRN2", target_bir_lowering=False, num_devices=1)
    io, arrays = {}, {}
    for name, a in feed.items():
        arrays[f"in_{name}"] = np.ascontiguousarray(a)
        io[name] = nc.dram_tensor(f"in_{name}", a.shape, mybir.dt.from_np(a.dtype), kind="ExternalInput").ap()
    outs = {}

    def output(name, shape):
        outs[name] = shape
        io[name] = nc.dram_tensor(f"out_{name}", shape, F32, kind="ExternalOutput").ap()
        return io[name]

    io["p_swa"] = [output(f"p_swa{g}", (min(w, S), 2, H, HD)) for g, (w, _) in enumerate(GROUPS)]
    ring_len = [min(w, PAST + TS) for w, _ in GROUPS]
    io["s_swa"] = [output(f"s_swa{g}", (NB, n, 2, H, HD)) for g, n in enumerate(ring_len)]
    io["s_swa_new"] = [a[:, n - TS:n] for a, n in zip(io["s_swa"], ring_len)]
    scratch = lambda name, shape: nc.dram_tensor(name, shape, F32).ap()
    io["smp_qk"] = scratch("smp_qk", (H, P, 2 * G, NSMP))
    io["smp_kv"] = scratch("smp_kv", (H, NSMP, G, 2, HD))
    io["smp_qm"] = scratch("smp_qm", (H, P, NSMP))
    io["bT_scr"] = scratch("bT_scr", (3, D, N))
    io["oA_scr"] = scratch("oA_scr", (H * HD, S))
    io["stat_scr"] = scratch("stat_scr", (H, PARTS, 2, S))
    io["w_scr"] = scratch("w_scr", (H, S))
    io["x1_scr"] = scratch("x1_scr", (N, D))
    output("y_p", (S, D))
    output("y_s", (NSMP, D))
    output("conv_last", (P, CHUNKS, 1 + NB, CONV - 1))
    io["qT_scr"] = scratch("qT_scr", (HB, NOPE + RB, N))
    io["kT_scr"] = scratch("kT_scr", (HB * NOPE, S))
    io["krT_scr"] = scratch("krT_scr", (RB, N))
    io["v_scr"] = scratch("v_scr", (S, HB * VD))
    output("p_ckv", (S, KR))
    output("p_kr", (S, RB))
    output("s_ckv", (NSMP, KR))
    output("s_kr", (NSMP, RB))
    output("p_mem", (NMEM, 2, H * HD))
    io["oT_scr"] = scratch("oT_scr", (3, 512, N))
    build(nc, io)
    r = run(nc, [arrays], core_ids=[0])
    got = {n: r.results[0][f"out_{n}"] for n in outs}
    conv = got["conv_last"].transpose(2, 3, 1, 0).reshape(1 + NB, CONV - 1, 2 * DFF)
    kept = lambda g: got[f"p_swa{g}"].reshape((1, 1) + got[f"p_swa{g}"].shape)
    return (got["y_p"].reshape(1, S, D), got["y_s"].reshape(NB, TS, D), kept(0), kept(1), kept(2),
            got["p_ckv"].reshape(1, 1, S, KR), got["p_kr"].reshape(1, 1, S, RB),
            got["p_mem"].reshape(1, 1, NMEM, 2, H, HD), conv[0:1].reshape(1, 1, CONV - 1, 2 * DFF),
            got["s_swa0"][None], got["s_swa1"][None], got["s_swa2"][None],
            got["s_ckv"].reshape(1, NB, TS, KR), got["s_kr"].reshape(1, NB, TS, RB), conv[1:][None])
```
